# Optimizing a Trainium2 kernel written in Bass

```python
import math
import jax, jax.numpy as jnp
from jax import lax
import numpy as np

D_MODEL = 1024
BATCH = 1
SEQ = 256
DEPTH = 2

CTX_LEN = 256
GRID_W = 64
N_BRANCH = 4
BRANCH_W = D_MODEL // N_BRANCH
HEAD_DIM = 64
GDN_HEADS = BRANCH_W // HEAD_DIM
GDN_CHUNK = 64
CONV_K = 5
RET_HEADS = BRANCH_W // HEAD_DIM
RET_CHUNK = 128
GQA_HEADS = BRANCH_W // HEAD_DIM
GQA_KV_HEADS = 2
Q_BLOCK = 128
FNET_GROUPS = 4
FNET_GROUP_DIM = BRANCH_W // FNET_GROUPS
ROPE_THETA = 10000.0
ROPE_FREQS = HEAD_DIM // 4
D_FF = 2816
N_EXPERTS = 8
TOP_K = 2
N_DENSE = (DEPTH + 1) // 2
N_MOE = DEPTH // 2
EPS = 1e-6

A_QKV = 3 * BRANCH_W
A_Z = BRANCH_W
A_AB = 4 * GDN_HEADS
B_W = 4 * BRANCH_W
C_Q = GQA_HEADS * HEAD_DIM
C_KV = 2 * GQA_KV_HEADS * HEAD_DIM
D_W = FNET_GROUPS * FNET_GROUP_DIM
OFF_B = A_QKV + A_Z + A_AB
OFF_C = OFF_B + B_W
OFF_D = OFF_C + C_Q + C_KV
P_IN = OFF_D + D_W

kernel_name = "hybrid_dit_prefix_block"

def _rmsnorm(x, g):
    xf = x.astype(jnp.float32)
    y = xf * lax.rsqrt(jnp.mean(xf * xf, axis=-1, keepdims=True) + EPS)
    return (y * g.astype(jnp.float32)).astype(x.dtype)

def _l2norm(x):
    return x * lax.rsqrt(jnp.sum(x * x, axis=-1, keepdims=True) + EPS)

def _flip(a):
    return jnp.flip(a, axis=1)

def _axial_rope_tables(n_tokens):
    rows = n_tokens // GRID_W
    row = jnp.repeat(jnp.arange(rows, dtype=jnp.float32), GRID_W)
    col = jnp.tile(jnp.arange(GRID_W, dtype=jnp.float32), rows)
    inv = ROPE_THETA ** (-jnp.arange(ROPE_FREQS, dtype=jnp.float32) / ROPE_FREQS)
    ang = jnp.concatenate([row[:, None] * inv, col[:, None] * inv], axis=-1)
    return jnp.cos(ang), jnp.sin(ang)

def _rope(x, cos, sin):
    xf = x.astype(jnp.float32)
    half = xf.shape[-1] // 2
    x1, x2 = xf[..., :half], xf[..., half:]
    cs, sn = cos[None, :, None, :], sin[None, :, None, :]
    return jnp.concatenate([x1 * cs - x2 * sn, x1 * sn + x2 * cs], axis=-1).astype(x.dtype)

def _short_conv(x, w):
    pad = (CONV_K - 1) // 2
    return lax.conv_general_dilated(x, w[:, None, :].astype(x.dtype), (1,), [(pad, pad)],
                                    dimension_numbers=("NWC", "WIO", "NWC"),
                                    feature_group_count=x.shape[-1])

def _to_chunks(a, c):
    b, t, h = a.shape[:3]
    a = a.reshape((b, t // c, c, h) + a.shape[3:])
    return jnp.swapaxes(jnp.moveaxis(a, 1, 0), 2, 3)

def _from_chunks(a):
    n, b, h, c = a.shape[:4]
    a = jnp.moveaxis(jnp.swapaxes(a, 2, 3), 0, 1)
    return a.reshape((b, n * c, h) + a.shape[4:])

def _gdn_scan(q, k, v, beta, g, s0):
    C = GDN_CHUNK
    qc, kc, vc = _to_chunks(q, C), _to_chunks(k, C), _to_chunks(v, C)
    bc, gc = _to_chunks(beta, C), _to_chunks(g, C)
    G = jnp.cumsum(gc, axis=-1)
    tril = jnp.tril(jnp.ones((C, C), dtype=bool))
    strict = jnp.tril(jnp.ones((C, C), dtype=bool), -1)
    diff = G[..., :, None] - G[..., None, :]
    decay = jnp.where(tril, jnp.exp(jnp.where(tril, diff, 0.0)), 0.0)
    kb = kc * bc[..., None]
    m = jnp.where(strict, jnp.einsum("nbhid,nbhjd->nbhij", kb, kc) * decay, 0.0)
    eye = jnp.eye(C, dtype=m.dtype)
    t_inv = jnp.linalg.solve(eye + m, jnp.broadcast_to(eye, m.shape))
    u = t_inv @ (vc * bc[..., None])
    w = t_inv @ (kb * jnp.exp(G)[..., None])
    qk = jnp.einsum("nbhid,nbhjd->nbhij", qc, kc) * decay
    g_last = G[..., -1]
    k_dec = kc * jnp.exp(g_last[..., None] - G)[..., None]

    def step(s, xs):
        u_n, w_n, k_n, gl_n = xs
        v_new = u_n - w_n @ s
        s_next = s * jnp.exp(gl_n)[..., None, None] + jnp.einsum("bhcd,bhce->bhde", k_n, v_new)
        return s_next, (s, v_new)

    s_final, (s_prev, v_new) = lax.scan(step, s0, (u, w, k_dec, g_last))
    o = jnp.einsum("nbhcd,nbhde->nbhce", qc * jnp.exp(G)[..., None], s_prev) + qk @ v_new
    return _from_chunks(o), s_final

def _retention_scan(q, k, v, log_gamma, s0):
    C = RET_CHUNK
    qc, kc, vc = _to_chunks(q, C), _to_chunks(k, C), _to_chunks(v, C)
    pos = jnp.arange(C, dtype=jnp.float32)
    diff = pos[:, None] - pos[None, :]
    decay = jnp.where(diff >= 0, jnp.exp(jnp.maximum(diff, 0.0) * log_gamma[:, None, None]), 0.0)
    q_dec = jnp.exp((pos + 1.0) * log_gamma[:, None])
    k_dec = jnp.exp((C - 1.0 - pos) * log_gamma[:, None])
    c_dec = jnp.exp(C * log_gamma)

    def step(s, xs):
        k_n, v_n = xs
        s_next = s * c_dec[:, None, None] + jnp.einsum("bhcd,bhce->bhde", k_n * k_dec[..., None], v_n)
        return s_next, s

    s_final, s_prev = lax.scan(step, s0, (kc, vc))
    inner = jnp.einsum("nbhid,nbhjd->nbhij", qc, kc) * decay
    o = inner @ vc + jnp.einsum("nbhcd,nbhde->nbhce", qc * q_dec[..., None], s_prev)
    return _from_chunks(o), s_final

def _gdn_branch(pc, pl, conv_w, a_log, dt_bias, norm_g, need_ctx):
    def prep(p):
        b, t, _ = p.shape
        qkv = jax.nn.silu(_short_conv(p[..., :A_QKV], conv_w))
        qkv = qkv.astype(jnp.float32).reshape(b, t, 3, GDN_HEADS, HEAD_DIM)
        q = _l2norm(qkv[:, :, 0]) * HEAD_DIM ** -0.5
        k = _l2norm(qkv[:, :, 1])
        v = qkv[:, :, 2]
        z = p[..., A_QKV:A_QKV + A_Z]
        ab = p[..., A_QKV + A_Z:OFF_B].astype(jnp.float32).reshape(b, t, 2, 2, GDN_HEADS)
        beta = jax.nn.sigmoid(ab[:, :, 0])
        g = -jnp.exp(a_log) * jax.nn.softplus(ab[:, :, 1] + dt_bias)
        return q, k, v, beta, g, z

    qc, kc, vc, bc, gc, zc = prep(pc)
    ql, kl, vl, bl, gl, zl = prep(pl)
    s0 = jnp.zeros((pc.shape[0], GDN_HEADS, HEAD_DIM, HEAD_DIM), jnp.float32)
    oc_f, sc_f = _gdn_scan(qc, kc, vc, bc[:, :, 0], gc[:, :, 0], s0)
    oc_b, sc_b = _gdn_scan(_flip(qc), _flip(kc), _flip(vc), _flip(bc[:, :, 1]), _flip(gc[:, :, 1]), s0)
    ol_f, _ = _gdn_scan(ql, kl, vl, bl[:, :, 0], gl[:, :, 0], sc_f)
    ol_b, _ = _gdn_scan(_flip(ql), _flip(kl), _flip(vl), _flip(bl[:, :, 1]), _flip(gl[:, :, 1]), sc_b)

    def finish(o, z):
        b, t = o.shape[:2]
        gate = jax.nn.silu(z.astype(jnp.float32)).reshape(b, t, GDN_HEADS, HEAD_DIM)
        return (_rmsnorm(o, norm_g) * gate).reshape(b, t, BRANCH_W).astype(z.dtype)

    out_l = finish(ol_f + _flip(ol_b), zl)
    out_c = finish(oc_f + _flip(oc_b), zc) if need_ctx else None
    return out_c, out_l

def _retention_branch(pc, pl, log_decay_raw, norm_g, cos, sin, need_ctx):
    log_gamma = -jnp.exp(log_decay_raw.astype(jnp.float32))

    def prep(p, rotate):
        b, t, _ = p.shape
        q, k, v, gate = jnp.split(p, 4, axis=-1)
        heads = lambda a: a.astype(jnp.float32).reshape(b, t, RET_HEADS, HEAD_DIM)
        q, k, v = heads(q), heads(k), heads(v)
        if rotate:
            q, k = _rope(q, cos, sin), _rope(k, cos, sin)
        return q, k * HEAD_DIM ** -0.5, v, gate

    qc, kc, vc, gtc = prep(pc, False)
    ql, kl, vl, gtl = prep(pl, True)
    s0 = jnp.zeros((pc.shape[0], RET_HEADS, HEAD_DIM, HEAD_DIM), jnp.float32)
    oc_f, sc_f = _retention_scan(qc, kc, vc, log_gamma[0], s0)
    oc_b, sc_b = _retention_scan(_flip(qc), _flip(kc), _flip(vc), log_gamma[1], s0)
    ol_f, _ = _retention_scan(ql, kl, vl, log_gamma[0], sc_f)
    ol_b, _ = _retention_scan(_flip(ql), _flip(kl), _flip(vl), log_gamma[1], sc_b)

    def finish(o, gate):
        b, t = o.shape[:2]
        mu = jnp.mean(o, axis=-1, keepdims=True)
        var = jnp.mean(jnp.square(o - mu), axis=-1, keepdims=True)
        on = ((o - mu) * lax.rsqrt(var + EPS)).reshape(b, t, BRANCH_W)
        return (on * norm_g.astype(jnp.float32) * jax.nn.silu(gate.astype(jnp.float32))).astype(gate.dtype)

    out_l = finish(ol_f + _flip(ol_b), gtl)
    out_c = finish(oc_f + _flip(oc_b), gtc) if need_ctx else None
    return out_c, out_l

def _attend(q, k, v):
    s = jnp.einsum("bqkgd,bskd->bkgqs", q, k).astype(jnp.float32) * HEAD_DIM ** -0.5
    p = jax.nn.softmax(s, axis=-1).astype(v.dtype)
    return jnp.einsum("bkgqs,bskd->bqkgd", p, v)

def _gqa_branch(pc, pl, qk_norm_g, cos, sin, need_ctx):
    groups = GQA_HEADS // GQA_KV_HEADS

    def prep(p, rotate):
        b, t, _ = p.shape
        q = _rmsnorm(p[..., :C_Q].reshape(b, t, GQA_HEADS, HEAD_DIM), qk_norm_g[0])
        kv = p[..., C_Q:].reshape(b, t, 2, GQA_KV_HEADS, HEAD_DIM)
        k = _rmsnorm(kv[:, :, 0], qk_norm_g[1])
        v = kv[:, :, 1]
        if rotate:
            q, k = _rope(q, cos, sin), _rope(k, cos, sin)
        return q.reshape(b, t, GQA_KV_HEADS, groups, HEAD_DIM), k, v

    qc, kc, vc = prep(pc, False)
    ql, kl, vl = prep(pl, True)
    k_all = jnp.concatenate([kc, kl], axis=1)
    v_all = jnp.concatenate([vc, vl], axis=1)
    b, t = ql.shape[:2]
    q_blocks = jnp.moveaxis(ql.reshape((b, t // Q_BLOCK, Q_BLOCK) + ql.shape[2:]), 1, 0)
    o = lax.map(lambda qb: _attend(qb, k_all, v_all), q_blocks)
    out_l = jnp.moveaxis(o, 0, 1).reshape(b, t, BRANCH_W)
    out_c = _attend(qc, kc, vc).reshape(pc.shape[0], pc.shape[1], BRANCH_W) if need_ctx else None
    return out_c, out_l

def _fourier(p):
    b, t, _ = p.shape
    f = p.astype(jnp.float32).reshape(b, t, FNET_GROUPS, FNET_GROUP_DIM)
    y = jnp.real(jnp.fft.fft2(f, axes=(1, 3), norm="ortho"))
    return y.reshape(b, t, BRANCH_W).astype(p.dtype)

def _merge(u, branches, w_branch, w_gate, b_gate, w_out):
    acc = None
    for i, y in enumerate(branches):
        gate = jax.nn.sigmoid((u @ w_gate[i] + b_gate[i]).astype(jnp.float32)).astype(u.dtype)
        term = gate * (y @ w_branch[i])
        acc = term if acc is None else acc + term
    return acc @ w_out

def _token_mixer(uc, ul, w_in, conv_w, gdn_a_log, gdn_dt_bias, gdn_norm_g, ret_log_decay_raw,
                 ret_norm_g, qk_norm_g, w_branch, w_gate, b_gate, w_out, cos, sin, need_ctx):
    splits = (OFF_B, OFF_C, OFF_D)
    pc = jnp.split(uc @ w_in, splits, axis=-1)
    pl = jnp.split(ul @ w_in, splits, axis=-1)
    a_c, a_l = _gdn_branch(pc[0], pl[0], conv_w, gdn_a_log, gdn_dt_bias, gdn_norm_g, need_ctx)
    b_c, b_l = _retention_branch(pc[1], pl[1], ret_log_decay_raw, ret_norm_g, cos, sin, need_ctx)
    c_c, c_l = _gqa_branch(pc[2], pl[2], qk_norm_g, cos, sin, need_ctx)
    out_l = _merge(ul, [a_l, b_l, c_l, _fourier(pl[3])], w_branch, w_gate, b_gate, w_out)
    out_c = _merge(uc, [a_c, b_c, c_c, _fourier(pc[3])], w_branch, w_gate, b_gate, w_out) if need_ctx else None
    return out_c, out_l

def _swiglu(x, w1, w3, w2):
    return (jax.nn.silu(x @ w1) * (x @ w3)) @ w2

def _moe(x, router, w1, w3, w2):
    logits = (x @ router).astype(jnp.float32)
    top_val, top_idx = lax.top_k(logits, TOP_K)
    weights = jax.nn.softmax(top_val, axis=-1)
    combine = jnp.sum(jax.nn.one_hot(top_idx, N_EXPERTS, dtype=jnp.float32) * weights[..., None], axis=-2)
    combine = combine.astype(x.dtype)
    out = combine[..., 0:1] * _swiglu(x, w1[0], w3[0], w2[0])
    for e in range(1, N_EXPERTS):
        out = out + combine[..., e:e + 1] * _swiglu(x, w1[e], w3[e], w2[e])
    return out

def setup_inputs(seed: int = 0) -> dict:
    key = jax.random.key(seed)
    ks = jax.random.split(key, 28)
    f32 = jnp.float32
    D = D_MODEL

    def nrm(k, shape, scale):
        return jax.random.normal(k, shape, f32) * scale

    dt = jnp.exp(jax.random.uniform(ks[10], (DEPTH, 2, GDN_HEADS), f32, math.log(1e-3), math.log(1e-1)))
    ret_base = np.log(-np.log1p(-(2.0 ** (-5.0 - np.arange(RET_HEADS)))))
    return {
        "x": nrm(ks[0], (BATCH, SEQ, D), 1.0),
        "c": nrm(ks[1], (BATCH, D), 1.0),
        "ctx": nrm(ks[2], (BATCH, CTX_LEN, D), 1.0),
        "c_ctx": nrm(ks[3], (D,), 1.0),
        "ada_w": nrm(ks[4], (DEPTH, D, 6 * D), 0.5 * D ** -0.5),
        "ada_b": nrm(ks[5], (DEPTH, 6 * D), 0.02),
        "norm_g": 1.0 + nrm(ks[6], (DEPTH, 4, D), 0.05),
        "w_in": nrm(ks[7], (DEPTH, D, P_IN), D ** -0.5),
        "conv_w": nrm(ks[8], (DEPTH, CONV_K, A_QKV), CONV_K ** -0.5),
        "gdn_a_log": jnp.log(jax.random.uniform(ks[9], (DEPTH, 2, GDN_HEADS), f32, 1.0, 16.0)),
        "gdn_dt_bias": dt + jnp.log(-jnp.expm1(-dt)),
        "gdn_norm_g": 1.0 + nrm(ks[11], (DEPTH, HEAD_DIM), 0.05),
        "ret_log_decay_raw": jnp.asarray(ret_base, dtype=f32) + nrm(ks[12], (DEPTH, 2, RET_HEADS), 0.1),
        "ret_norm_g": 1.0 + nrm(ks[13], (DEPTH, BRANCH_W), 0.05),
        "qk_norm_g": 1.0 + nrm(ks[14], (DEPTH, 2, HEAD_DIM), 0.05),
        "w_branch": nrm(ks[15], (DEPTH, N_BRANCH, BRANCH_W, D), BRANCH_W ** -0.5),
        "w_gate": nrm(ks[16], (DEPTH, N_BRANCH, D, D), D ** -0.5),
        "b_gate": nrm(ks[17], (DEPTH, N_BRANCH, D), 0.02),
        "w_out": nrm(ks[18], (DEPTH, D, D), D ** -0.5),
        "ffn_w1": nrm(ks[19], (N_DENSE, D, D_FF), D ** -0.5),
        "ffn_w3": nrm(ks[20], (N_DENSE, D, D_FF), D ** -0.5),
        "ffn_w2": nrm(ks[21], (N_DENSE, D_FF, D), D_FF ** -0.5),
        "moe_router": nrm(ks[22], (N_MOE, D, N_EXPERTS), D ** -0.5),
        "moe_w1": nrm(ks[23], (N_MOE, N_EXPERTS, D, D_FF), D ** -0.5),
        "moe_w3": nrm(ks[24], (N_MOE, N_EXPERTS, D, D_FF), D ** -0.5),
        "moe_w2": nrm(ks[25], (N_MOE, N_EXPERTS, D_FF, D), D_FF ** -0.5),
    }

def reference(x, c, ctx, c_ctx, ada_w, ada_b, norm_g, w_in, conv_w, gdn_a_log, gdn_dt_bias, gdn_norm_g,
              ret_log_decay_raw, ret_norm_g, qk_norm_g, w_branch, w_gate, b_gate, w_out,
              ffn_w1, ffn_w3, ffn_w2, moe_router, moe_w1, moe_w3, moe_w2):
    cos, sin = _axial_rope_tables(x.shape[1])
    hl, hc = x, ctx
    for l in range(DEPTH):
        need_ctx = l < DEPTH - 1
        mod_l = (jax.nn.silu(c) @ ada_w[l] + ada_b[l])[:, None, :]
        mod_c = (jax.nn.silu(c_ctx) @ ada_w[l] + ada_b[l])[None, None, :]
        sh1, sc1, g1, sh2, sc2, g2 = jnp.split(mod_l, 6, axis=-1)
        csh1, csc1, cg1, csh2, csc2, cg2 = jnp.split(mod_c, 6, axis=-1)

        ul = _rmsnorm(hl, norm_g[l, 0]) * (1.0 + sc1) + sh1
        uc = _rmsnorm(hc, norm_g[l, 0]) * (1.0 + csc1) + csh1
        mc, ml = _token_mixer(uc, ul, w_in[l], conv_w[l], gdn_a_log[l], gdn_dt_bias[l], gdn_norm_g[l],
                              ret_log_decay_raw[l], ret_norm_g[l], qk_norm_g[l], w_branch[l], w_gate[l],
                              b_gate[l], w_out[l], cos, sin, need_ctx)
        hl = hl + g1 * _rmsnorm(ml, norm_g[l, 1])

        if l % 2 == 0:
            i = l // 2
            ffn = lambda v, i=i: _swiglu(v, ffn_w1[i], ffn_w3[i], ffn_w2[i])
        else:
            i = l // 2
            ffn = lambda v, i=i: _moe(v, moe_router[i], moe_w1[i], moe_w3[i], moe_w2[i])

        vl = _rmsnorm(hl, norm_g[l, 2]) * (1.0 + sc2) + sh2
        hl = hl + g2 * _rmsnorm(ffn(vl), norm_g[l, 3])
        if need_ctx:
            hc = hc + cg1 * _rmsnorm(mc, norm_g[l, 1])
            vc = _rmsnorm(hc, norm_g[l, 2]) * (1.0 + csc2) + csh2
            hc = hc + cg2 * _rmsnorm(ffn(vc), norm_g[l, 3])
    return hl


_drawn_inputs = setup_inputs


def setup_inputs(seed=0):
    import zlib

    import numpy as np

    out = dict(_drawn_inputs(seed))
    spreads = {}
    factors = {'gdn_norm_g': 2.739, 'ret_norm_g': 3.147, 'qk_norm_g': 6.115, 'b_gate': 5.327}
    for name, (base, spread) in spreads.items():
        noise = np.random.default_rng([zlib.crc32(name.encode()), seed]).standard_normal(out[name].shape)
        drawn = base * np.exp(spread * noise) if base else spread * noise
        out[name] = __import__('jax').numpy.asarray(drawn.astype(out[name].dtype))
    for name, factor in factors.items():
        out[name] = (out[name] * factor).astype(out[name].dtype)
    return out
```

```python
from collections import namedtuple
from contextlib import ExitStack

import concourse.bass as bass
from concourse import mybir

F32 = mybir.dt.float32
F16 = mybir.dt.float16
ACT = mybir.ActivationFunctionType
ALU = mybir.AluOpType
AX = mybir.AxisListType.X

P = 128
D = 1024
KD = D // P
SEQ = 256
TOK = 2 * SEQ
NT = TOK // P
DEPTH = 2
BW = 256
HD = 64
NH = BW // HD
P_IN = 2832
OFF_Z, OFF_AB, OFF_RET, OFF_GQA, OFF_F = 768, 1024, 1040, 2064, 2576
D_FF = 2816
NF = D_FF // P
NE = 8
EPS = 1e-6
CW = 256
RING = 6
LEVELS = 6
HALO = 2
TAPS = 5

C_ID, C_ONE, C_U, C_L, C_ROPE, C_FD, C_FT = 0, 128, 256, 384, 512, 640, 896
C_END = C_FT + 1024
H_MASK = 0
H_DIST = 2 * 10 * P
H_RM = H_DIST + 2 * 4 * SEQ
H_END = H_RM + 2 * 2 * SEQ

A_CI = 0
A_CO = A_CI + 6 * 2 * (SEQ + 2 * HALO)
A_Z = A_CO + 6 * TOK
A_GQ = A_Z + NT * BW
A_RT = A_GQ + NT * 512
A_FT = A_RT + NT * 1024
A_YT = A_FT + 2 * TOK
A_TR = A_YT + 4 * 2 * TOK
A_END = A_TR + 7168
A_VEC = NF * TOK

V_ADA, V_NG, V_BG, V_CONV = 0, 48, 0, 32

SIGNALS = {
    "vec_T": 1, "vec_ok": 1, "ada_mm": 24, "mod_ok": 1,
    "ssq1": 4, "rms1": 1, "rs1": 1, "xs1": 4, "tp1": 8, "u_ok": 8, "ssq2": 4, "rms2": 1, "rs2": 1, "xs2": 4, "tp2": 8, "v_ok": 8,
    "pad_ok": 1, "win_mm": 23, "win_ok": 23, "conv_ok": 1, "silu_ok": 6, "ab_x": 1, "prm_e": 1, "ab_e": 1, "ab_ok": 1,
    "fn_mm1": 4, "fn_c": 4, "fn_mm2": 2, "fn_ok": 2,
    "gq_sq": 1, "gq_rs": 1, "gq_n": 1, "gq_tp": 4, "gq_T": 4, "gq_s": 16, "gq_max": 16, "gq_e": 16, "gq_pt": 16, "gq_ptc": 16, "gq_o": 16, "gq_on": 16, "gq_yt": 2, "gq_y": 2,
    "rt_n": 1, "rt_tp": 4, "rt_T": 4, "rt_w": 1, "rt_wm": 8, "rt_wok": 4, "rt_s": 8, "rt_p": 8, "rt_o": 8, "rt_var": 1, "rt_rs": 1, "rt_on": 1, "rt_silu": 1, "rt_yt": 2, "rt_y": 2,
    "cT_mm": 8, "cT_ok": 8, "kz_0": 1, "l2_sq": 1, "l2_rs": 1, "l2_ok": 1, "qk_mm": 4, "qk_ok": 4, "gl_mm": 1, "gl_ok": 2, "gl_e": 2,
    "gd_mm": 8, "gd_abs": 8, "gd_exp": 8, "gd_es": 8, "gd_M": 8, "gd_A": 8, "gd_MT": 8, "gd_MTs": 8, "gd_X": 8, "gd_XT": 8,
    "lv_mm1": 48, "lv_T1": 48, "lv_mm2": 48, "lv_X": 48, "gd_R": 2, "uw_mm": 8, "uw_ok": 8, "gd_q": 2, "wq_mm": 8, "wq_ok": 8,
    "st_mm": 6, "st_v": 8, "st_o": 8, "st_s": 6, "st_S": 6, "st_oa": 8,
    "z_silu": 1, "gdy_sq": 1, "gdy_rs": 1, "gdy_n": 1, "gdy_tp": 2, "gdy_ok": 2,
    "mg_mm": 32, "mg_sig": 32, "mg_add": 32,
    "gb_d1": 4, "gb_m1": 4, "gb_ok1": 4, "gb_d2": 4, "gb_m2": 4, "gb_ok2": 4,
    "po_mm": 1, "po_sq1": 8, "po_ss1": 1, "po_rs1": 1, "po_h1": 4, "po_sq2": 8, "po_ss2": 1, "po_rs2": 1, "po_h2": 4,
    "f_mm": 22, "f_sil": 22, "f_hid": 22, "f_out": 1, "f_acc": 0, "rlog": 0, "rcomb": 0,
}



class Signal:

    def __init__(self, semaphore, base):
        self.semaphore, self.base, self.raised = semaphore, base, 0

    def __call__(self, n):
        return self.semaphore, self.base + n

    @property
    def up(self):
        self.raised += 1
        return self.semaphore


Signals = namedtuple("Signals", list(SIGNALS))


def build_program(nc, d, out):
    with ExitStack() as ctx:
        def sb(name, shape, dt=F32):
            return ctx.enter_context(nc.sbuf_tensor(name, shape, dt))

        def sem(name):
            return ctx.enter_context(nc.semaphore(name))

        bank = [ctx.enter_context(nc.psum_tensor(f"bank{i}", [P, 512], F32)) for i in range(8)]
        consts = sb("consts", [P, C_END])
        halfc = sb("halfc", [P, H_END], F16)
        h = sb("h", [P, NT, D])
        uT = sb("uT", [P, KD, TOK])
        ring = sb("ring", [P, RING, KD * CW])
        arena = sb("arena", [P, A_END])
        colA = sb("colA", [P, 80])
        colB = sb("colB", [P, 62])
        silu_c = sb("silu_c", [P, 2, KD])
        mod = sb("mod", [P, 48, 2])
        scl = sb("scl", [P, 2, KD, 2])
        gpost = sb("gpost", [P, 2, KD, 2])
        stat = sb("stat", [P, 2, 4 * NT])
        bc = sb("bc", [P, 256 + HD + 2 * HD + 8 + 8 + 8])
        retg, gdng, qkg = bc[:, 0:256], bc[:, 256:320], bc[:, 320:448]
        alog, dtb, rraw = bc[:, 448:456], bc[:, 456:464], bc[:, 464:472]
        lgam = sb("lgam", [P, 8])
        gs = sb("gs", [P, 12, NT, 8])
        negG = sb("negG", [P, NT, NH])
        betaG = sb("betaG", [P, NT, NH])
        gg = sb("gg", [P, 6, NT, NH])
        S = sb("S", [P, 2, 2, P])
        small = sb("small", [P, 256])
        prm_exp = sb("prm_exp", [P, 24])
        rt8 = sb("rt8", [P, KD, NE])
        iota8 = sb("iota8", [P, NE])

        ident = consts[:, C_ID:C_ID + P]
        ones = consts[:, C_ONE:C_ONE + P]
        tri = [consts[:, C_U:C_U + P], consts[:, C_L:C_L + P]]

        def gmask(dr, n):
            return halfc[:, (10 * dr + n) * P:(10 * dr + n + 1) * P].unsqueeze(1).to_broadcast([P, 4, P])

        def area(at, *shape):
            n = 1
            for x in shape:
                n *= x
            v = arena[:, at:at + n]
            names = "abcd"[:len(shape)]
            if len(shape) == 1:
                return v
            return v.rearrange(f"p ({' '.join(names)}) -> p {' '.join(names)}",
                               **{names[i]: shape[i] for i in range(1, len(shape))})

        conv_in = area(A_CI, 6, 2, SEQ + 2 * HALO)
        qkv = area(A_CI, NT, 768)
        conv_out = area(A_CO, 6, TOK)
        qT = area(A_CO, 2, TOK)
        kz = area(A_CO + 1024, NH, TOK)
        Eb = area(A_TR + 6144, 2, NH, P)
        zn = area(A_Z, NT, BW)
        gqn = area(A_GQ, NT, 512)
        rtn = area(A_RT, NT, 1024)
        X, XT, MT = (area(A_GQ + 2048 * i, NT, NH, P) for i in range(3))
        qtilT, kdec = area(A_GQ, 2, TOK), area(A_GQ + 1024, NT, BW)
        wT, qtil = area(A_GQ + 4096, 2, TOK), area(A_GQ + 5120, NT, BW)
        fT = area(A_FT, 2, TOK)
        o_gdn = area(A_FT, NT, BW)
        yT = area(A_YT, 4, 2, TOK)
        GB = area(A_YT, 2, D)
        macc = area(A_YT + 2048, 2, D)
        AT, T1 = area(A_TR, NT, NH, P), area(A_TR + 2048, NT, NH, P)
        un, wn = area(A_TR + 2048, NT, BW), area(A_TR + 3072, NT, BW)
        Es = area(A_TR + 4096, 2, 2, NH, P)
        R = area(A_TR + 4096, NT, NH, P)
        vnew = area(A_TR + 4096, NT, BW)
        xs, junk = area(A_TR, NT, D), area(A_TR + 4096, D)
        accT = area(A_CI, KD, TOK)
        route = area(A_TR + 2048, 6, 2, NE)
        wbr = area(A_Z, 4, 2, D)
        hid = area(0, NF, TOK)
        vecA, vecB = arena[0:80, A_VEC:A_VEC + P], arena[0:62, A_VEC + P:A_VEC + 2 * P]
        crow = arena[0:16, A_VEC + 2 * P:A_VEC + 3 * P]

        semaphores = {name: sem(name) for name in SIGNALS}
        sig = [Signals(*[Signal(semaphores[name], total * l) for name, total in SIGNALS.items()])
               for l in range(DEPTH)]
        consts_in, c_in, h_in, out_in = sem("consts_in"), sem("c_in"), sem("h_in"), sem("out_in")
        c_T, c_silu, vec_in, prm_in = sem("c_T"), sem("c_silu"), [sem("vec0"), sem("vec1")], [sem("prm0"), sem("prm1")]
        slot_full = [sem(f"slot_full{i}") for i in range(RING)]
        slot_free = sem("slot_free")
        branch_in = [sem(f"branch_in{i}") for i in range(4)]
        dve_chain, act_chain, pool_chain = sem("dve_chain"), sem("act_chain"), sem("pool_chain")

        def linker(eng, s):
            n = [0]

            def link(ins):
                n[0] += 1
                ins.then_inc(s, 1)
                eng.wait_ge(s, n[0])
            return link

        def cols(w, c0, cn=CW):
            return w[:, c0:c0 + cn].rearrange("(k p) n -> p k n", p=P), (KD, cn)

        def rows(w, r0, rn):
            return w[r0:r0 + rn * P, :].rearrange("(k p) n -> p k n", p=P), (rn, D)

        WIN = ([0, 256, 512], [OFF_Z], [OFF_AB], [OFF_F], [OFF_GQA, OFF_GQA + 256],
               [OFF_RET + 256 * i for i in range(4)])

        def layer_slots(l):
            out_ = [cols(d["ada_w"][l], CW * i) for i in range(24)]
            for part in WIN:
                for c0 in part:
                    out_.append(cols(d["w_in"][l], c0, 16 if c0 == OFF_AB else CW))
            for i in (3, 2, 1, 0):
                out_ += [cols(d["w_gate"][l][i], CW * j) for j in range(4)]
            out_ += [cols(d["w_out"][l], CW * j) for j in range(4)]
            return out_

        def ffn_slots(w1, w3, w2):
            out_ = []
            for c in range(NF // 2):
                out_ += [cols(w1, CW * c), cols(w3, CW * c)]
            return out_ + [rows(w2, 2 * P * c, 2) for c in range(NF // 2)]

        slots = layer_slots(0) + ffn_slots(d["ffn_w1"][0], d["ffn_w3"][0], d["ffn_w2"][0]) + layer_slots(1)
        MOE0 = len(slots)
        PER = 3 * NF // 2

        def slot_view(n, shape):
            return ring[:, n % RING, 0:shape[0] * shape[1]].rearrange("p (k n) -> p k n", k=shape[0])

        class Weights:

            def __init__(self, pe):
                self.pe, self.n = pe, 0

            def take(self):
                n, self.n = self.n, self.n + 1
                self.pe.wait_ge(slot_full[n % RING], 16 * (n // RING + 1))
                return slot_view(n, slots[n][1])

        block = ctx.enter_context(nc.Block())

        @block.sync
        def _(sp):
            for n, (src, shape) in enumerate(slots):
                if n >= RING:
                    sp.wait_ge(slot_free, n - RING + 1)
                sp.dma_start(slot_view(n, shape), src).then_inc(slot_full[n % RING], 16)
            w1, w3, w2 = d["moe_w1"], d["moe_w3"], d["moe_w2"]
            with sp.Fori(0, NE // 2) as i:
                j = 0
                for e in range(2):
                    order = [(w, c) for c in range(NF // 2) for w in (w1, w3)] + [(w2, c) for c in range(NF // 2)]
                    for w, c in order:
                        n = MOE0 + j
                        sp.wait_ge(slot_free, 2 * PER * i + (n - RING + 1))
                        if w is w2:
                            src = w[bass.ds(2 * i + e, 1), 2 * P * c:2 * P * (c + 1), :].rearrange(
                                "e (k p) n -> p (e k) n", p=P)
                            dst = slot_view(n, (2, D))
                        else:
                            src = w[bass.ds(2 * i + e, 1), :, CW * c:CW * (c + 1)].rearrange(
                                "e (k p) n -> p (e k) n", p=P)
                            dst = slot_view(n, (KD, CW))
                        sp.dma_start(dst, src).then_inc(slot_full[n % RING], 16)
                        j += 1
            for t in range(2):
                sp.wait_ge(*sig[1].po_h2(t + 1))
                sp.dma_start(out[P * t:P * (t + 1), :], h[:, 2 + t, :]).then_inc(out_in, 16)
            sp.wait_ge(out_in, 32)

        @block.tensor
        def _(pe):
            W = Weights(pe)

            def transpose(dst, src):
                return pe.transpose(dst, src, ident)

            def prenorm_T(g_xs, g_tp, g_ok, tiles):
                pe.wait_ge(*g_xs(len(tiles)))
                for k in range(KD):
                    if k >= 4:
                        pe.wait_ge(*g_ok(k - 3))
                    for t in tiles:
                        last = transpose(bank[k % 4][:, P * t:P * (t + 1)], xs[:, t, P * k:P * (k + 1)])
                    last.then_inc(g_tp.up, 1)

            def gate_rows(g_d, g_m, g_ok, streams):
                for n in range(2 * len(streams)):
                    pe.wait_ge(*g_d(n + 1))
                    pe.matmul(bank[4 + n][:, :], ones, area(A_TR + 5120 + 512 * (n % 2), 512),
                              start=True, stop=True).then_inc(g_m.up, 1)

            pe.wait_ge(c_in, 32)
            pe.wait_ge(consts_in, 32)
            pe.transpose(bank[0][:, 0:16], crow[:, :], consts[0:16, C_ID:C_ID + 16]).then_inc(c_T, 1)

            for l in range(DEPTH):
                s = sig[l]
                ctx_out = l < DEPTH - 1
                tiles = list(range(NT)) if ctx_out else [2, 3]
                lo = 0 if ctx_out else SEQ
                width = TOK - lo

                pe.wait_ge(vec_in[l], 64)
                if l == 0:
                    pe.wait_ge(c_silu, 1)
                pe.transpose(bank[0][:, 0:80], vecA[:, :], consts[0:80, C_ID:C_ID + 80])
                pe.transpose(bank[0][:, 80:142], vecB[:, :], consts[0:62, C_ID:C_ID + 62]).then_inc(s.vec_T.up, 1)
                for n in range(48):
                    if n % 2 == 0:
                        w = W.take()
                    for k in range(KD):
                        mm = pe.matmul(bank[1][:, 2 * n:2 * n + 2], w[:, k, P * (n % 2):P * (n % 2 + 1)],
                                       silu_c[:, :, k], start=(k == 0), stop=(k == KD - 1))
                    if n % 2:
                        mm.then_inc(s.ada_mm.up, 1)
                        pe.wait_ge(*s.ada_mm(n // 2 + 1))
                        pe.sem_inc(slot_free, 1)
                pe.wait_ge(*s.vec_ok(1))
                pe.wait_ge(*s.mod_ok(1))
                prenorm_T(s.xs1, s.tp1, s.u_ok, range(NT))

                pe.wait_ge(*s.u_ok(KD))
                unit = 0
                for part in WIN:
                    for c0 in part:
                        w = W.take()
                        if c0 < OFF_Z or c0 == OFF_F:
                            for n in range(2):
                                if unit >= 4:
                                    pe.wait_ge(*s.win_ok(unit - 3))
                                for k in range(KD):
                                    mm = pe.matmul(bank[unit % 4][:, :], w[:, k, P * n:P * (n + 1)], uT[:, k, :],
                                                   start=(k == 0), stop=(k == KD - 1))
                                mm.then_inc(s.win_mm.up, 1)
                                unit += 1
                        elif c0 == OFF_AB:
                            pe.wait_ge(*s.win_ok(unit - 3))
                            for t in range(NT):
                                for k in range(KD):
                                    mm = pe.matmul(bank[unit % 4][:, 16 * t:16 * t + 16],
                                                   uT[:, k, P * t:P * (t + 1)], w[:, k, :],
                                                   start=(k == 0), stop=(k == KD - 1))
                            mm.then_inc(s.win_mm.up, 1)
                            unit += 1
                        else:
                            for t in range(NT):
                                if t % 2 == 0:
                                    pe.wait_ge(*s.win_ok(unit - 3))
                                for k in range(KD):
                                    mm = pe.matmul(bank[unit % 4][:, CW * (t % 2):CW * (t % 2 + 1)],
                                                   uT[:, k, P * t:P * (t + 1)], w[:, k, :],
                                                   start=(k == 0), stop=(k == KD - 1))
                                if t % 2:
                                    mm.then_inc(s.win_mm.up, 1)
                                    unit += 1
                        pe.wait_ge(*s.win_mm(unit))
                        pe.sem_inc(slot_free, 1)
                n_units = unit

                pe.wait_ge(*s.win_ok(n_units))
                for t in range(NT):
                    for c in range(2):
                        mm = pe.matmul(bank[t][:, 256 * c:256 * (c + 1)], fT[:, c, P * t:P * (t + 1)],
                                       consts[:, C_FD:C_FD + 256], start=True, stop=True)
                    mm.then_inc(s.fn_mm1.up, 1)
                pe.wait_ge(*s.fn_c(NT))
                xc = area(A_TR, NT, 2, 2, P)
                ftab = consts[:, C_FT:C_FT + 1024].rearrange("p (t c n) -> p t c n", t=2, c=2)
                for c in range(2):
                    for st in range(2):
                        for t in range(2):
                            for cs in range(2):
                                mm = pe.matmul(bank[4 + c][:, SEQ * st:SEQ * (st + 1)], xc[:, 2 * st + t, c, cs, :],
                                               ftab[:, t, cs, :], start=(t == 0 and cs == 0), stop=(t == 1 and cs == 1))
                    mm.then_inc(s.fn_mm2.up, 1)

                pe.wait_ge(*s.gq_n(1))
                gn = area(A_TR, NT, 8, HD)
                gT = area(A_TR + 2048, 4, TOK)
                for t in range(NT):
                    for c in range(4):
                        mm = transpose(bank[t][:, P * c:P * (c + 1)],
                                       gn[:, t, 2 * c:2 * c + 2, :].rearrange("p a b -> p (a b)"))
                    mm.then_inc(s.gq_tp.up, 1)
                pe.wait_ge(*s.gq_T(NT))
                Pb, PTb = area(A_TR + 4608, 2, 512), area(A_TR + 5632, 2, 4, P)
                work = [(t, hh) for t in tiles for hh in range(NH)]

                def gq_scores(n):
                    t, hh = work[n]
                    keys = SEQ if t < 2 else TOK
                    if n >= 2:
                        pe.wait_ge(*s.gq_e(n - 1))
                    q = gT[HD * (hh % 2):HD * (hh % 2 + 1), hh // 2, P * t:P * (t + 1)]
                    k = gT[HD * (hh % 2):HD * (hh % 2 + 1), 2 + hh // 2, 0:keys]
                    pe.matmul(bank[n % 2][:, 0:keys], q, k, start=True, stop=True).then_inc(s.gq_s.up, 1)

                def gq_values(n):
                    t, hh = work[n]
                    nk = 2 if t < 2 else 4
                    pe.wait_ge(*s.gq_e(n + 1))
                    if n >= 2:
                        pe.wait_ge(*s.gq_ptc(n - 1))
                    for j in range(nk):
                        mm = transpose(bank[2 + n % 2][:, P * j:P * (j + 1)], Pb[:, n % 2, P * j:P * (j + 1)])
                    mm.then_inc(s.gq_pt.up, 1)

                def gq_out(n):
                    t, hh = work[n]
                    nk = 2 if t < 2 else 4
                    pe.wait_ge(*s.gq_ptc(n + 1))
                    if n >= 2:
                        pe.wait_ge(*s.gq_on(n - 1))
                    for j in range(nk):
                        mm = pe.matmul(bank[4 + n % 2][:, 0:HD], PTb[:, n % 2, j, :],
                                       gqn[:, j, 384 + HD * (hh // 2):384 + HD * (hh // 2 + 1)],
                                       start=(j == 0), stop=(j == nk - 1))
                    mm.then_inc(s.gq_o.up, 1)

                for n in range(len(work) + 2):
                    if n < len(work):
                        gq_scores(n)
                    if 1 <= n <= len(work):
                        gq_values(n - 1)
                    if n >= 2:
                        gq_out(n - 2)

                def y_transposes(src, g_ready, g_tp):
                    pe.wait_ge(*g_ready(1))
                    for c in range(2):
                        for t in tiles:
                            mm = transpose(bank[6 + c][:, P * t:P * (t + 1)], src[:, t, P * c:P * (c + 1)])
                        mm.then_inc(g_tp.up, 1)

                pe.wait_ge(*s.gq_on(len(work)))
                y_transposes(area(A_TR, NT, BW), s.gq_on, s.gq_yt)

                pe.wait_ge(*s.rt_n(1))
                pe.wait_ge(*s.gq_y(2))
                rT = area(A_TR, 4, TOK)
                for t in range(NT):
                    for c in range(4):
                        mm = transpose(bank[t][:, P * c:P * (c + 1)], rtn[:, t, P * c:P * (c + 1)])
                    mm.then_inc(s.rt_tp.up, 1)
                pe.wait_ge(*s.rt_T(NT))
                PR = area(A_TR + 5120, 2, 4, SEQ)
                runits = [(hh, st) for hh in range(NH) for st in ((0, 1) if ctx_out else (1,))]
                def rt_scores(n):
                    hh, st = runits[n]
                    if n >= 2:
                        pe.wait_ge(*s.rt_p(n - 1))
                    part = slice(HD * (hh % 2), HD * (hh % 2 + 1))
                    for j in range(2 + 2 * st):
                        mm = pe.matmul(bank[4 + 2 * (n % 2) + j // 2][:, SEQ * (j % 2):SEQ * (j % 2 + 1)],
                                       rT[part, 2 + hh // 2, P * j:P * (j + 1)],
                                       rT[part, hh // 2, SEQ * st:SEQ * (st + 1)], start=True, stop=True)
                    mm.then_inc(s.rt_s.up, 1)

                rt_scores(0)
                for n, (hh, st) in enumerate(runits):
                    nk = 2 + 2 * st
                    if n + 1 < len(runits):
                        rt_scores(n + 1)
                    pe.wait_ge(*s.rt_p(n + 1))
                    for t in range(2):
                        for j in range(nk):
                            mm = pe.matmul(bank[2 * st + t][:, HD * hh:HD * (hh + 1)],
                                           PR[:, n % 2, j, P * t:P * (t + 1)],
                                           rtn[:, j, 512 + HD * hh:512 + HD * (hh + 1)],
                                           start=(j == 0), stop=(j == nk - 1))
                    mm.then_inc(s.rt_o.up, 1)
                y_transposes(area(A_TR, NT, BW), s.rt_on, s.rt_yt)

                pe.wait_ge(*s.silu_ok(6))
                for t in range(NT):
                    for c in range(6):
                        mm = transpose(bank[2 * (t % 2) + c // 4][:, P * (c % 4):P * (c % 4 + 1)],
                                       conv_out[:, c, P * t:P * (t + 1)])
                        if c in (3, 5):
                            mm.then_inc(s.cT_mm.up, 1)
                            if c == 5 and t in (1, 2):
                                pe.wait_ge(*s.cT_ok(2 * t))
                pe.wait_ge(*s.l2_ok(1))
                pe.wait_ge(*s.rt_y(2))
                for t in range(NT):
                    for c in range(4):
                        mm = transpose(bank[4 + t][:, P * c:P * (c + 1)], qkv[:, t, P * c:P * (c + 1)])
                    mm.then_inc(s.qk_mm.up, 1)
                pe.wait_ge(*s.ab_ok(1))
                pe.wait_ge(*s.cT_ok(2 * NT))
                for dr in range(2):
                    pe.matmul(bank[0][:, 32 * dr:32 * dr + 32], tri[dr], gs[:, 1, :, :].rearrange("p a b -> p (a b)"),
                              start=True, stop=True)
                pe.matmul(bank[0][:, 64:96], ones, gs[:, 1, :, :].rearrange("p a b -> p (a b)"),
                          start=True, stop=True).then_inc(s.gl_mm.up, 1)
                pe.wait_ge(*s.qk_ok(NT))

                for dr in range(2):
                    pe.wait_ge(*s.gl_ok(1 + dr))
                    if dr:
                        pe.wait_ge(*s.st_oa(NT))
                    for t in range(NT):
                        n = NT * dr + t
                        if t >= 2:
                            pe.wait_ge(*s.gd_abs(n - 1))
                            pe.wait_ge(*s.gd_M(n - 1))
                            pe.wait_ge(*s.gd_A(n - 1))
                        tok = slice(P * t, P * (t + 1))
                        for hh in range(NH):
                            c = slice(P * hh, P * (hh + 1))
                            pe.matmul(bank[t % 2][:, c], gs[:, 1, t, 4 * dr + hh:4 * dr + hh + 1].to_broadcast([P, P]),
                                      tri[dr], start=True, stop=True)
                            pe.matmul(bank[2 + t % 2][:, c], kz[:, hh, tok], kz[:, hh, tok], start=True, stop=True)
                            mm = pe.matmul(bank[4 + t % 2][:, c], kz[:, hh, tok], qT[:, hh // 2, tok],
                                           start=True, stop=True)
                        mm.then_inc(s.gd_mm.up, 1)
                        if t >= 1:
                            m_transposes = n - 1
                        else:
                            continue
                        for u in ([m_transposes] if t < NT - 1 else [m_transposes, n]):
                            pe.wait_ge(*s.gd_M(u + 1))
                            if u % NT >= 2:
                                pe.wait_ge(*s.gd_MTs(u - 1))
                            for hh in range(NH):
                                mm = transpose(bank[6 + u % 2][:, P * hh:P * (hh + 1)], T1[:, u % NT, hh, :])
                            mm.then_inc(s.gd_MT.up, 1)
                    pe.wait_ge(*s.gd_X(NT * (dr + 1)))
                    pe.wait_ge(*s.gd_XT(NT * (dr + 1)))
                    pe.wait_ge(*s.gd_A(NT * (dr + 1)))
                    for v in range(LEVELS):
                        base = (LEVELS * dr + v) * NT
                        for t in range(NT):
                            if v:
                                pe.wait_ge(*s.lv_X(base - NT + t + 1))
                            for hh in range(NH):
                                mm = pe.matmul(bank[t][:, P * hh:P * (hh + 1)], MT[:, t, hh, :], X[:, t, hh, :],
                                               start=True, stop=True)
                            mm.then_inc(s.lv_mm1.up, 1)
                        for t in range(NT):
                            pe.wait_ge(*s.lv_T1(base + t + 1))
                            for hh in range(NH):
                                if v < LEVELS - 1:
                                    pe.matmul(bank[4 + t][:, P * hh:P * (hh + 1)], XT[:, t, hh, :], T1[:, t, hh, :],
                                              start=True, stop=True)
                                mm = pe.matmul(bank[t][:, P * hh:P * (hh + 1)], T1[:, t, hh, :], XT[:, t, hh, :],
                                               start=True, stop=True)
                            mm.then_inc(s.lv_mm2.up, 1)
                    pe.wait_ge(*s.gd_R(dr + 1))
                    for t in range(NT):
                        pe.wait_ge(*s.lv_X((LEVELS * dr + LEVELS - 1) * NT + t + 1))
                        for hh in range(NH):
                            mm = pe.matmul(bank[4 + t][:, P * hh:P * (hh + 1)], XT[:, t, hh, :], R[:, t, hh, :],
                                           start=True, stop=True)
                        mm.then_inc(s.uw_mm.up, 1)
                    pe.wait_ge(*s.uw_ok(NT * (dr + 1)))
                    pe.wait_ge(*s.gd_q(dr + 1))
                    for t in range(NT):
                        for c in range(2):
                            transpose(bank[t][:, P * c:P * (c + 1)], wn[:, t, P * c:P * (c + 1)])
                            mm = transpose(bank[t][:, 256 + P * c:256 + P * (c + 1)], qtil[:, t, P * c:P * (c + 1)])
                        mm.then_inc(s.wq_mm.up, 1)
                    pe.wait_ge(*s.wq_ok(NT * (dr + 1)))
                    for i, t in enumerate((0, 1, 2, 3) if dr == 0 else (1, 0, 3, 2)):
                        n = NT * dr + i
                        tok = slice(P * t, P * (t + 1))
                        if i:
                            pe.wait_ge(*s.st_S(n - dr))
                            for c in range(2):
                                mm = pe.matmul(bank[4][:, P * c:P * (c + 1)], wT[:, c, tok], S[:, i % 2, c, :],
                                               start=True, stop=True)
                            mm.then_inc(s.st_mm.up, 1)
                        pe.wait_ge(*s.st_v(n + 1))
                        if i < NT - 1:
                            for c in range(2):
                                mm = pe.matmul(bank[5][:, P * c:P * (c + 1)], kdec[:, t, P * c:P * (c + 1)],
                                               vnew[:, t, P * c:P * (c + 1)], start=True, stop=True)
                            mm.then_inc(s.st_s.up, 1)
                        if n >= 2:
                            pe.wait_ge(*s.st_oa(n - 1))
                        for hh in range(NH):
                            if i and hh % 2 == 0:
                                pe.matmul(bank[6 + n % 2][:, HD * hh:HD * (hh + 2)], qtilT[:, hh // 2, tok],
                                          S[:, i % 2, hh // 2, :], start=True, stop=True,
                                          skip_group_check=True)
                            mm = pe.matmul(bank[6 + n % 2][:, HD * hh:HD * (hh + 1)], AT[:, t, hh, :],
                                           vnew[:, t, HD * hh:HD * (hh + 1)], start=(i == 0), stop=True,
                                           skip_group_check=bool(i))
                        mm.then_inc(s.st_o.up, 1)
                pe.wait_ge(*s.gdy_n(1))
                for c in range(2):
                    for t in tiles:
                        mm = transpose(bank[c][:, P * t:P * (t + 1)], un[:, t, P * c:P * (c + 1)])
                    mm.then_inc(s.gdy_tp.up, 1)

                pe.wait_ge(*s.gdy_ok(2))
                n = 0
                for br in (3, 2, 1, 0):
                    pe.wait_ge(branch_in[br], 16 * (l + 1))
                    wb = wbr[:, br]
                    for j in range(4):
                        wg = W.take()
                        for m in range(2):
                            if n >= 2:
                                pe.wait_ge(*s.mg_add(n - 1))
                            for k in range(KD):
                                pe.matmul(bank[n % 2][:, lo:TOK], wg[:, k, P * m:P * (m + 1)], uT[:, k, lo:TOK],
                                          start=(k == 0), stop=(k == KD - 1))
                            c = 2 * j + m
                            for k in range(2):
                                mm = pe.matmul(bank[2 + n % 2][:, lo:TOK], wb[:, k, P * c:P * (c + 1)], yT[:, br, k, lo:TOK],
                                               start=(k == 0), stop=(k == 1))
                            mm.then_inc(s.mg_mm.up, 1)
                            n += 1
                        pe.wait_ge(*s.mg_mm(n))
                        pe.sem_inc(slot_free, 1)

                pe.wait_ge(*s.mg_add(n))
                gate_rows(s.gb_d1, s.gb_m1, s.gb_ok1, [0, 1] if ctx_out else [1])
                pe.wait_ge(*s.gb_ok1(4 if ctx_out else 2))
                for j in range(4):
                    w = W.take()
                    for t in tiles:
                        for k in range(KD):
                            mm = pe.matmul(bank[2 * t + j // 2][:, CW * (j % 2):CW * (j % 2 + 1)],
                                           accT[:, k, P * t:P * (t + 1)], w[:, k, :], start=(k == 0), stop=(k == KD - 1))
                    mm.then_inc(slot_free, 1)
                pe.wait_ge(slot_free, W.n)
                pe.sem_inc(s.po_mm.up, 1)
                pe.wait_ge(*s.po_h1(len(tiles)))
                gate_rows(s.gb_d2, s.gb_m2, s.gb_ok2, [0, 1] if ctx_out else [1])

                pe.wait_ge(*s.gb_ok2(2 * (2 if ctx_out else 1)))
                prenorm_T(s.xs2, s.tp2, s.v_ok, tiles)
                pe.wait_ge(*s.v_ok(KD))

                if ctx_out:
                    for c in range(NF // 2):
                        wa, wb = W.take(), W.take()
                        for m in range(2):
                            f = 2 * c + m
                            if f >= 2:
                                pe.wait_ge(*s.f_hid(f - 1))
                            for k in range(KD):
                                pe.matmul(bank[f % 2][:, :], wa[:, k, P * m:P * (m + 1)], uT[:, k, :],
                                          start=(k == 0), stop=(k == KD - 1))
                            for k in range(KD):
                                mm = pe.matmul(bank[2 + f % 2][:, :], wb[:, k, P * m:P * (m + 1)], uT[:, k, :],
                                               start=(k == 0), stop=(k == KD - 1))
                            mm.then_inc(s.f_mm.up, 1)
                        pe.wait_ge(*s.f_mm(2 * c + 2))
                        pe.sem_inc(slot_free, 2)
                    pe.wait_ge(*s.f_hid(NF))
                    for c in range(NF // 2):
                        w = W.take()
                        for m in range(2):
                            f = 2 * c + m
                            for t in range(NT):
                                for hf in range(2):
                                    mm = pe.matmul(bank[2 * t + hf][:, :], hid[:, f, P * t:P * (t + 1)],
                                                   w[:, m, 512 * hf:512 * (hf + 1)], start=(f == 0), stop=(f == NF - 1))
                        mm.then_inc(slot_free, 1)
                    pe.wait_ge(slot_free, W.n)
                    pe.sem_inc(s.f_out.up, 1)
                    pe.wait_ge(*s.po_h2(NT))
                else:
                    for t in range(2):
                        for k in range(KD):
                            mm = pe.matmul(bank[0][:, NE * t:NE * (t + 1)], uT[:, k, SEQ + P * t:SEQ + P * (t + 1)],
                                           rt8[:, k, :], start=(k == 0), stop=(k == KD - 1))
                    mm.then_inc(s.rlog.up, 1)
                    pe.wait_ge(*s.rcomb(1))
                    with pe.Fori(0, NE // 2) as i:
                        for e in range(2):
                            at = PER * e
                            for c in range(NF // 2):
                                views = []
                                for q in range(2):
                                    n = MOE0 + at
                                    pe.wait_ge(slot_full[n % RING], 16 * (2 * PER // RING) * i + 16 * (n // RING + 1))
                                    views.append(slot_view(n, (KD, CW)))
                                    at += 1
                                for m in range(2):
                                    f = 2 * c + m
                                    pe.wait_ge(*s.f_hid(2 * NF * i + (NF * e + f - 1) + 2))
                                    for q in range(2):
                                        for k in range(KD):
                                            mm = pe.matmul(bank[2 * q + f % 2][:, 0:SEQ], views[q][:, k, P * m:P * (m + 1)],
                                                           uT[:, k, SEQ:TOK], start=(k == 0), stop=(k == KD - 1))
                                    mm.then_inc(s.f_mm.up, 1)
                                pe.wait_ge(*s.f_mm(2 * NF * i + (NF * e + 2 * c + 2)))
                                pe.sem_inc(slot_free, 2)
                            pe.wait_ge(*s.f_hid(2 * NF * i + (NF * (e + 1) + 2)))
                            pe.wait_ge(*s.f_acc(2 * i + (e + 1)))
                            for c in range(NF // 2):
                                n = MOE0 + at
                                pe.wait_ge(slot_full[n % RING], 16 * (2 * PER // RING) * i + 16 * (n // RING + 1))
                                w = slot_view(n, (2, D))
                                at += 1
                                for m in range(2):
                                    f = 2 * c + m
                                    for t in range(2):
                                        for hf in range(2):
                                            mm = pe.matmul(bank[4 + 2 * t + hf][:, :],
                                                           hid[:, f, P * t:P * (t + 1)],
                                                           w[:, m, 512 * hf:512 * (hf + 1)],
                                                           start=(f == 0), stop=(f == NF - 1))
                                mm.then_inc(slot_free, 1)
                            pe.wait_ge(slot_free, 2 * PER * i + (MOE0 + at))
                            pe.sem_inc(s.f_out.up, 1)

        @block.scalar
        def _(act):
            link = linker(act, act_chain)
            act.dma_start(consts[:, :], d["consts"]).then_inc(consts_in, 16)
            act.dma_start(halfc[:, :], d["halfc"]).then_inc(consts_in, 16)
            act.dma_start(crow[0:8, :], d["c"].rearrange("a (k p) -> (a k) p", p=P)).then_inc(c_in, 16)
            act.dma_start(crow[8:16, :], d["c_ctx"].rearrange("(k p) -> k p", p=P)).then_inc(c_in, 16)
            act.dma_start(h[:, 0:2, :], d["ctx"].rearrange("b (t p) n -> p (b t) n", p=P)).then_inc(h_in, 16)
            act.dma_start(h[:, 2:4, :], d["x"].rearrange("b (t p) n -> p (b t) n", p=P)).then_inc(h_in, 16)
            act.dma_start(rt8[:, :, :], d["moe_router"][0].rearrange("(k p) e -> p k e", p=P)).then_inc(h_in, 16)
            act.dma_start(iota8[:, :], d["iota8"]).then_inc(h_in, 16)

            def load_vectors(l):
                s = sig[l]
                act.dma_start(vecA[0:48, :], d["ada_b"][l].rearrange("(k p) -> k p", p=P)).then_inc(vec_in[l], 16)
                act.dma_start(vecA[48:80, :], d["norm_g"][l].rearrange("a (k p) -> (a k) p", p=P)).then_inc(vec_in[l], 16)
                act.dma_start(vecB[0:32, :], d["b_gate"][l].rearrange("a (k p) -> (a k) p", p=P)).then_inc(vec_in[l], 16)
                act.dma_start(vecB[32:62, :], d["conv_w"][l].rearrange("a (k p) -> (a k) p", p=P)).then_inc(vec_in[l], 16)
                for dst, src in ((retg, d["ret_norm_g"][l]), (gdng, d["gdn_norm_g"][l]),
                                 (qkg, d["qk_norm_g"][l].rearrange("a b -> (a b)")),
                                 (alog, d["gdn_a_log"][l].rearrange("a b -> (a b)")),
                                 (dtb, d["gdn_dt_bias"][l].rearrange("a b -> (a b)")),
                                 (rraw, d["ret_log_decay_raw"][l].rearrange("a b -> (a b)"))):
                    act.dma_start(dst, src.partition_broadcast(P)).then_inc(prm_in[l], 16)

            load_vectors(0)
            act.wait_ge(c_T, 1)
            act.activation(silu_c[:, :, :], bank[0][:, 0:16].rearrange("p (a k) -> p a k", a=2), ACT.Silu).then_inc(c_silu, 1)
            act.wait_ge(h_in, 64)

            def squares(g, tiles, at):
                for t in tiles:
                    if t > tiles[0]:
                        act.wait_ge(*g(t - tiles[0]))
                    act.activation(junk, h[:, t, :], ACT.Square, accum_out=stat[:, 0, at + t:at + t + 1]).then_inc(g.up, 1)

            def root(x, g_ready, g_done):
                act.wait_ge(*g_ready(1))
                act.activation(x, x, ACT.Sqrt).then_inc(g_done.up, 1)

            def prenorm_evac(sub, g_tp, g_ok, tiles):
                for k in range(1, KD, 2):
                    act.wait_ge(*g_tp(k + 1))
                    act.wait_ge(*g_ok(k))
                    for st in ((0, 1) if len(tiles) == NT else (1,)):
                        ins = act.activation(uT[:, k, SEQ * st:SEQ * (st + 1)], bank[k % 4][:, SEQ * st:SEQ * (st + 1)],
                                             ACT.Identity, scale=scl[:, sub, k, 1 - st:2 - st],
                                             bias=mod[:, 24 * sub + k, 1 - st:2 - st])
                    ins.then_inc(g_ok.up, 1)

            def gate_rows(g_m, g_ok, streams):
                for n in range(2 * len(streams)):
                    act.wait_ge(*g_m(n + 1))
                    act.copy(GB[:, streams[n // 2], 512 * (n % 2):512 * (n % 2 + 1)], bank[4 + n][:, :]).then_inc(g_ok.up, 1)

            def post_squares(g, l, tiles):
                for i, t in enumerate(tiles):
                    for hf in range(2):
                        if i or hf:
                            act.wait_ge(*g(2 * i + hf))
                        act.activation(area(A_TR + 6144, 512), bank[2 * t + hf][:, :], ACT.Square,
                                       accum_out=stat[:, 1, 2 * t + hf:2 * t + hf + 1]).then_inc(g.up, 1)

            for l in range(DEPTH):
                s = sig[l]
                ctx_out = l < DEPTH - 1
                tiles = list(range(NT)) if ctx_out else [2, 3]
                lo = 0 if ctx_out else SEQ
                if l:
                    act.wait_ge(*sig[0].po_h2(NT))
                squares(s.ssq1, range(NT), 0)
                root(stat[:, 0, 0:NT], s.rms1, s.rs1)
                prenorm_evac(0, s.tp1, s.u_ok, range(NT))

                unit = 0
                act.wait_ge(*s.pad_ok(1))
                for part in WIN:
                    for c0 in part:
                        for q in range(1 if c0 == OFF_AB else 2):
                            act.wait_ge(*s.win_mm(unit + 1))
                            b = bank[unit % 4]
                            half = b[:, :].rearrange("p (a n) -> p a n", a=2)
                            if c0 < OFF_Z:
                                dst, src = conv_in[:, 2 * (c0 // 256) + q, :, HALO:HALO + SEQ], half
                            elif c0 == OFF_F:
                                dst, src = fT[:, q, :], b[:, :]
                            elif c0 == OFF_AB:
                                dst, src = gs[:, 2:4, :, :].rearrange("p a t n -> p t a n"), \
                                    b[:, 0:64].rearrange("p (t a n) -> p t a n", t=NT, a=2)
                            elif c0 == OFF_Z:
                                dst, src = zn[:, 2 * q:2 * q + 2, :], half
                            elif c0 >= OFF_GQA:
                                dst, src = gqn[:, 2 * q:2 * q + 2, c0 - OFF_GQA:c0 - OFF_GQA + 256], half
                            else:
                                dst, src = rtn[:, 2 * q:2 * q + 2, c0 - OFF_RET:c0 - OFF_RET + 256], half
                            act.copy(dst, src).then_inc(s.win_ok.up, 1)
                            unit += 1

                act.wait_ge(prm_in[l], 96)
                act.activation(prm_exp[:, :], bc[:, 448:472], ACT.Exp).then_inc(s.prm_e.up, 1)
                act.wait_ge(*s.ab_x(1))
                link(act.activation(gs[:, 5], gs[:, 4], ACT.Abs))
                act.activation(gs[:, 6], gs[:, 2], ACT.Exp, scale=-1.0)
                link(act.activation(gs[:, 7], gs[:, 5], ACT.Exp, scale=-1.0))
                act.activation(gs[:, 8], gs[:, 7], ACT.Ln, bias=1.0).then_inc(s.ab_e.up, 1)

                for t in range(NT):
                    act.wait_ge(*s.fn_mm1(t + 1))
                    act.copy(area(A_TR, NT, 512)[:, t, :], bank[t][:, :]).then_inc(s.fn_c.up, 1)
                for c in range(2):
                    act.wait_ge(*s.fn_mm2(c + 1))
                    act.copy(yT[:, 3, c, :], bank[4 + c][:, :]).then_inc(s.fn_ok.up, 1)

                root(small[:, 32:56], s.gq_sq, s.gq_rs)
                gT = area(A_TR + 2048, 4, TOK)
                for t in range(NT):
                    act.wait_ge(*s.gq_tp(t + 1))
                    act.copy(gT[:, :, P * t:P * (t + 1)], bank[t][:, :].rearrange("p (c n) -> p c n", c=4)).then_inc(s.gq_T.up, 1)
                Pb = area(A_TR + 4608, 2, 512)
                work = [(t, hh) for t in tiles for hh in range(NH)]
                for n, (t, hh) in enumerate(work):
                    keys = SEQ if t < 2 else TOK
                    act.wait_ge(*s.gq_max(n + 1))
                    if n >= 2:
                        act.wait_ge(*s.gq_pt(n - 1))
                    act.activation(Pb[:, n % 2, 0:keys], bank[n % 2][:, 0:keys], ACT.Exp, bias=small[:, n:n + 1],
                                   scale=HD ** -0.5, accum_out=small[:, 16 + n:17 + n]).then_inc(s.gq_e.up, 1)
                for c in range(2):
                    act.wait_ge(*s.gq_yt(c + 1))
                    act.copy(yT[:, 2, c, lo:TOK], bank[6 + c][:, lo:TOK]).then_inc(s.gq_y.up, 1)

                act.wait_ge(*s.rt_w(1))
                for t in range(NT):
                    act.wait_ge(*s.rt_tp(t + 1))
                    act.copy(area(A_TR, 4, TOK)[:, :, P * t:P * (t + 1)],
                             bank[t][:, :].rearrange("p (c n) -> p c n", c=4)).then_inc(s.rt_T.up, 1)
                for hh in range(NH):
                    if hh:
                        act.wait_ge(*s.rt_wok(hh))
                    for dr in range(2):
                        act.activation(area(A_TR + 2048 + 1024 * dr, 4 * SEQ),
                                       halfc[:, H_DIST + 1024 * dr:H_DIST + 1024 * (dr + 1)], ACT.Exp,
                                       scale=lgam[:, 4 * dr + hh:4 * dr + hh + 1]).then_inc(s.rt_wm.up, 1)
                act.wait_ge(*s.rt_o((2 if ctx_out else 1) * NH))
                act.activation(area(A_TR + 3072, NT, BW), rtn[:, :, 768:1024], ACT.Silu).then_inc(s.rt_silu.up, 1)
                root(small[:, 112 + NH * tiles[0]:112 + NH * NT], s.rt_var, s.rt_rs)
                for c in range(2):
                    act.wait_ge(*s.rt_yt(c + 1))
                    act.copy(yT[:, 1, c, lo:TOK], bank[6 + c][:, lo:TOK]).then_inc(s.rt_y.up, 1)

                act.wait_ge(*s.conv_ok(1))
                for c in range(6):
                    act.activation(conv_out[:, c, :], conv_out[:, c, :], ACT.Silu).then_inc(s.silu_ok.up, 1)
                for t in range(NT):
                    for q in range(2):
                        act.wait_ge(*s.cT_mm(2 * t + q + 1))
                        act.copy(qkv[:, t, 512 * q:512 * q + (256 if q else 512)],
                                 bank[2 * (t % 2) + q][:, 0:(256 if q else 512)]).then_inc(s.cT_ok.up, 1)
                root(small[:, 128:160], s.l2_sq, s.l2_rs)
                for t in range(NT):
                    act.wait_ge(*s.qk_mm(t + 1))
                    tok, b = slice(P * t, P * (t + 1)), bank[4 + t][:, :].rearrange("p (c n) -> p c n", c=4)
                    if t == 0:
                        act.wait_ge(*s.kz_0(1))
                    act.copy(qT[:, :, tok], b[:, 0:2, :])
                    act.copy(kz[0:HD, 0:NH:2, tok], b[0:HD, 2:4, :])
                    act.copy(kz[HD:P, 1:NH:2, tok], b[HD:P, 2:4, :]).then_inc(s.qk_ok.up, 1)
                for dr in range(2):
                    act.wait_ge(*s.gl_ok(1 + dr))
                    act.activation(gg[:, 3:6, :, :], gg[:, 0:3, :, :], ACT.Exp).then_inc(s.gl_e.up, 1)
                    for t in range(NT):
                        n = NT * dr + t
                        act.wait_ge(*s.gd_mm(n + 1))
                        if n >= 2:
                            act.wait_ge(*s.gd_es(n - 1))
                        for hh in range(NH):
                            ins = act.activation(Eb[:, n % 2, hh, :], bank[n % 2][:, P * hh:P * (hh + 1)], ACT.Abs,
                                                 bias=negG[:, t, hh:hh + 1])
                        ins.then_inc(s.gd_abs.up, 1)
                        act.wait_ge(*s.gd_abs(n + 1))
                        act.activation(Eb[:, n % 2, :, :], Eb[:, n % 2, :, :], ACT.Exp, scale=-1.0).then_inc(s.gd_exp.up, 1)
                        if t >= 1:
                            for u in ([n - 1] if t < NT - 1 else [n - 1, n]):
                                act.wait_ge(*s.gd_MT(u + 1))
                                act.copy(MT[:, u % NT, :, :], bank[6 + u % 2][:, :].rearrange("p (h n) -> p h n", h=NH)).then_inc(s.gd_MTs.up, 1)
                    for t in range(NT):
                        act.wait_ge(*s.uw_mm(NT * dr + t + 1))
                        v = bank[4 + t][:, :].rearrange("p (h a n) -> p h a n", h=NH, a=2)
                        act.copy(un[:, t, :].rearrange("p (h n) -> p h n", h=NH), v[:, :, 0, :])
                        act.copy(wn[:, t, :].rearrange("p (h n) -> p h n", h=NH), v[:, :, 1, :]).then_inc(s.uw_ok.up, 1)
                    for t in range(NT):
                        act.wait_ge(*s.wq_mm(NT * dr + t + 1))
                        v = bank[t][:, :].rearrange("p (a c n) -> p a c n", a=2, c=2)
                        act.copy(wT[:, :, P * t:P * (t + 1)], v[:, 0, :, :])
                        act.copy(qtilT[:, :, P * t:P * (t + 1)], v[:, 1, :, :]).then_inc(s.wq_ok.up, 1)
                act.activation(zn[:, :, :], zn[:, :, :], ACT.Silu).then_inc(s.z_silu.up, 1)
                root(small[:, 160 + NH * tiles[0]:160 + NH * NT], s.gdy_sq, s.gdy_rs)
                for c in range(2):
                    act.wait_ge(*s.gdy_tp(c + 1))
                    act.copy(yT[:, 0, c, lo:TOK], bank[c][:, lo:TOK]).then_inc(s.gdy_ok.up, 1)

                act.wait_ge(*s.gdy_n(1))
                for br in (3, 2, 1, 0):
                    act.dma_start(wbr[:, br], d["w_branch"][l][br].rearrange("(k p) n -> p k n", p=P)).then_inc(branch_in[br], 16)
                n = 0
                for br in (3, 2, 1, 0):
                    for c in range(KD):
                        act.wait_ge(*s.mg_mm(n + 1))
                        if n >= 2:
                            act.wait_ge(*s.mg_add(n - 1))
                        act.activation(area(A_TR, 2, TOK)[:, n % 2, lo:TOK], bank[n % 2][:, lo:TOK], ACT.Sigmoid,
                                       bias=colB[:, V_BG + 8 * br + c:V_BG + 8 * br + c + 1]).then_inc(s.mg_sig.up, 1)
                        n += 1
                gate_rows(s.gb_m1, s.gb_ok1, [0, 1] if ctx_out else [1])
                act.wait_ge(*s.po_mm(1))
                post_squares(s.po_sq1, l, tiles)
                root(stat[:, 1, 8 + tiles[0]:12], s.po_ss1, s.po_rs1)
                act.wait_ge(*s.po_h1(len(tiles)))
                squares(s.ssq2, tiles, 4)
                root(stat[:, 0, 4 + tiles[0]:4 + NT], s.rms2, s.rs2)
                gate_rows(s.gb_m2, s.gb_ok2, [0, 1] if ctx_out else [1])
                prenorm_evac(1, s.tp2, s.v_ok, tiles)
                if l == 0:
                    act.wait_ge(*s.v_ok(KD))
                    load_vectors(1)

                sil = area(A_TR, 2, TOK)
                if ctx_out:
                    for f in range(NF):
                        act.wait_ge(*s.f_mm(f + 1))
                        if f >= 2:
                            act.wait_ge(*s.f_hid(f - 1))
                        act.activation(sil[:, f % 2, :], bank[f % 2][:, :], ACT.Silu).then_inc(s.f_sil.up, 1)
                    act.wait_ge(*s.f_out(1))
                    post_squares(s.po_sq2, l, tiles)
                    root(stat[:, 1, 8:12], s.po_ss2, s.po_rs2)
                else:
                    act.wait_ge(*s.rcomb(1))
                    act.activation(small[:, 188:190], small[:, 188:190], ACT.Exp).then_inc(s.rcomb.up, 1)
                    with act.Fori(0, NE) as e:
                        for f in range(NF):
                            act.wait_ge(*s.f_mm(NF * e + (f + 1)))
                            act.wait_ge(*s.f_hid(NF * e + (f + 1)))
                            act.activation(sil[:, f % 2, 0:SEQ], bank[f % 2][:, 0:SEQ], ACT.Silu).then_inc(s.f_sil.up, 1)
                    act.wait_ge(*s.f_acc(NE + 1))
                    for t in range(2):
                        if t:
                            act.wait_ge(*s.po_sq2(t))
                        act.activation(area(A_TR + 6144, D), macc[:, t, :], ACT.Square,
                                       accum_out=stat[:, 1, 10 + t:11 + t]).then_inc(s.po_sq2.up, 1)
                    root(stat[:, 1, 10:12], s.po_ss2, s.po_rs2)

        @block.gpsimd
        def _(pool):
            link = linker(pool, pool_chain)
            pool.wait_ge(consts_in, 32)

            for l in range(DEPTH):
                s = sig[l]
                ctx_out = l < DEPTH - 1
                t0 = 0 if ctx_out else 2
                if l:
                    pool.wait_ge(*sig[0].po_h2(NT))
                link(pool.memset(conv_in[:, :, :, 0:HALO], 0.0))
                pool.memset(conv_in[:, :, :, HALO + SEQ:], 0.0).then_inc(s.pad_ok.up, 1)

                for hh in range(NH):
                    pool.wait_ge(*s.rt_wm(2 * hh + 2))
                    wf, wb = area(A_TR + 2048, 4, SEQ), area(A_TR + 3072, 4, SEQ)
                    m = halfc[:, H_RM:H_RM + 1024].rearrange("p (d j n) -> p d j n", d=2, j=2)
                    link(pool.tensor_tensor(wf[:, 0:2, :], wf[:, 0:2, :], m[:, 0], ALU.mult))
                    link(pool.tensor_tensor(wb[:, 0:2, :], wb[:, 0:2, :], m[:, 1], ALU.mult))
                    if hh:
                        pool.wait_ge(*s.rt_p((2 if ctx_out else 1) * hh))
                    pool.tensor_tensor(area(A_TR + 4096, 4, SEQ), wf, wb, ALU.add).then_inc(s.rt_wok.up, 1)

                pool.wait_ge(*s.cT_mm(2 * NT))
                pool.memset(kz[HD:P, 0:NH:2, :], 0.0)
                pool.memset(kz[0:HD, 1:NH:2, :], 0.0).then_inc(s.kz_0.up, 1)
                for dr in range(2):
                    for t in range(NT):
                        n = NT * dr + t
                        pool.wait_ge(*s.gd_exp(n + 1))
                        if n >= 2:
                            pool.wait_ge(*s.gd_M(n - 1))
                            pool.wait_ge(*s.gd_A(n - 1))
                        if dr and t == 0:
                            pool.wait_ge(*s.st_oa(NT))
                        pool.tensor_tensor(Es[:, 0, n % 2], Eb[:, n % 2], gmask(dr, 0), ALU.mult)
                        pool.tensor_tensor(Es[:, 1, n % 2], Eb[:, n % 2], gmask(dr, 1), ALU.mult).then_inc(s.gd_es.up, 1)
                        if t >= 1:
                            for u in ([n - 1] if t < NT - 1 else [n - 1, n]):
                                ut = u % NT
                                eye = ident.unsqueeze(1).to_broadcast([P, NH, P])
                                pool.wait_ge(*s.gd_M(u + 1))
                                link(pool.tensor_tensor(X[:, ut], T1[:, ut], gmask(dr, 2), ALU.mult))
                                pool.tensor_tensor(X[:, ut], eye, X[:, ut], ALU.subtract).then_inc(s.gd_X.up, 1)
                                pool.wait_ge(*s.gd_MTs(u + 1))
                                link(pool.tensor_tensor(XT[:, ut], MT[:, ut], gmask(dr, 3), ALU.mult))
                                pool.tensor_tensor(XT[:, ut], eye, XT[:, ut], ALU.subtract).then_inc(s.gd_XT.up, 1)
                    pool.wait_ge(*s.gd_A(NT * (dr + 1)))
                    pool.wait_ge(*s.gl_e(dr + 1))
                    beta = gs[:, 0, :, NH * dr:NH * (dr + 1)]
                    link(pool.tensor_tensor(betaG[:, :, :], beta, gg[:, 3], ALU.mult))
                    q4, k4, v4 = (qkv[:, :, BW * i:BW * (i + 1)].rearrange("p t (h n) -> p t h n", h=NH) for i in range(3))
                    for t in range(NT):
                        pool.tensor_tensor(R[:, t, :, 0:HD], v4[:, t], beta[:, t].unsqueeze(2).to_broadcast([P, NH, HD]), ALU.mult)
                        ins = pool.tensor_tensor(R[:, t, :, HD:P], k4[:, t],
                                                 betaG[:, t].unsqueeze(2).to_broadcast([P, NH, HD]), ALU.mult)
                    ins.then_inc(s.gd_R.up, 1)
                    pool.wait_ge(*s.lv_mm1(LEVELS * NT * (dr + 1)))
                    for t in range(NT):
                        pool.tensor_tensor(qtil[:, t, :].rearrange("p (h n) -> p h n", h=NH), q4[:, t],
                                           gg[:, 3, t].unsqueeze(2).to_broadcast([P, NH, HD]), ALU.mult)
                        ins = pool.tensor_tensor(kdec[:, t, :].rearrange("p (h n) -> p h n", h=NH), k4[:, t],
                                                 gg[:, 4, t].unsqueeze(2).to_broadcast([P, NH, HD]), ALU.mult)
                    ins.then_inc(s.gd_q.up, 1)

        @block.vector
        def _(v):
            link = linker(v, dve_chain)
            v.wait_ge(consts_in, 32)
            v.wait_ge(h_in, 64)

            def per_head(x):
                return x.unsqueeze(2).to_broadcast([P, x.shape[1], HD])

            def mean_eps(x, n, g_ready):
                v.tensor_scalar(x, x, 1.0 / n, EPS, ALU.mult, ALU.add).then_inc(g_ready.up, 1)

            def inverse(x, g_done):
                v.wait_ge(*g_done(1))
                link(v.reciprocal(x, x))

            def prenorm(sub, g_sq, g_ss, g_rs, g_xs, g_tp, g_ok, tiles, at):
                v.wait_ge(*g_sq(len(tiles)))
                x = stat[:, 0, at + tiles[0]:at + NT]
                mean_eps(x, D, g_ss)
                inverse(x, g_rs)
                for t in tiles:
                    v.tensor_scalar(xs[:, t, :], h[:, t, :], stat[:, 0, at + t:at + t + 1], None, ALU.mult).then_inc(g_xs.up, 1)
                for k in range(0, KD, 2):
                    v.wait_ge(*g_tp(k + 1))
                    if k:
                        v.wait_ge(*g_ok(k))
                    for st in ((0, 1) if len(tiles) == NT else (1,)):
                        ins = v.tensor_scalar(uT[:, k, SEQ * st:SEQ * (st + 1)], bank[k % 4][:, SEQ * st:SEQ * (st + 1)],
                                              scl[:, sub, k, 1 - st:2 - st], mod[:, 24 * sub + k, 1 - st:2 - st],
                                              ALU.mult, ALU.add)
                    ins.then_inc(g_ok.up, 1)

            def gate_diag(sub, g_d, g_m, streams):
                for n in range(2 * len(streams)):
                    if n >= 2:
                        v.wait_ge(*g_m(n - 1))
                    st = streams[n // 2]
                    for q in range(4):
                        k = 4 * (n % 2) + q
                        ins = v.tensor_scalar(area(A_TR + 5120 + 512 * (n % 2), 4, P)[:, q], ident,
                                              gpost[:, sub, k, 1 - st:2 - st], None, ALU.mult)
                    ins.then_inc(g_d.up, 1)

            def post_add(g_sq, g_ss, g_rs, g_gb, g_h, tiles):
                t0, nt = tiles[0], len(tiles)
                v.wait_ge(*g_sq(2 * nt))
                ss = stat[:, 1, 0:8].rearrange("p (t a) -> p t a", a=2)
                x = stat[:, 1, 8 + t0:12]
                link(v.tensor_tensor(x, ss[:, t0:NT, 0], ss[:, t0:NT, 1], ALU.add))
                mean_eps(x, D, g_ss)
                inverse(x, g_rs)
                v.wait_ge(*g_gb(nt))
                for t in tiles:
                    for hf in range(2):
                        c = slice(512 * hf, 512 * (hf + 1))
                        link(v.scalar_tensor_tensor(area(A_TR + 512 * hf, 512), bank[2 * t + hf][:, :],
                                                    stat[:, 1, 8 + t:9 + t], GB[:, t // 2, c], ALU.mult, ALU.mult))
                        ins = v.tensor_tensor(h[:, t, c], h[:, t, c], area(A_TR + 512 * hf, 512), ALU.add)
                    ins.then_inc(g_h.up, 1)

            def rope(x, tmp, t, heads):
                tab = consts[:, C_ROPE + 64 * (t - 2):C_ROPE + 64 * (t - 1)]
                cs = tab[:, 0:32].unsqueeze(1).to_broadcast([P, heads, 32])
                sn = tab[:, 32:64].unsqueeze(1).to_broadcast([P, heads, 32])
                y = x.rearrange("p h (a n) -> p h a n", a=2)
                m = tmp.rearrange("p (q h n) -> p q h n", q=4, n=32)
                v.tensor_tensor(m[:, 0], y[:, :, 0], cs, ALU.mult)
                v.tensor_tensor(m[:, 1], y[:, :, 1], sn, ALU.mult)
                v.tensor_tensor(m[:, 2], y[:, :, 0], sn, ALU.mult)
                link(v.tensor_tensor(m[:, 3], y[:, :, 1], cs, ALU.mult))
                v.tensor_tensor(y[:, :, 0], m[:, 0], m[:, 1], ALU.subtract)
                link(v.tensor_tensor(y[:, :, 1], m[:, 2], m[:, 3], ALU.add))

            link(v.memset(S[:, :, :, :], 0.0))
            for l in range(DEPTH):
                s = sig[l]
                ctx_out = l < DEPTH - 1
                tiles = list(range(NT)) if ctx_out else [2, 3]
                t0 = tiles[0]
                streams = [0, 1] if ctx_out else [1]
                lo = 0 if ctx_out else SEQ

                v.wait_ge(*s.vec_T(1))
                v.tensor_copy(colA[:, :], bank[0][:, 0:80])
                link(v.tensor_copy(colB[:, :], bank[0][:, 80:142]))
                v.sem_inc(s.vec_ok.up, 1)
                v.wait_ge(*s.ada_mm(24))
                link(v.tensor_tensor(mod[:, :, :], bank[1][:, 0:96].rearrange("p (n a) -> p n a", a=2),
                                     colA[:, 0:48].unsqueeze(2).to_broadcast([P, 48, 2]), ALU.add))

                def gvec(i):
                    return colA[:, V_NG + 8 * i:V_NG + 8 * (i + 1)].unsqueeze(2).to_broadcast([P, KD, 2])

                for sub in range(2):
                    v.scalar_tensor_tensor(scl[:, sub], mod[:, 24 * sub + 8:24 * sub + 16, :], 1.0, gvec(2 * sub),
                                           ALU.add, ALU.mult)
                    link(v.tensor_tensor(gpost[:, sub], mod[:, 24 * sub + 16:24 * sub + 24, :], gvec(2 * sub + 1), ALU.mult))
                v.sem_inc(s.mod_ok.up, 1)
                prenorm(0, s.ssq1, s.rms1, s.rs1, s.xs1, s.tp1, s.u_ok, range(NT), 0)

                v.wait_ge(*s.win_ok(6))
                for j in range(TAPS):
                    for c in range(6):
                        o = conv_out[:, c, :].rearrange("p (a n) -> p a n", a=2)
                        x = conv_in[:, c, :, j:j + SEQ]
                        w = colB[:, V_CONV + 6 * j + c:V_CONV + 6 * j + c + 1]
                        if j == 0:
                            ins = v.tensor_scalar(o, x, w, None, ALU.mult)
                        else:
                            ins = v.scalar_tensor_tensor(o, x, w, o, ALU.mult, ALU.add)
                    link(ins)
                v.sem_inc(s.conv_ok.up, 1)

                v.wait_ge(prm_in[l], 96)
                v.wait_ge(*s.win_ok(9))
                v.tensor_tensor(gs[:, 4], gs[:, 3], dtb.unsqueeze(1).to_broadcast([P, NT, 8]), ALU.add).then_inc(s.ab_x.up, 1)
                v.wait_ge(*s.ab_e(1))
                v.wait_ge(*s.prm_e(1))
                v.tensor_scalar(lgam[:, :], prm_exp[:, 16:24], -1.0, None, ALU.mult).then_inc(s.rt_w.up, 1)
                link(v.tensor_scalar(gs[:, 6], gs[:, 6], 1.0, None, ALU.add))
                link(v.reciprocal(gs[:, 0], gs[:, 6]))
                link(v.scalar_tensor_tensor(gs[:, 8], gs[:, 4], 0.0, gs[:, 8], ALU.max, ALU.add))
                v.scalar_tensor_tensor(gs[:, 1], gs[:, 8], -1.0, prm_exp[:, 0:8].unsqueeze(1).to_broadcast([P, NT, 8]),
                                       ALU.mult, ALU.mult).then_inc(s.ab_ok.up, 1)

                v.wait_ge(*s.win_ok(15))
                v.wait_ge(*s.fn_mm2(2))
                gn = area(A_TR, NT, 8, HD)
                sq6 = area(A_TR + 4096, 6, HD)
                for t in range(NT):
                    x = gqn[:, t, 0:384].rearrange("p (h n) -> p h n", h=6)
                    link(v.tensor_tensor(sq6, x, x, ALU.mult))
                    ins = v.tensor_reduce(small[:, 32 + 6 * t:38 + 6 * t], sq6, AX, ALU.add)
                    link(ins)
                mean_eps(small[:, 32:56], HD, s.gq_sq)
                inverse(small[:, 32:56], s.gq_rs)
                for t in range(NT):
                    x = gqn[:, t, 0:384].rearrange("p (h n) -> p h n", h=6)
                    link(v.tensor_tensor(sq6, x, per_head(small[:, 32 + 6 * t:38 + 6 * t]), ALU.mult))
                    v.tensor_tensor(x[:, 0:4], sq6[:, 0:4], qkg[:, 0:HD].unsqueeze(1).to_broadcast([P, 4, HD]), ALU.mult)
                    link(v.tensor_tensor(x[:, 4:6], sq6[:, 4:6], qkg[:, HD:2 * HD].unsqueeze(1).to_broadcast([P, 2, HD]), ALU.mult))
                    if t >= 2:
                        rope(x, area(A_TR + 4608, 768), t, 6)
                    v.tensor_copy(gn[:, t, 0:4, :], x[:, 0:4])
                    for q in range(4):
                        ins = v.tensor_copy(gn[:, t, 4 + q, :], x[:, 4 + q // 2])
                    link(ins)
                v.sem_inc(s.gq_n.up, 1)
                work = [(t, hh) for t in tiles for hh in range(NH)]
                PTb = area(A_TR + 5632, 2, 4, P)
                og = area(A_TR, NT, BW)

                def gq_max(n):
                    t, hh = work[n]
                    keys = SEQ if t < 2 else TOK
                    v.wait_ge(*s.gq_s(n + 1))
                    link(v.tensor_reduce(small[:, 64 + n:65 + n], bank[n % 2][:, 0:keys], AX, ALU.max))
                    v.tensor_scalar(small[:, n:n + 1], small[:, 64 + n:65 + n], -HD ** -0.5, None, ALU.mult).then_inc(s.gq_max.up, 1)

                def gq_pt(n):
                    nk = 2 if work[n][0] < 2 else 4
                    v.wait_ge(*s.gq_pt(n + 1))
                    if n >= 2:
                        v.wait_ge(*s.gq_o(n - 1))
                    v.tensor_copy(PTb[:, n % 2, 0:nk, :], bank[2 + n % 2][:, 0:P * nk].rearrange("p (a n) -> p a n", a=nk)).then_inc(s.gq_ptc.up, 1)

                def gq_norm(n):
                    t, hh = work[n]
                    v.wait_ge(*s.gq_o(n + 1))
                    link(v.reciprocal(small[:, 80 + n:81 + n], small[:, 16 + n:17 + n]))
                    v.tensor_scalar(og[:, t, HD * hh:HD * (hh + 1)], bank[4 + n % 2][:, 0:HD], small[:, 80 + n:81 + n],
                                    None, ALU.mult).then_inc(s.gq_on.up, 1)

                v.wait_ge(*s.gq_tp(NT))
                for n in range(len(work) + 2):
                    if n < len(work):
                        gq_max(n)
                    if 1 <= n <= len(work):
                        gq_pt(n - 1)
                    if n >= 2:
                        gq_norm(n - 2)

                v.wait_ge(*s.win_ok(23))
                v.wait_ge(*s.gq_yt(2))
                for t in (2, 3):
                    for q in range(2):
                        rope(rtn[:, t, 256 * q:256 * (q + 1)].rearrange("p (h n) -> p h n", h=NH),
                             area(A_TR + 5120, 512), t, NH)
                v.sem_inc(s.rt_n.up, 1)
                PR = area(A_TR + 5120, 2, 4, SEQ)
                runits = [(hh, st) for hh in range(NH) for st in streams]
                for n, (hh, st) in enumerate(runits):
                    v.wait_ge(*s.rt_s(n + 1))
                    v.wait_ge(*s.rt_wok(hh + 1))
                    if n >= 2:
                        v.wait_ge(*s.rt_o(n - 1))
                    wsum = area(A_TR + 4096, 4, SEQ)
                    for q in range(1 + st):
                        wq = wsum[:, 2:4, :] if (st == 1 and q == 0) else wsum[:, 0:2, :]
                        ins = v.scalar_tensor_tensor(PR[:, n % 2, 2 * q:2 * q + 2, :],
                                                     bank[4 + 2 * (n % 2) + q][:, :].rearrange("p (a n) -> p a n", a=2),
                                                     HD ** -0.5, wq, ALU.mult, ALU.mult)
                    ins.then_inc(s.rt_p.up, 1)
                v.wait_ge(*s.rt_o(len(runits)))
                orr, cen = area(A_TR, NT, BW), area(A_TR + 1024, NT, BW)
                o4 = orr.rearrange("p t (h n) -> p t h n", h=NH)
                c4 = cen.rearrange("p t (h n) -> p t h n", h=NH)
                mu = small[:, 96:96 + NT * NH].rearrange("p (t h) -> p t h", t=NT)
                va = small[:, 112:112 + NT * NH].rearrange("p (t h) -> p t h", t=NT)
                for t in tiles:
                    ins = v.tensor_copy(orr[:, t, :], bank[t][:, 0:BW])
                link(ins)
                link(v.tensor_reduce(mu[:, t0:NT], o4[:, t0:NT], AX, ALU.add))
                link(v.tensor_scalar(mu[:, t0:NT], mu[:, t0:NT], 1.0 / HD, None, ALU.mult))
                for t in tiles:
                    ins = v.tensor_tensor(o4[:, t], o4[:, t], per_head(mu[:, t]), ALU.subtract)
                link(ins)
                link(v.tensor_tensor(cen[:, t0:NT], orr[:, t0:NT], orr[:, t0:NT], ALU.mult))
                link(v.tensor_reduce(va[:, t0:NT], c4[:, t0:NT], AX, ALU.add))
                mean_eps(va[:, t0:NT], HD, s.rt_var)
                inverse(va[:, t0:NT], s.rt_rs)
                v.wait_ge(*s.rt_silu(1))
                for t in tiles:
                    link(v.tensor_tensor(o4[:, t], o4[:, t], per_head(va[:, t]), ALU.mult))
                    link(v.tensor_tensor(orr[:, t], orr[:, t], retg, ALU.mult))
                    ins = v.tensor_tensor(orr[:, t], orr[:, t], area(A_TR + 3072, NT, BW)[:, t], ALU.mult)
                link(ins)
                v.sem_inc(s.rt_on.up, 1)

                ss8 = small[:, 128:160].rearrange("p (t h) -> p t h", t=NT)
                for t in range(NT):
                    v.wait_ge(*s.cT_ok(2 * t + 1))
                    x = qkv[:, t, 0:512].rearrange("p (h n) -> p h n", h=8)
                    sq = area(A_TR + 4096, 8, HD)
                    link(v.tensor_tensor(sq, x, x, ALU.mult))
                    link(v.tensor_reduce(ss8[:, t], sq, AX, ALU.add))
                mean_eps(ss8, 1, s.l2_sq)
                inverse(ss8, s.l2_rs)
                link(v.tensor_scalar(ss8[:, :, 0:NH], ss8[:, :, 0:NH], HD ** -0.5, None, ALU.mult))
                v.wait_ge(*s.cT_ok(2 * NT))
                for t in range(NT):
                    x = qkv[:, t, 0:512].rearrange("p (h n) -> p h n", h=8)
                    ins = v.tensor_tensor(x, x, per_head(ss8[:, t]), ALU.mult)
                link(ins)
                v.sem_inc(s.l2_ok.up, 1)
                v.wait_ge(*s.gl_mm(1))
                link(v.tensor_copy(gs[:, 9:12], bank[0][:, 0:96].rearrange("p (a t n) -> p a t n", a=3, t=NT)))
                for dr in range(2):
                    hd = slice(NH * dr, NH * (dr + 1))
                    if dr:
                        v.wait_ge(*s.gd_q(1))
                    v.tensor_copy(gg[:, 0], gs[:, 9 + dr, :, hd])
                    v.tensor_scalar(negG[:, :, :], gs[:, 9 + dr, :, hd], -1.0, None, ALU.mult)
                    v.tensor_tensor(gg[:, 1], gs[:, 11, :, hd], gs[:, 9 + dr, :, hd], ALU.subtract)
                    link(v.tensor_copy(gg[:, 2], gs[:, 11, :, hd]))
                    v.sem_inc(s.gl_ok.up, 1)

                    def tile_matrices(n):
                        t = n % NT
                        v.wait_ge(*s.gd_es(n + 1))
                        for hh in range(NH):
                            ins = v.scalar_tensor_tensor(T1[:, t, hh, :], bank[2 + n % 2][:, P * hh:P * (hh + 1)],
                                                         gs[:, 0, t, NH * dr + hh:NH * dr + hh + 1], Es[:, 0, n % 2, hh, :],
                                                         ALU.mult, ALU.mult)
                        ins.then_inc(s.gd_M.up, 1)
                        v.tensor_tensor(AT[:, t], bank[4 + n % 2][:, :].rearrange("p (h n) -> p h n", h=NH),
                                        Es[:, 1, n % 2], ALU.mult).then_inc(s.gd_A.up, 1)

                    for n in range(NT * dr, NT * dr + NT):
                        tile_matrices(n)
                    v.wait_ge(*s.gd_X(NT * (dr + 1)))
                    v.wait_ge(*s.gd_MT(NT * (dr + 1)))
                    for q in range(LEVELS):
                        base = (LEVELS * dr + q) * NT
                        for t in range(NT):
                            v.wait_ge(*s.lv_mm1(base + t + 1))
                            v.tensor_tensor(T1[:, t], bank[t][:, :].rearrange("p (h n) -> p h n", h=NH),
                                            gmask(dr, 4 + q), ALU.mult).then_inc(s.lv_T1.up, 1)
                        for t in range(NT):
                            v.wait_ge(*s.lv_mm2(base + t + 1))
                            if q < LEVELS - 1:
                                v.tensor_tensor(X[:, t], X[:, t], bank[4 + t][:, :].rearrange("p (h n) -> p h n", h=NH),
                                                ALU.subtract)
                            v.tensor_tensor(XT[:, t], XT[:, t], bank[t][:, :].rearrange("p (h n) -> p h n", h=NH),
                                            ALU.subtract).then_inc(s.lv_X.up, 1)
                    v.wait_ge(*s.uw_ok(NT * (dr + 1)))
                    v.wait_ge(*s.gl_e(dr + 1))
                    for i, t in enumerate((0, 1, 2, 3) if dr == 0 else (1, 0, 3, 2)):
                        n = NT * dr + i
                        if i == 0:
                            v.tensor_copy(vnew[:, t, :], un[:, t, :]).then_inc(s.st_v.up, 1)
                        else:
                            v.wait_ge(*s.st_mm(n - dr))
                            v.tensor_tensor(vnew[:, t, :], un[:, t, :], bank[4][:, 0:BW], ALU.subtract).then_inc(s.st_v.up, 1)
                        if i < NT - 1:
                            v.wait_ge(*s.st_s(n - dr + 1))
                            for hh in range(NH):
                                part, c = slice(HD * (hh % 2), HD * (hh % 2 + 1)), hh // 2
                                own = slice(HD * (hh % 2), HD * (hh % 2 + 1))
                                new = S[part, (i + 1) % 2, c, own]
                                upd = bank[5][part, P * c + HD * (hh % 2):P * c + HD * (hh % 2 + 1)]
                                if i == 0:
                                    ins = v.tensor_copy(new, upd)
                                else:
                                    ins = v.scalar_tensor_tensor(new, S[part, i % 2, c, own], gg[part, 5, t, hh:hh + 1], upd,
                                                                 ALU.mult, ALU.add)
                            link(ins)
                            v.sem_inc(s.st_S.up, 1)
                        v.wait_ge(*s.st_o(n + 1))
                        if dr == 0:
                            ins = v.tensor_copy(o_gdn[:, t, :], bank[6 + n % 2][:, 0:BW])
                        else:
                            ins = v.tensor_tensor(o_gdn[:, t, :], o_gdn[:, t, :], bank[6 + n % 2][:, 0:BW], ALU.add)
                        link(ins)
                        v.sem_inc(s.st_oa.up, 1)

                og4 = o_gdn.rearrange("p t (h n) -> p t h n", h=NH)
                ssg = small[:, 160:176].rearrange("p (t h) -> p t h", t=NT)
                link(v.tensor_tensor(wn[:, t0:NT], o_gdn[:, t0:NT], o_gdn[:, t0:NT], ALU.mult))
                ins = v.tensor_reduce(ssg[:, t0:NT], wn.rearrange("p t (h n) -> p t h n", h=NH)[:, t0:NT], AX, ALU.add)
                link(ins)
                mean_eps(ssg[:, t0:NT], HD, s.gdy_sq)
                inverse(ssg[:, t0:NT], s.gdy_rs)
                v.wait_ge(*s.z_silu(1))
                for t in tiles:
                    y = un[:, t, :].rearrange("p (h n) -> p h n", h=NH)
                    link(v.tensor_tensor(y, og4[:, t], per_head(ssg[:, t]), ALU.mult))
                    link(v.tensor_tensor(y, y, gdng.unsqueeze(1).to_broadcast([P, NH, HD]), ALU.mult))
                    ins = v.tensor_tensor(un[:, t], un[:, t], zn[:, t], ALU.mult)
                link(ins)
                v.sem_inc(s.gdy_n.up, 1)

                for n in range(4 * KD):
                    c = n % KD
                    v.wait_ge(*s.mg_sig(n + 1))
                    g = area(A_TR, 2, TOK)[:, n % 2, lo:TOK]
                    if n < KD:
                        ins = v.tensor_tensor(accT[:, c, lo:TOK], g, bank[2 + n % 2][:, lo:TOK], ALU.mult)
                    else:
                        link(v.tensor_tensor(g, g, bank[2 + n % 2][:, lo:TOK], ALU.mult))
                        ins = v.tensor_tensor(accT[:, c, lo:TOK], accT[:, c, lo:TOK], g, ALU.add)
                    ins.then_inc(s.mg_add.up, 1)
                gate_diag(0, s.gb_d1, s.gb_m1, streams)
                post_add(s.po_sq1, s.po_ss1, s.po_rs1, s.gb_ok1, s.po_h1, tiles)
                gate_diag(1, s.gb_d2, s.gb_m2, streams)
                prenorm(1, s.ssq2, s.rms2, s.rs2, s.xs2, s.tp2, s.v_ok, tiles, 4)

                sil = area(A_TR, 2, TOK)
                if ctx_out:
                    for f in range(NF):
                        v.wait_ge(*s.f_sil(f + 1))
                        v.tensor_tensor(hid[:, f, :], sil[:, f % 2, :], bank[2 + f % 2][:, :], ALU.mult).then_inc(s.f_hid.up, 1)
                    post_add(s.po_sq2, s.po_ss2, s.po_rs2, s.gb_ok2, s.po_h2, tiles)
                    continue

                v.wait_ge(*s.rlog(1))
                lg, pick1, pick2, t_a, t_b, comb = (route[:, i] for i in range(6))
                idx = iota8[:, :].unsqueeze(1).to_broadcast([P, 2, NE])
                m1, m2, mi, e1, e2, rr = (small[:, 180 + 2 * i:182 + 2 * i] for i in range(6))

                def along(x):
                    return x.unsqueeze(2).to_broadcast([P, 2, NE])

                def first_max(scores, m, pick):
                    link(v.tensor_reduce(m, scores, AX, ALU.max))
                    link(v.tensor_tensor(t_a, scores, along(m), ALU.is_equal))
                    link(v.scalar_tensor_tensor(t_b, idx, float(-NE), t_a, ALU.add, ALU.mult))
                    link(v.tensor_reduce(mi, t_b, AX, ALU.min))
                    link(v.tensor_scalar(mi, mi, float(NE), None, ALU.add))
                    link(v.tensor_tensor(pick, idx, along(mi), ALU.is_equal))

                link(v.tensor_copy(lg, bank[0][:, 0:2 * NE].rearrange("p (t e) -> p t e", t=2)))
                first_max(lg, m1, pick1)
                link(v.tensor_scalar(t_a, pick1, -1.0, 1.0, ALU.mult, ALU.add))
                link(v.tensor_tensor(lg, lg, t_a, ALU.mult))
                link(v.scalar_tensor_tensor(lg, pick1, -3.0e38, lg, ALU.mult, ALU.add))
                first_max(lg, m2, pick2)
                link(v.tensor_tensor(e2, m2, m1, ALU.subtract))
                v.sem_inc(s.rcomb.up, 1)
                v.wait_ge(*s.rcomb(2))
                link(v.tensor_scalar(e1, e2, 1.0, None, ALU.add))
                link(v.reciprocal(rr, e1))
                link(v.tensor_tensor(e2, e2, rr, ALU.mult))
                link(v.tensor_tensor(pick1, pick1, along(rr), ALU.mult))
                link(v.tensor_tensor(pick2, pick2, along(e2), ALU.mult))
                link(v.tensor_tensor(comb, pick1, pick2, ALU.add))
                link(v.memset(macc[:, :, :], 0.0))
                v.sem_inc(s.f_hid.semaphore, 2)
                v.sem_inc(s.f_acc.semaphore, 1)
                with v.Fori(0, NE) as e:
                    for f in range(NF):
                        v.wait_ge(*s.f_sil(NF * e + (f + 1)))
                        v.tensor_tensor(hid[:, f, 0:SEQ], sil[:, f % 2, 0:SEQ], bank[2 + f % 2][:, 0:SEQ],
                                        ALU.mult).then_inc(s.f_hid.up, 1)
                    v.wait_ge(*s.f_out(e + 1))
                    v.wait_ge(*s.f_acc(e + 1))
                    for t in range(2):
                        for hf in range(2):
                            c = slice(512 * hf, 512 * (hf + 1))
                            ins = v.scalar_tensor_tensor(macc[:, t, c], bank[4 + 2 * t + hf][:, :], comb[:, t, bass.ds(e, 1)],
                                                         macc[:, t, c], ALU.mult, ALU.add)
                    ins.then_inc(s.f_acc.up, 1)
                v.wait_ge(*s.po_sq2(2))
                mean_eps(stat[:, 1, 10:12], D, s.po_ss2)
                inverse(stat[:, 1, 10:12], s.po_rs2)
                v.wait_ge(*s.gb_ok2(2))
                for t in range(2):
                    link(v.scalar_tensor_tensor(area(A_TR + D * t, D), macc[:, t, :], stat[:, 1, 10 + t:11 + t], GB[:, 1, :],
                                                ALU.mult, ALU.mult))
                    v.tensor_tensor(h[:, 2 + t, :], h[:, 2 + t, :], area(A_TR + D * t, D), ALU.add).then_inc(s.po_h2.up, 1)

        for signal, (name, total) in zip(sig[0], SIGNALS.items()):
            assert signal.raised == total, (name, signal.raised)


def shape_constants():
    import numpy as np
    i = np.arange(P)
    c = np.zeros((P, C_END), np.float32)
    c[:, C_ID:C_ID + P] = np.eye(P)
    c[:, C_ONE:C_ONE + P] = 1
    c[:, C_U:C_U + P] = i[:, None] <= i[None]
    c[:, C_L:C_L + P] = i[:, None] >= i[None]
    tok = np.arange(SEQ)
    inv = np.float32(10000.0) ** (-np.arange(HD // 4, dtype=np.float32) / np.float32(HD // 4))
    ang = np.concatenate([(tok // 64).astype(np.float32)[:, None] * inv, (tok % 64).astype(np.float32)[:, None] * inv], 1)
    rope = np.stack([np.cos(ang), np.sin(ang)], 1).reshape(2, P, 64)
    c[:, C_ROPE:C_ROPE + 128] = rope.transpose(1, 0, 2).reshape(P, 128)
    a = 2 * np.pi * np.outer(np.arange(HD), np.arange(HD)) / HD
    for cs, f in enumerate((np.cos(a), np.sin(a))):
        c[:, C_FD + P * cs:C_FD + P * (cs + 1)] = np.kron(np.eye(2), f / np.sqrt(SEQ * HD))
    a = 2 * np.pi * (np.outer(tok, tok) % SEQ) / SEQ
    ft = np.stack([np.cos(a), -np.sin(a)], 1).reshape(2, P, 2, SEQ)
    c[:, C_FT:C_FT + 1024] = ft.transpose(1, 0, 2, 3).reshape(P, 1024)

    g = np.zeros((P, H_END), np.float16)
    r, q = i[:, None], i[None]
    for dr in range(2):
        low = [r > q, r <= q]
        for lv in range(1 + LEVELS):
            sz = 2 ** lv
            m = (r // (2 * sz) == q // (2 * sz)) & (r // sz % 2 == 1) & (q // sz % 2 == 0)
            low += [m, m.T] if lv == 0 else [m]
        for n, m in enumerate(low):
            g[:, (10 * dr + n) * P:(10 * dr + n + 1) * P] = m.T if dr else m
    key = np.arange(SEQ)[:, None]
    qry = np.arange(SEQ)[None]
    for dr in range(2):
        same = (key - qry) if dr else (qry - key)
        far = (SEQ - qry + key) if dr else (SEQ + qry - key)
        dist = np.concatenate([np.maximum(same, 0), far]).reshape(4, P, SEQ)
        g[:, H_DIST + 1024 * dr:H_DIST + 1024 * (dr + 1)] = dist.transpose(1, 0, 2).reshape(P, 1024)
        msk = (same >= 0).astype(np.float16).reshape(2, P, SEQ)
        g[:, H_RM + 512 * dr:H_RM + 512 * (dr + 1)] = msk.transpose(1, 0, 2).reshape(P, 512)
    iota8 = np.tile(np.arange(NE, dtype=np.float32), (P, 1))
    return {"consts": c, "halfc": g, "iota8": iota8}


_INS = ["x", "c", "ctx", "c_ctx", "ada_w", "ada_b", "norm_g", "w_in", "conv_w", "gdn_a_log", "gdn_dt_bias",
        "gdn_norm_g", "ret_log_decay_raw", "ret_norm_g", "qk_norm_g", "w_branch", "w_gate", "b_gate", "w_out",
        "ffn_w1", "ffn_w3", "ffn_w2", "moe_router", "moe_w1", "moe_w3", "moe_w2"]


def kernel(**inputs):
    import numpy as _np
    import concourse.bacc as _bacc
    from concourse.bass_utils import run_bass_kernel_spmd as _run

    nc = _bacc.Bacc("TRN2", target_bir_lowering=False, num_devices=1)
    arrays, d = {}, {}
    given = {name: inputs[name] for name in _INS}
    for name, a in {**given, **shape_constants()}.items():
        a = _np.ascontiguousarray(a)
        arrays[f"in_{name}_dram"] = a
        d[name] = nc.dram_tensor(f"in_{name}_dram", a.shape, mybir.dt.from_np(a.dtype), kind="ExternalInput").ap()
    for name in ("moe_w1", "moe_w3", "moe_w2"):
        d[name] = d[name].rearrange("a e k n -> (a e) k n")
    out = nc.dram_tensor("out_dram", (1, SEQ, D), F32, kind="ExternalOutput").ap()
    build_program(nc, d, out.rearrange("b t n -> (b t) n"))
    r = _run(nc, [arrays], core_ids=[0])
    return r.results[0]["out_dram"]
```

```python
from collections import namedtuple
from contextlib import ExitStack

import concourse.bass as bass
from concourse import mybir

F32 = mybir.dt.float32
F32R = mybir.dt.float32r
F16 = mybir.dt.float16
I32 = mybir.dt.int32
ACT = mybir.ActivationFunctionType
ALU = mybir.AluOpType
AX = mybir.AxisListType.X

P = 128
D = 1024
KD = D // P
SEQ = 256
TOK = 2 * SEQ
NT = TOK // P
DEPTH = 2
BW = 256
HD = 64
NH = BW // HD
OFF_Z, OFF_AB, OFF_RET, OFF_GQA, OFF_F = 768, 1024, 1040, 2064, 2576
D_FF = 2816
NF = D_FF // P
NE = 8
EPS = 1e-6
CW = 256
MW = 32
AHEAD = (4, 6)
UNITS = 15
NADA = 6 * D // CW
RING = 6
LEVELS = 6
HALO = 2
TAPS = 5

C_ID, C_ONE, C_U, C_L, C_ROPE, C_FD, C_FT = 0, 128, 256, 384, 512, 640, 896
C_END = C_FT + 1024
H_MASK = 0
H_DIST = 2 * 10 * P
H_RM = H_DIST + 2 * 4 * SEQ
H_END = H_RM + 2 * 2 * SEQ

A_CI = 0
A_CO = A_CI + 6 * 2 * (SEQ + 2 * HALO)
A_Z = A_CO + 6 * TOK
A_GQ = A_Z + NT * BW
A_RT = A_GQ + NT * 512
A_FT = A_RT + NT * 1024
A_YT = A_FT + 2 * TOK
A_TR = A_YT + 4 * 2 * TOK
A_END = A_TR + 7168
A_GS = KD * TOK
A_WB = A_GS + 6 * D
A_ADA = NF * TOK
A_VEC = A_TR + 6656

V_ADA, V_NG, V_BG, V_CONV = 0, 48, 0, 32

REUSED = ("gq_s", "gq_max", "gq_e", "gq_pt", "gq_ptc", "gq_o", "gq_on")
SIGNALS = {
    "vec_T": 1, "vec_ok": 1, "ada_mm": 25, "ada_row": 24, "mod_ok": 1,
    "ssq1": 4, "rms1": 1, "rs1": 1, "xs1": 4, "tp1": 8, "u_ok": 8, "ssq2": 4, "rms2": 1, "rs2": 1, "xs2": 4, "tp2": 8, "v_ok": 8,
    "pad_ok": 1, "win_mm": 23, "win_ok": 23, "conv_ok": 1, "silu_ok": 6, "ab_x": 1, "prm_e": 1, "ab_e": 1, "ab_ok": 1,
    "fn_mm1": 4, "fn_c": 4, "fn_mm2": 2, "fn_ok": 2,
    "gq_sq": 1, "gq_rs": 1, "gq_n": 1, "gq_tp": 4, "gq_T": 4, "gq_s": 16, "gq_max": 16, "gq_e": 16, "gq_pt": 16, "gq_ptc": 16, "gq_o": 16, "gq_on": 16, "gq_yt": 2, "gq_y": 2,
    "rt_n": 1, "rt_tp": 4, "rt_T": 4, "rt_w": 1, "rt_wm": 8, "rt_wok": 4, "rt_s": 8, "rt_p": 8, "rt_o": 8, "rt_var": 1, "rt_rs": 1, "rt_on": 1, "rt_silu": 1, "rt_yt": 2, "rt_y": 2,
    "cT_mm": 8, "cT_ok": 8, "kz_0": 1, "l2_sq": 1, "l2_rs": 1, "l2_ok": 1, "qk_mm": 4, "qk_ok": 4, "gl_mm": 1, "gl_ok": 2, "gl_e": 2,
    "gd_mm": 8, "gd_abs": 8, "gd_exp": 8, "gd_es": 8, "gd_M": 8, "gd_A": 8, "gd_MT": 8, "gd_MTs": 8, "gd_X": 8, "gd_XT": 8,
    "lv_mm1": 48, "lv_T1": 48, "lv_mm2": 48, "lv_X": 48, "gd_R": 2, "uw_mm": 8, "uw_ok": 8, "gd_q": 2, "wq_mm": 8, "wq_ok": 8,
    "st_mm": 6, "st_v": 8, "st_o": 8, "st_s": 6, "st_S": 6, "st_oa": 8,
    "z_silu": 1, "gdy_sq": 1, "gdy_rs": 1, "gdy_n": 1, "gdy_tp": 2, "gdy_ok": 2,
    "mg_mm": 32, "mg_sig": 32, "mg_add": 32,
    "gb_d1": 4, "gb_m1": 4, "gb_ok1": 4, "gb_d2": 4, "gb_m2": 4, "gb_ok2": 4,
    "po_mm": 1, "po_sq1": 8, "po_ss1": 1, "po_rs1": 1, "po_h1": 4, "po_sq2": 8, "po_ss2": 1, "po_rs2": 1, "po_h2": 4,
    "f_mm": 0, "f_sil": 22, "f_hid": 22, "f_out": 1, "f_acc": 0, "rlog": 0, "rcomb": 0,
    "m_hTs": 98, "m_y": 98, "m_sel": 38, "m_st": 98, "m_sT": 38,
}



class Signal:

    def __init__(self, semaphore, base):
        self.semaphore, self.base, self.raised = semaphore, base, 0

    def __call__(self, n):
        return self.semaphore, self.base + n

    @property
    def up(self):
        self.raised += 1
        return self.semaphore


Signals = namedtuple("Signals", list(SIGNALS))


def build_program(nc, d, out):
    with ExitStack() as ctx:
        def sb(name, shape, dt=F32):
            return ctx.enter_context(nc.sbuf_tensor(name, shape, dt))

        def sem(name):
            return ctx.enter_context(nc.semaphore(name))

        bank = [ctx.enter_context(nc.psum_tensor(f"bank{i}", [P, 512], F32)) for i in range(8)]
        consts = sb("consts", [P, C_END])
        halfc = sb("halfc", [P, H_END], F16)
        h = sb("h", [P, NT, D])
        uT = sb("uT", [P, KD, TOK])
        ring = sb("ring", [P, RING, KD * CW])
        arena = sb("arena", [P, A_END])
        colA = sb("colA", [P, 80])
        colB = sb("colB", [P, 62])
        silu_c = sb("silu_c", [P, 2, KD])
        mod = sb("mod", [P, 48, 2])
        scl = sb("scl", [P, 2, KD, 2])
        gpost = sb("gpost", [P, 2, KD, 2])
        stat = sb("stat", [P, 2, 4 * NT])
        bc = sb("bc", [P, 256 + HD + 2 * HD + 8 + 8 + 8])
        retg, gdng, qkg = bc[:, 0:256], bc[:, 256:320], bc[:, 320:448]
        alog, dtb, rraw = bc[:, 448:456], bc[:, 456:464], bc[:, 464:472]
        lgam = sb("lgam", [P, 8])
        gs = sb("gs", [P, 12, NT, 8])
        negG = sb("negG", [P, NT, NH])
        betaG = sb("betaG", [P, NT, NH])
        gg = sb("gg", [P, 6, NT, NH])
        S = sb("S", [P, 2, 2, P])
        small = sb("small", [P, 256])
        prm_exp = sb("prm_exp", [P, 24])
        rt8 = sb("rt8", [P, KD, NE])
        iota = sb("iota", [P, P])

        ident = consts[:, C_ID:C_ID + P]
        ones = consts[:, C_ONE:C_ONE + P]
        tri = [consts[:, C_U:C_U + P], consts[:, C_L:C_L + P]]

        def gmask(dr, n):
            return halfc[:, (10 * dr + n) * P:(10 * dr + n + 1) * P].unsqueeze(1).to_broadcast([P, 4, P])

        def area(at, *shape):
            n = 1
            for x in shape:
                n *= x
            v = arena[:, at:at + n]
            names = "abcd"[:len(shape)]
            if len(shape) == 1:
                return v
            return v.rearrange(f"p ({' '.join(names)}) -> p {' '.join(names)}",
                               **{names[i]: shape[i] for i in range(1, len(shape))})

        conv_in = area(A_CI, 6, 2, SEQ + 2 * HALO)
        qkv = area(A_CI, NT, 768)
        conv_out = area(A_CO, 6, TOK)
        qT = area(A_CO, 2, TOK)
        kz = area(A_CO + 1024, NH, TOK)
        Eb = area(A_TR + 6144, 2, NH, P)
        zn = area(A_Z, NT, BW)
        gqn = area(A_GQ, NT, 512)
        rtn = area(A_RT, NT, 1024)
        X, XT, MT = (area(A_GQ + 2048 * i, NT, NH, P) for i in range(3))
        qtilT, kdec = area(A_GQ, 2, TOK), area(A_GQ + 1024, NT, BW)
        wT, qtil = area(A_GQ + 4096, 2, TOK), area(A_GQ + 5120, NT, BW)
        fT = area(A_FT, 2, TOK)
        o_gdn = area(A_FT, NT, BW)
        yT = area(A_YT, 4, 2, TOK)
        GB = area(A_YT, 2, D)
        macc = area(A_YT + 2048, 2, D)
        AT, T1 = area(A_TR, NT, NH, P), area(A_TR + 2048, NT, NH, P)
        un, wn = area(A_TR + 2048, NT, BW), area(A_TR + 3072, NT, BW)
        Es = area(A_TR + 4096, 2, 2, NH, P)
        R = area(A_TR + 4096, NT, NH, P)
        vnew = area(A_TR + 4096, NT, BW)
        xs, junk = area(A_TR, NT, D), area(A_TR + 4096, D)
        accT = area(A_CI, KD, TOK)

        arena_at, u_at = nc.lookup_mloc(arena).addr, nc.lookup_mloc(uT).addr

        def parts(name, at, words, *shape):
            return [nc.alloc_sbuf_tensor_at(f"{name}_{'hl'[q]}", [P, *shape], F32R, offset=at + 4 * words * q)
                    for q in range(2)]

        GB_END = A_YT + 2 * D
        dsp = parts("dsp", arena_at + 4 * GB_END, 3 * D, 3, D)
        x_hi = [nc.alloc_sbuf_tensor_at(f"x_hi{q}", [P, n, TOK], F32R, offset=arena_at + 4 * at)
                for q, (n, at) in enumerate(((6, A_ADA), (2, GB_END + 6 * D)))]
        x_lo = nc.alloc_sbuf_tensor_at("x_lo", [P, KD, TOK], F32R, offset=u_at)
        hsp = parts("hsp", arena_at + 4 * A_ADA, 3 * TOK, 3, TOK)
        gsp = parts("gsp", arena_at + 4 * A_GS, 3 * D, 3, D)
        xg_hi = nc.alloc_sbuf_tensor_at("xg_hi", [P, KD, TOK], F32R, offset=arena_at + 4 * (A_TR + 2 * TOK))
        sil0 = area(GB_END + 7 * D, 2, TOK)

        def x_high(k):
            return x_hi[k // 6][:, k % 6, :]

        wsp = parts("wsp", arena_at, 4 * D, 4, D)
        hTs = parts("hTs", arena_at + 4 * 8 * D, NF * P, NF, P)
        vns = parts("vns", arena_at + 4 * A_TR, 2 * D, 2, D)
        sel_r = nc.alloc_sbuf_tensor_at("sel_r", [P, 2, P], F32R, offset=arena_at + 4 * (A_TR + 4096))
        sel, selT = area(A_TR + 4352, 2, P), area(A_TR + 4608, 2, P)
        xTs = parts("xTs", u_at, D, KD, P)
        hn, sil2 = uT[:, 4, :].rearrange("p (a n) -> p a n", a=2), uT[:, 5, :].rearrange("p (a n) -> p a n", a=2)
        ysb = uT[:, 6:8, :].rearrange("p a n -> p (a n)")
        rank = area(A_TR + 4992, 2, NE + 1)
        comb = area(A_TR + 5024, 2, NE + 1)
        crowded = sb("crowded", [P, 1], I32)
        route = area(A_TR + 4864, 6, 2, NE)
        wbr = area(A_WB, 2, 2, D)
        hid = area(0, NF, TOK)
        vecA, vecB = arena[0:80, A_VEC:A_VEC + P], arena[0:62, A_VEC + P:A_VEC + 2 * P]
        ada_rows = arena[0:2, A_ADA:A_ADA + 6 * D]
        crow = arena[0:16, A_VEC + 2 * P:A_VEC + 3 * P]

        semaphores = {name: sem(name) for name in SIGNALS}
        sig = [Signals(*[Signal(semaphores[name], total * l) for name, total in SIGNALS.items()])
               for l in range(DEPTH)]
        again = sig[DEPTH - 1]._replace(**{name: Signal(semaphores[name], SIGNALS[name] + 2 * NH) for name in REUSED})
        moe = sig[DEPTH - 1]._replace(**{name: Signal(semaphores[name], SIGNALS[name] + n) for name, n in
                                         (("m_y", MW), ("m_hTs", MW), ("m_st", MW), ("m_sel", KD), ("m_sT", KD))})
        consts_in, c_in, h_in, out_in = sem("consts_in"), sem("c_in"), sem("h_in"), sem("out_in")
        c_T, c_silu, vec_in, prm_in = sem("c_T"), sem("c_silu"), [sem("vec0"), sem("vec1")], [sem("prm0"), sem("prm1")]
        slot_full = [sem(f"slot_full{i}") for i in range(RING)]
        slot_free = sem("slot_free")
        branch_in = [sem(f"branch_in{i}") for i in range(4)]
        dve_chain, act_chain, pool_chain = sem("dve_chain"), sem("act_chain"), sem("pool_chain")

        def linker(eng, s):
            n = [0]

            def link(ins):
                n[0] += 1
                ins.then_inc(s, 1)
                eng.wait_ge(s, n[0])
            return link

        def cols(w, c0, cn=CW):
            return w[:, c0:c0 + cn].rearrange("(k p) n -> p k n", p=P), (KD, cn)

        def rows(w, r0, rn):
            return w[r0:r0 + rn * P, :].rearrange("(k p) n -> p k n", p=P), (rn, D)

        WIN = ([0, 256, 512], [OFF_Z], [OFF_AB], [OFF_F], [OFF_GQA, OFF_GQA + 256],
               [OFF_RET + 256 * i for i in range(4)])

        def layer_slots(l):
            out_ = [cols(d["ada_w"][l], CW * i) for i in range(NADA)]
            for part in WIN:
                for c0 in part:
                    out_.append(cols(d["w_in"][l], c0, 16 if c0 == OFF_AB else CW))
            for i in (3, 2, 1, 0):
                out_ += [cols(d["w_gate"][l][i], CW * j) for j in range(4)]
            out_ += [cols(d["w_out"][l], CW * j) for j in range(4)]
            return out_

        def ffn_slots(w1, w3, w2):
            out_ = []
            for c in range(NF // 2):
                out_ += [cols(w1, CW * c), cols(w3, CW * c)]
            return out_ + [rows(w2, 2 * P * c, 2) for c in range(NF // 2)]

        slots = layer_slots(0) + ffn_slots(d["ffn_w1"][0], d["ffn_w3"][0], d["ffn_w2"][0]) + layer_slots(1)
        FFN0 = len(layer_slots(0))
        GATES = [NADA + sum(len(part) for part in WIN) + l * (FFN0 + 3 * NF // 2) for l in range(DEPTH)]
        MOE0 = len(slots)
        PER = 3 * NF // 2

        def half_slot(n, q):
            return ring[:, (n + q // 2) % RING, D * (q % 2):D * (q % 2 + 1)]

        def slot_view(n, shape):
            return ring[:, n % RING, 0:shape[0] * shape[1]].rearrange("p (k n) -> p k n", k=shape[0])

        class Weights:

            def __init__(self, pe):
                self.pe, self.n = pe, 0

            def take(self):
                n, self.n = self.n, self.n + 1
                self.pe.wait_ge(slot_full[n % RING], 16 * (n // RING + 1))
                return slot_view(n, slots[n][1])

        block = ctx.enter_context(nc.Block())

        @block.sync
        def _(sp):
            for n, (src, shape) in enumerate(slots):
                if n >= RING:
                    sp.wait_ge(slot_free, n - RING + 1)
                sp.dma_start(slot_view(n, shape), src).then_inc(slot_full[n % RING], 16)
            w1, w3, w2 = d["moe_w1"], d["moe_w3"], d["moe_w2"]
            with sp.Fori(0, NE // 2) as i:
                j = 0
                for e in range(2):
                    order = [(w, c) for c in range(NF // 2) for w in (w1, w3)] + [(w2, c) for c in range(NF // 2)]
                    for w, c in order:
                        n = MOE0 + j
                        sp.wait_ge(slot_free, 2 * PER * i + (n - RING + 1))
                        if w is w2:
                            src = w[bass.ds(2 * i + e, 1), 2 * P * c:2 * P * (c + 1), :].rearrange(
                                "e (k p) n -> p (e k) n", p=P)
                            dst = slot_view(n, (2, D))
                        else:
                            src = w[bass.ds(2 * i + e, 1), :, CW * c:CW * (c + 1)].rearrange(
                                "e (k p) n -> p (e k) n", p=P)
                            dst = slot_view(n, (KD, CW))
                        sp.dma_start(dst, src).then_inc(slot_full[n % RING], 16)
                        j += 1
            for t in range(2):
                sp.wait_ge(*sig[1].po_h2(t + 1))
                sp.dma_start(out[P * t:P * (t + 1), :], h[:, 2 + t, :]).then_inc(out_in, 16)
            sp.wait_ge(out_in, 32)

        @block.tensor
        def _(pe):
            W = Weights(pe)

            def transpose(dst, src):
                return pe.transpose(dst, src, ident)

            def prenorm_T(g_xs, g_tp, g_ok, tiles):
                pe.wait_ge(*g_xs(len(tiles)))
                for k in range(KD):
                    if k >= 4:
                        pe.wait_ge(*g_ok(k - 3))
                    for t in tiles:
                        last = transpose(bank[k % 4][:, P * t:P * (t + 1)], xs[:, t, P * k:P * (k + 1)])
                    last.then_inc(g_tp.up, 1)

            def gate_rows(g_d, g_m, g_ok, streams):
                for n in range(2 * len(streams)):
                    pe.wait_ge(*g_d(n + 1))
                    pe.matmul(bank[4 + n][:, :], ones, area(A_TR + 5120 + 512 * (n % 2), 512),
                              start=True, stop=True).then_inc(g_m.up, 1)

            def dense_experts_pe(s):
                with pe.Fori(0, NE // 2) as i:
                    for e in range(2):
                        at = PER * e
                        for c in range(NF // 2):
                            views = []
                            for q in range(2):
                                n = MOE0 + at
                                pe.wait_ge(slot_full[n % RING], 16 * (2 * PER // RING) * i + 16 * (n // RING + 1))
                                views.append(slot_view(n, (KD, CW)))
                                at += 1
                            for m in range(2):
                                f = 2 * c + m
                                pe.wait_ge(*s.f_hid(2 * NF * i + (NF * e + f - 1) + 2))
                                for q in range(2):
                                    for k in range(KD):
                                        mm = pe.matmul(bank[2 * q + f % 2][:, 0:SEQ], views[q][:, k, P * m:P * (m + 1)],
                                                       uT[:, k, SEQ:TOK], start=(k == 0), stop=(k == KD - 1))
                                mm.then_inc(s.f_mm.up, 1)
                            pe.wait_ge(*s.f_mm(2 * NF * i + (NF * e + 2 * c + 2)))
                            pe.sem_inc(slot_free, 2)
                        pe.wait_ge(*s.f_hid(2 * NF * i + (NF * (e + 1) + 2)))
                        pe.wait_ge(*s.f_acc(2 * i + (e + 1)))
                        for c in range(NF // 2):
                            n = MOE0 + at
                            pe.wait_ge(slot_full[n % RING], 16 * (2 * PER // RING) * i + 16 * (n // RING + 1))
                            w = slot_view(n, (2, D))
                            at += 1
                            for m in range(2):
                                f = 2 * c + m
                                for t in range(2):
                                    for hf in range(2):
                                        mm = pe.matmul(bank[4 + 2 * t + hf][:, :],
                                                       hid[:, f, P * t:P * (t + 1)],
                                                       w[:, m, 512 * hf:512 * (hf + 1)],
                                                       start=(f == 0), stop=(f == NF - 1))
                            mm.then_inc(slot_free, 1)
                        pe.wait_ge(slot_free, 2 * PER * i + (MOE0 + at))
                        pe.sem_inc(s.f_out.up, 1)

            def sparse_experts_pe(s):
                a, used = moe, s.gq_s
                pe.sem_inc(used.semaphore, 4)
                for k in range(KD):
                    for t in range(2):
                        mm = transpose(bank[2 + 4 * t + k // 4][:, P * (k % 4):P * (k % 4 + 1)],
                                       uT[:, k, SEQ + P * t:SEQ + P * (t + 1)])
                mm.then_inc(a.m_st.up, 1)

                def gather():
                    for k in range(KD):
                        for q, (t, part) in enumerate(((0, 0), (0, 1), (1, 0), (1, 1))):
                            mm = pe.matmul(bank[2 + k // 4][:, P * (k % 4):P * (k % 4 + 1)],
                                           vns[part][:, t, P * k:P * (k + 1)], sel_r[:, t, :],
                                           start=(q == 0), stop=(q == 3))
                    mm.then_inc(s.gq_max.up, 1)

                def scatter():
                    for t in range(2):
                        for hf in range(2):
                            mm = pe.matmul(bank[(6, 4)[t] + hf][:, :], selT[:, t, :], ysb[:, 512 * hf:512 * (hf + 1)],
                                           start=True, stop=True)
                    mm.then_inc(a.f_out.up, 1)

                def sel_transposes():
                    for t in range(2):
                        mm = transpose(bank[1][:, P * t:P * (t + 1)], sel[:, t, :])
                    mm.then_inc(a.m_st.up, 1)

                pe.wait_ge(*a.m_sel(1))
                gather()
                scatter()
                sel_transposes()
                with pe.Fori(0, NE // 2) as i:
                    for e in range(2):
                        def past(per, n):
                            return 2 * per * i + (per * e + n)

                        pe.wait_ge(*s.gq_e(past(1, 1)))

                        def hidden_transposes(c):
                            pe.wait_ge(*a.f_hid(past(NF // 2, c + 3)))
                            if c >= 2:
                                pe.wait_ge(*a.m_hTs(past(NF // 2, c - 1)))
                            for m in range(2):
                                mm = transpose(bank[2 + c % 2][:, P * m:P * (m + 1)], hn[:, c % 2, P * m:P * (m + 1)])
                            mm.then_inc(a.f_sil.up, 1)

                        for c in range(NF // 2):
                            pe.wait_ge(*a.f_hid(past(NF // 2, c + 1)))
                            if c == 1:
                                pe.wait_ge(*a.m_sT(past(1, 1)))
                            for r in range(4):
                                q = 4 * c + r
                                pe.wait_ge(*s.gq_pt(past(3 * NF, q + 1)))
                                whi, wlo = (wsp[x][:, q % 4, :].rearrange("p (k n) -> p k n", k=4) for x in range(2))
                                for k in range(4):
                                    kk = 4 * (r % 2) + k
                                    o = bank[c % 2][:, CW * (r // 2):CW * (r // 2 + 1)]
                                    pe.matmul(o, xTs[0][:, kk, :], whi[:, k, :], start=(kk == 0), stop=False)
                                    pe.matmul(o, xTs[0][:, kk, :], wlo[:, k, :], start=False, stop=False)
                                    mm = pe.matmul(o, xTs[1][:, kk, :], whi[:, k, :], start=False, stop=(kk == KD - 1))
                                mm.then_inc(used.semaphore, 1)
                                if r == 1 and c:
                                    hidden_transposes(c - 1)
                        for f in range(NF):
                            q = 2 * NF + f
                            pe.wait_ge(*s.gq_pt(past(3 * NF, q + 1)))
                            if f % 2 == 0:
                                pe.wait_ge(*a.m_hTs(past(NF // 2, f // 2 + 1)))
                            if f == 0:
                                pe.wait_ge(*a.f_acc(past(1, 2)))
                            for x, w in ((0, 0), (0, 1), (1, 0)):
                                for hf in range(2):
                                    mm = pe.matmul(bank[4 + hf][:, :], hTs[x][:, f, :],
                                                   wsp[w][:, q % 4, 512 * hf:512 * (hf + 1)],
                                                   start=(f == 0 and x == w == 0), stop=(f == NF - 1 and x == 1))
                            mm.then_inc(used.semaphore, 1)
                            if f == 1:
                                hidden_transposes(NF // 2 - 1)
                        pe.wait_ge(*a.m_sel(past(1, 2)))
                        gather()
                        pe.wait_ge(*a.m_y(past(1, 2)))
                        scatter()
                        sel_transposes()

            pe.wait_ge(c_in, 48)
            pe.transpose(bank[0][:, 0:16], crow[:, :], consts[0:16, C_ID:C_ID + 16]).then_inc(c_T, 1)

            for l in range(DEPTH):
                s = sig[l]
                ctx_out = l < DEPTH - 1
                tiles = list(range(NT)) if ctx_out else [2, 3]
                lo = 0 if ctx_out else SEQ
                g_whi, g_wlo, g_xhi, g_xlo, g_used = s.m_y, s.m_hTs, s.m_sel, s.m_sT, s.m_st

                if l == 0:
                    pe.wait_ge(c_silu, 1)
                for j in range(NADA + 1):
                    if j == 4:
                        pe.wait_ge(vec_in[l], 64)
                        pe.wait_ge(consts_in, 32)
                        pe.transpose(bank[0][:, 0:80], vecA[:, :], consts[0:80, C_ID:C_ID + 80])
                        pe.transpose(bank[0][:, 80:142], vecB[:, :], consts[0:62, C_ID:C_ID + 62]).then_inc(s.vec_T.up, 1)
                    if j < NADA:
                        w = W.take()
                        if j >= 2:
                            pe.wait_ge(*s.ada_row(j - 1))
                        for k in range(KD):
                            mm = pe.matmul(bank[2 + j % 2][0:2, 0:CW], silu_c[:, :, k], w[:, k, :],
                                           start=(k == 0), stop=(k == KD - 1))
                        mm.then_inc(s.ada_mm.up, 1)
                    if j:
                        pe.wait_ge(*s.ada_row(j))
                        for n in (2 * j - 2, 2 * j - 1):
                            mm = pe.transpose(bank[1][:, 2 * n:2 * n + 2], ada_rows[:, P * n:P * (n + 1)],
                                              consts[0:2, C_ID:C_ID + 2])
                    if j < NADA:
                        pe.wait_ge(*s.ada_mm(j + 1))
                        pe.sem_inc(slot_free, 1)
                mm.then_inc(s.ada_mm.up, 1)
                pe.wait_ge(*s.vec_ok(1))
                pe.wait_ge(*s.mod_ok(1))
                prenorm_T(s.xs1, s.tp1, s.u_ok, range(NT))

                pe.wait_ge(*s.u_ok(KD))
                unit = 0
                for part in WIN[:-1]:
                    for c0 in part:
                        w = W.take()
                        if c0 < OFF_Z or c0 == OFF_F:
                            for n in range(2):
                                if unit >= 4:
                                    pe.wait_ge(*s.win_ok(unit - 3))
                                for k in range(KD):
                                    mm = pe.matmul(bank[unit % 4][:, :], w[:, k, P * n:P * (n + 1)], uT[:, k, :],
                                                   start=(k == 0), stop=(k == KD - 1))
                                mm.then_inc(s.win_mm.up, 1)
                                unit += 1
                        elif c0 == OFF_AB:
                            pe.wait_ge(*s.win_ok(unit - 3))
                            for t in range(NT):
                                for k in range(KD):
                                    mm = pe.matmul(bank[unit % 4][:, 16 * t:16 * t + 16],
                                                   uT[:, k, P * t:P * (t + 1)], w[:, k, :],
                                                   start=(k == 0), stop=(k == KD - 1))
                            mm.then_inc(s.win_mm.up, 1)
                            unit += 1
                        else:
                            for t in range(NT):
                                if t % 2 == 0:
                                    pe.wait_ge(*s.win_ok(unit - 3))
                                for k in range(KD):
                                    mm = pe.matmul(bank[unit % 4][:, CW * (t % 2):CW * (t % 2 + 1)],
                                                   uT[:, k, P * t:P * (t + 1)], w[:, k, :],
                                                   start=(k == 0), stop=(k == KD - 1))
                                if t % 2:
                                    mm.then_inc(s.win_mm.up, 1)
                                    unit += 1
                        pe.wait_ge(*s.win_mm(unit))
                        pe.sem_inc(slot_free, 1)

                def retention_columns(g):
                    t, unit = g % NT, UNITS + g // 2
                    if t == 0:
                        if g:
                            retention_release(g)
                        rw[0] = W.take()
                    if t % 2 == 0 and unit >= UNITS + 2:
                        pe.wait_ge(*s.win_ok(unit - 1))
                    for k in range(KD):
                        mm = pe.matmul(bank[6 + unit % 2][:, CW * (t % 2):CW * (t % 2 + 1)],
                                       uT[:, k, P * t:P * (t + 1)], rw[0][:, k, :], start=(k == 0), stop=(k == KD - 1))
                    if t % 2:
                        mm.then_inc(s.win_mm.up, 1)

                def retention_release(g):
                    pe.wait_ge(*s.win_mm(UNITS + g // 2))
                    pe.sem_inc(slot_free, 1)

                rw, steps = [None], 4 * NT - AHEAD[l]
                ahead = AHEAD[l]

                pe.wait_ge(*s.win_ok(UNITS))
                for t in range(NT):
                    for c in range(2):
                        mm = pe.matmul(bank[t][:, 256 * c:256 * (c + 1)], fT[:, c, P * t:P * (t + 1)],
                                       consts[:, C_FD:C_FD + 256], start=True, stop=True)
                    mm.then_inc(s.fn_mm1.up, 1)
                pe.wait_ge(*s.fn_c(NT))
                xc = area(A_TR, NT, 2, 2, P)
                ftab = consts[:, C_FT:C_FT + 1024].rearrange("p (t c n) -> p t c n", t=2, c=2)
                for c in range(2):
                    for st in range(2):
                        for t in range(2):
                            for cs in range(2):
                                mm = pe.matmul(bank[4 + c][:, SEQ * st:SEQ * (st + 1)], xc[:, 2 * st + t, c, cs, :],
                                               ftab[:, t, cs, :], start=(t == 0 and cs == 0), stop=(t == 1 and cs == 1))
                    mm.then_inc(s.fn_mm2.up, 1)

                for g in range(ahead):
                    retention_columns(g)
                pe.wait_ge(*s.gq_n(1))
                gn = area(A_TR, NT, 8, HD)
                gT = area(A_TR + 2048, 4, TOK)
                for t in range(NT):
                    for c in range(4):
                        mm = transpose(bank[t][:, P * c:P * (c + 1)],
                                       gn[:, t, 2 * c:2 * c + 2, :].rearrange("p a b -> p (a b)"))
                    mm.then_inc(s.gq_tp.up, 1)
                pe.wait_ge(*s.gq_T(NT))
                Pb, PTb = area(A_TR + 4608, 2, 512), area(A_TR + 5632, 2, 4, P)
                work = [(t, hh) for t in tiles for hh in range(NH)]

                def gq_scores(n):
                    t, hh = work[n]
                    keys = SEQ if t < 2 else TOK
                    if n >= 2:
                        pe.wait_ge(*s.gq_e(n - 1))
                    q = gT[HD * (hh % 2):HD * (hh % 2 + 1), hh // 2, P * t:P * (t + 1)]
                    k = gT[HD * (hh % 2):HD * (hh % 2 + 1), 2 + hh // 2, 0:keys]
                    pe.matmul(bank[n % 2][:, 0:keys], q, k, start=True, stop=True).then_inc(s.gq_s.up, 1)

                def gq_values(n):
                    t, hh = work[n]
                    nk = 2 if t < 2 else 4
                    pe.wait_ge(*s.gq_e(n + 1))
                    if n >= 2:
                        pe.wait_ge(*s.gq_ptc(n - 1))
                    for j in range(nk):
                        mm = transpose(bank[2 + n % 2][:, P * j:P * (j + 1)], Pb[:, n % 2, P * j:P * (j + 1)])
                    mm.then_inc(s.gq_pt.up, 1)

                def gq_out(n):
                    t, hh = work[n]
                    nk = 2 if t < 2 else 4
                    pe.wait_ge(*s.gq_ptc(n + 1))
                    if n >= 2:
                        pe.wait_ge(*s.gq_on(n - 1))
                    for j in range(nk):
                        mm = pe.matmul(bank[4 + n % 2][:, 0:HD], PTb[:, n % 2, j, :],
                                       gqn[:, j, 384 + HD * (hh // 2):384 + HD * (hh // 2 + 1)],
                                       start=(j == 0), stop=(j == nk - 1))
                    mm.then_inc(s.gq_o.up, 1)

                for n in range(len(work) + 2):
                    if n < len(work):
                        gq_scores(n)
                    if 1 <= n <= len(work):
                        gq_values(n - 1)
                    if n >= 2:
                        gq_out(n - 2)
                    if n < steps:
                        retention_columns(ahead + n)
                retention_release(4 * NT)
                pe.wait_ge(*s.win_ok(UNITS + 8))

                def y_transposes(src, g_ready, g_tp):
                    pe.wait_ge(*g_ready(1))
                    for c in range(2):
                        for t in tiles:
                            mm = transpose(bank[6 + c][:, P * t:P * (t + 1)], src[:, t, P * c:P * (c + 1)])
                        mm.then_inc(g_tp.up, 1)

                pe.wait_ge(*s.gq_on(len(work)))
                y_transposes(area(A_TR, NT, BW), s.gq_on, s.gq_yt)

                pe.wait_ge(*s.rt_n(1))
                pe.wait_ge(*s.gq_y(2))
                rT = area(A_TR, 4, TOK)
                for t in range(NT):
                    for c in range(4):
                        mm = transpose(bank[t][:, P * c:P * (c + 1)], rtn[:, t, P * c:P * (c + 1)])
                    mm.then_inc(s.rt_tp.up, 1)
                pe.wait_ge(*s.rt_T(NT))
                PR = area(A_TR + 5120, 2, 4, SEQ)
                runits = [(hh, st) for hh in range(NH) for st in ((0, 1) if ctx_out else (1,))]
                def rt_scores(n):
                    hh, st = runits[n]
                    if n >= 2:
                        pe.wait_ge(*s.rt_p(n - 1))
                    part = slice(HD * (hh % 2), HD * (hh % 2 + 1))
                    for j in range(2 + 2 * st):
                        mm = pe.matmul(bank[4 + 2 * (n % 2) + j // 2][:, SEQ * (j % 2):SEQ * (j % 2 + 1)],
                                       rT[part, 2 + hh // 2, P * j:P * (j + 1)],
                                       rT[part, hh // 2, SEQ * st:SEQ * (st + 1)], start=True, stop=True)
                    mm.then_inc(s.rt_s.up, 1)

                rt_scores(0)
                for n, (hh, st) in enumerate(runits):
                    nk = 2 + 2 * st
                    if n + 1 < len(runits):
                        rt_scores(n + 1)
                    pe.wait_ge(*s.rt_p(n + 1))
                    for t in range(2):
                        for j in range(nk):
                            mm = pe.matmul(bank[2 * st + t][:, HD * hh:HD * (hh + 1)],
                                           PR[:, n % 2, j, P * t:P * (t + 1)],
                                           rtn[:, j, 512 + HD * hh:512 + HD * (hh + 1)],
                                           start=(j == 0), stop=(j == nk - 1))
                    mm.then_inc(s.rt_o.up, 1)
                y_transposes(area(A_TR, NT, BW), s.rt_on, s.rt_yt)

                pe.wait_ge(*s.silu_ok(6))
                for t in range(NT):
                    for c in range(6):
                        mm = transpose(bank[2 * (t % 2) + c // 4][:, P * (c % 4):P * (c % 4 + 1)],
                                       conv_out[:, c, P * t:P * (t + 1)])
                        if c in (3, 5):
                            mm.then_inc(s.cT_mm.up, 1)
                            if c == 5 and t in (1, 2):
                                pe.wait_ge(*s.cT_ok(2 * t))
                pe.wait_ge(*s.l2_ok(1))
                pe.wait_ge(*s.rt_y(2))
                for t in range(NT):
                    for c in range(4):
                        mm = transpose(bank[4 + t][:, P * c:P * (c + 1)], qkv[:, t, P * c:P * (c + 1)])
                    mm.then_inc(s.qk_mm.up, 1)
                pe.wait_ge(*s.ab_ok(1))
                pe.wait_ge(*s.cT_ok(2 * NT))
                for dr in range(2):
                    pe.matmul(bank[0][:, 32 * dr:32 * dr + 32], tri[dr], gs[:, 1, :, :].rearrange("p a b -> p (a b)"),
                              start=True, stop=True)
                pe.matmul(bank[0][:, 64:96], ones, gs[:, 1, :, :].rearrange("p a b -> p (a b)"),
                          start=True, stop=True).then_inc(s.gl_mm.up, 1)
                pe.wait_ge(*s.qk_ok(NT))

                for dr in range(2):
                    pe.wait_ge(*s.gl_ok(1 + dr))
                    if dr:
                        pe.wait_ge(*s.st_oa(NT))
                    for t in range(NT):
                        n = NT * dr + t
                        if t >= 2:
                            pe.wait_ge(*s.gd_abs(n - 1))
                            pe.wait_ge(*s.gd_M(n - 1))
                            pe.wait_ge(*s.gd_A(n - 1))
                        tok = slice(P * t, P * (t + 1))
                        for hh in range(NH):
                            c = slice(P * hh, P * (hh + 1))
                            pe.matmul(bank[t % 2][:, c], gs[:, 1, t, 4 * dr + hh:4 * dr + hh + 1].to_broadcast([P, P]),
                                      tri[dr], start=True, stop=True)
                            pe.matmul(bank[2 + t % 2][:, c], kz[:, hh, tok], kz[:, hh, tok], start=True, stop=True)
                            mm = pe.matmul(bank[4 + t % 2][:, c], kz[:, hh, tok], qT[:, hh // 2, tok],
                                           start=True, stop=True)
                        mm.then_inc(s.gd_mm.up, 1)
                        for u in ([], [n - 1], [n - 1], [n - 1, n])[t]:
                            pe.wait_ge(*s.gd_M(u + 1))
                            if u % NT >= 2:
                                pe.wait_ge(*s.gd_MTs(u - 1))
                            for hh in range(NH):
                                mm = transpose(bank[6 + u % 2][:, P * hh:P * (hh + 1)], T1[:, u % NT, hh, :])
                            mm.then_inc(s.gd_MT.up, 1)
                    pe.wait_ge(*s.gd_X(NT * (dr + 1)))
                    pe.wait_ge(*s.gd_XT(NT * (dr + 1)))
                    pe.wait_ge(*s.gd_A(NT * (dr + 1)))
                    for v in range(LEVELS):
                        base = (LEVELS * dr + v) * NT
                        for t in range(NT):
                            if v:
                                pe.wait_ge(*s.lv_X(base - NT + t + 1))
                            for hh in range(NH):
                                mm = pe.matmul(bank[t][:, P * hh:P * (hh + 1)], MT[:, t, hh, :], X[:, t, hh, :],
                                               start=True, stop=True)
                            mm.then_inc(s.lv_mm1.up, 1)
                        for t in range(NT):
                            pe.wait_ge(*s.lv_T1(base + t + 1))
                            for hh in range(NH):
                                if v < LEVELS - 1:
                                    pe.matmul(bank[4 + t][:, P * hh:P * (hh + 1)], XT[:, t, hh, :], T1[:, t, hh, :],
                                              start=True, stop=True)
                                mm = pe.matmul(bank[t][:, P * hh:P * (hh + 1)], T1[:, t, hh, :], XT[:, t, hh, :],
                                               start=True, stop=True)
                            mm.then_inc(s.lv_mm2.up, 1)
                    pe.wait_ge(*s.gd_R(dr + 1))
                    for t in range(NT):
                        pe.wait_ge(*s.lv_X((LEVELS * dr + LEVELS - 1) * NT + t + 1))
                        for hh in range(NH):
                            mm = pe.matmul(bank[4 + t][:, P * hh:P * (hh + 1)], XT[:, t, hh, :], R[:, t, hh, :],
                                           start=True, stop=True)
                        mm.then_inc(s.uw_mm.up, 1)
                    pe.wait_ge(*s.uw_ok(NT * (dr + 1)))
                    pe.wait_ge(*s.gd_q(dr + 1))
                    for t in range(NT):
                        for c in range(2):
                            transpose(bank[t][:, P * c:P * (c + 1)], wn[:, t, P * c:P * (c + 1)])
                            mm = transpose(bank[t][:, 256 + P * c:256 + P * (c + 1)], qtil[:, t, P * c:P * (c + 1)])
                        mm.then_inc(s.wq_mm.up, 1)
                    pe.wait_ge(*s.wq_ok(NT * (dr + 1)))
                    for i, t in enumerate((0, 1, 2, 3) if dr == 0 else (1, 0, 3, 2)):
                        n = NT * dr + i
                        tok = slice(P * t, P * (t + 1))
                        if i:
                            pe.wait_ge(*s.st_S(n - dr))
                            for c in range(2):
                                mm = pe.matmul(bank[4][:, P * c:P * (c + 1)], wT[:, c, tok], S[:, i % 2, c, :],
                                               start=True, stop=True)
                            mm.then_inc(s.st_mm.up, 1)
                        pe.wait_ge(*s.st_v(n + 1))
                        if i < NT - 1:
                            for c in range(2):
                                mm = pe.matmul(bank[5][:, P * c:P * (c + 1)], kdec[:, t, P * c:P * (c + 1)],
                                               vnew[:, t, P * c:P * (c + 1)], start=True, stop=True)
                            mm.then_inc(s.st_s.up, 1)
                        if n >= 2:
                            pe.wait_ge(*s.st_oa(n - 1))
                        for hh in range(NH):
                            if i and hh % 2 == 0:
                                pe.matmul(bank[6 + n % 2][:, HD * hh:HD * (hh + 2)], qtilT[:, hh // 2, tok],
                                          S[:, i % 2, hh // 2, :], start=True, stop=True,
                                          skip_group_check=True)
                            mm = pe.matmul(bank[6 + n % 2][:, HD * hh:HD * (hh + 1)], AT[:, t, hh, :],
                                           vnew[:, t, HD * hh:HD * (hh + 1)], start=(i == 0), stop=True,
                                           skip_group_check=bool(i))
                        mm.then_inc(s.st_o.up, 1)
                pe.wait_ge(*s.gdy_n(1))
                for c in range(2):
                    for t in tiles:
                        mm = transpose(bank[c][:, P * t:P * (t + 1)], un[:, t, P * c:P * (c + 1)])
                    mm.then_inc(s.gdy_tp.up, 1)

                pe.wait_ge(*s.gdy_ok(2))
                for q in range(MW):
                    g, half = q // 2, q % 2
                    br, b = (3, 2, 1, 0)[g // 4], 4 * (g % 2)
                    pe.wait_ge(*g_wlo(q + 1))
                    if g == 0:
                        pe.wait_ge(*g_xlo(4 * half + 4))
                    if g >= 2 and half == 0:
                        pe.wait_ge(*s.mg_add(2 * g - 2))
                    for k in range(4 * half, 4 * half + 4):
                        for m in range(2):
                            n = CW * (k % 4) + P * m
                            for i, (w, x) in enumerate(((0, xg_hi), (0, x_lo), (1, xg_hi))):
                                mm = pe.matmul(bank[b + m][:, lo:TOK], gsp[w][:, q % 3, n:n + P], x[:, k, lo:TOK],
                                               start=(k == 0 and i == 0), stop=(k == KD - 1 and i == 2))
                    mm.then_inc(g_used.up, 1)
                    if half:
                        if g % 4 == 0:
                            pe.wait_ge(branch_in[br], 16 * (l + 1))
                        for m in range(2):
                            c = 2 * (g % 4) + m
                            for k in range(2):
                                mm = pe.matmul(bank[b + 2 + m][:, lo:TOK], wbr[:, (3 - br) % 2, k, P * c:P * (c + 1)],
                                               yT[:, br, k, lo:TOK], start=(k == 0), stop=(k == 1))
                            mm.then_inc(s.mg_mm.up, 1)
                W.n += MW // 2

                pe.wait_ge(*s.mg_add(MW))
                gate_rows(s.gb_d1, s.gb_m1, s.gb_ok1, [0, 1] if ctx_out else [1])
                pe.wait_ge(*s.gb_ok1(4 if ctx_out else 2))
                for j in range(4):
                    w = W.take()
                    for t in tiles:
                        for k in range(KD):
                            mm = pe.matmul(bank[2 * t + j // 2][:, CW * (j % 2):CW * (j % 2 + 1)],
                                           accT[:, k, P * t:P * (t + 1)], w[:, k, :], start=(k == 0), stop=(k == KD - 1))
                    mm.then_inc(slot_free, 1)
                pe.wait_ge(slot_free, W.n)
                pe.sem_inc(s.po_mm.up, 1)
                pe.wait_ge(*s.po_h1(len(tiles)))
                gate_rows(s.gb_d2, s.gb_m2, s.gb_ok2, [0, 1] if ctx_out else [1])

                pe.wait_ge(*s.gb_ok2(2 * (2 if ctx_out else 1)))
                prenorm_T(s.xs2, s.tp2, s.v_ok, tiles)
                pe.wait_ge(*s.v_ok(KD))

                if ctx_out:
                    for q in range(2 * NF):
                        c, j, half = q // 4, q // 2 % 2, q % 2
                        pe.wait_ge(*g_wlo(MW + q + 1))
                        if c == 0:
                            pe.wait_ge(*g_xlo(KD + 4 * half + 4))
                        if c >= 2 and q % 4 == 0:
                            pe.wait_ge(*s.f_hid(2 * c - 2))
                        for k in range(4 * half, 4 * half + 4):
                            for m in range(2):
                                n = CW * (k % 4) + P * m
                                for i, (w, x) in enumerate(((0, x_high(k)), (0, x_lo[:, k, :]), (1, x_high(k)))):
                                    mm = pe.matmul(bank[4 * (c % 2) + 2 * j + m][:, :], dsp[w][:, q % 3, n:n + P], x,
                                                   start=(k == 0 and i == 0), stop=(k == KD - 1 and i == 2))
                        mm.then_inc(g_used.up, 1)
                    pe.wait_ge(*s.f_hid(NF))
                    for f in range(NF):
                        q = 2 * NF + f
                        pe.wait_ge(*g_wlo(MW + q + 1))
                        pe.wait_ge(*g_xlo(2 * KD + f + 1))
                        for t in range(NT):
                            for x, w in ((0, 0), (0, 1), (1, 0)):
                                for hf in range(2):
                                    mm = pe.matmul(bank[2 * t + hf][:, :], hsp[x][:, f % 3, P * t:P * (t + 1)],
                                                   dsp[w][:, q % 3, 512 * hf:512 * (hf + 1)],
                                                   start=(f == 0 and x == w == 0), stop=(f == NF - 1 and x == 1))
                        mm.then_inc(g_used.up, 1)
                    W.n += 3 * NF // 2
                    pe.wait_ge(*g_used(MW + 3 * NF))
                    pe.sem_inc(s.f_out.up, 1)
                    pe.wait_ge(*s.po_h2(2))
                else:
                    for t in range(2):
                        for k in range(KD):
                            mm = pe.matmul(bank[0][:, NE * t:NE * (t + 1)], uT[:, k, SEQ + P * t:SEQ + P * (t + 1)],
                                           rt8[:, k, :], start=(k == 0), stop=(k == KD - 1))
                    mm.then_inc(s.rlog.up, 1)
                    pe.wait_ge(*s.rcomb(1))
                    pe.wait_ge(*s.rcomb(3))
                    msk = route[:, 3]
                    pe.matmul(bank[1][:, 0:NE], tri[0], msk[:, 0, :], start=True, stop=True)
                    for m, (a, b) in enumerate(((ones, tri[0]), (ones, ones))):
                        c = slice(NE * (m + 1), NE * (m + 2))
                        pe.matmul(bank[1][:, c], a, msk[:, 0, :], start=True, stop=False)
                        mm = pe.matmul(bank[1][:, c], b, msk[:, 1, :], start=False, stop=True)
                    mm.then_inc(s.rlog.up, 1)
                    pe.wait_ge(*s.rcomb(4))
                    dense = pe.value_load(crowded[0:1, 0:1], min_val=0, max_val=1)
                    with pe.If(dense):
                        dense_experts_pe(s)
                    with pe.Else():
                        sparse_experts_pe(again)

        @block.scalar
        def _(act):
            link = linker(act, act_chain)
            act.dma_start(crow[0:8, :], d["c"].rearrange("a (k p) -> (a k) p", p=P)).then_inc(c_in, 16)
            act.dma_start(crow[8:16, :], d["c_ctx"].rearrange("(k p) -> k p", p=P)).then_inc(c_in, 16)
            act.dma_start(ident, d["consts"][:, C_ID:C_ID + P]).then_inc(c_in, 16)
            act.dma_start(h[:, 0:2, :], d["ctx"].rearrange("b (t p) n -> p (b t) n", p=P)).then_inc(h_in, 16)
            act.dma_start(h[:, 2:4, :], d["x"].rearrange("b (t p) n -> p (b t) n", p=P)).then_inc(h_in, 16)
            act.wait_ge(c_T, 1)
            act.activation(silu_c[:, :, :], bank[0][:, 0:16].rearrange("p (a k) -> p a k", a=2), ACT.Silu).then_inc(c_silu, 1)
            act.dma_start(rt8[:, :, :], d["moe_router"][0].rearrange("(k p) e -> p k e", p=P)).then_inc(h_in, 16)
            act.dma_start(iota[:, :], d["iota"]).then_inc(h_in, 16)

            def load_vectors(l):
                s = sig[l]
                act.dma_start(vecA[0:48, :], d["ada_b"][l].rearrange("(k p) -> k p", p=P)).then_inc(vec_in[l], 16)
                act.dma_start(vecA[48:80, :], d["norm_g"][l].rearrange("a (k p) -> (a k) p", p=P)).then_inc(vec_in[l], 16)
                act.dma_start(vecB[0:32, :], d["b_gate"][l].rearrange("a (k p) -> (a k) p", p=P)).then_inc(vec_in[l], 16)
                act.dma_start(vecB[32:62, :], d["conv_w"][l].rearrange("a (k p) -> (a k) p", p=P)).then_inc(vec_in[l], 16)
                for dst, src in ((retg, d["ret_norm_g"][l]), (gdng, d["gdn_norm_g"][l]),
                                 (qkg, d["qk_norm_g"][l].rearrange("a b -> (a b)")),
                                 (alog, d["gdn_a_log"][l].rearrange("a b -> (a b)")),
                                 (dtb, d["gdn_dt_bias"][l].rearrange("a b -> (a b)")),
                                 (rraw, d["ret_log_decay_raw"][l].rearrange("a b -> (a b)"))):
                    act.dma_start(dst, src.partition_broadcast(P)).then_inc(prm_in[l], 16)

            def dense_experts_act(s, sil):
                with act.Fori(0, NE) as e:
                    for f in range(NF):
                        act.wait_ge(*s.f_mm(NF * e + (f + 1)))
                        act.wait_ge(*s.f_hid(NF * e + (f + 1)))
                        act.activation(sil[:, f % 2, 0:SEQ], bank[f % 2][:, 0:SEQ], ACT.Silu).then_inc(s.f_sil.up, 1)
                act.wait_ge(*s.f_acc(NE + 1))

            def sparse_experts_act(s):
                a, used = moe, s.gq_s
                act.wait_ge(*a.m_st(1))
                for t in range(2):
                    for q in range(2):
                        ins = act.copy(vns[0][:, t, 512 * q:512 * (q + 1)], bank[2 + 4 * t + q][:, :])
                ins.then_inc(a.m_y.up, 1)

                def tokens_high():
                    for q in range(2):
                        ins = act.copy(xTs[0][:, 4 * q:4 * q + 4, :].rearrange("p a b -> p (a b)"), bank[2 + q][:, :])
                    ins.then_inc(s.gq_ptc.up, 1)

                def selection(n):
                    act.wait_ge(*a.m_st(n))
                    act.copy(selT[:, :, :], bank[1][:, 0:2 * P].rearrange("p (a n) -> p a n", a=2)).then_inc(a.m_sT.up, 1)

                act.wait_ge(*s.gq_max(1))
                tokens_high()
                selection(2)
                with act.Fori(0, NE // 2) as i:
                    for e in range(2):
                        def past(per, n):
                            return 2 * per * i + (per * e + n)

                        def high(q):
                            n = MOE0 + PER * e + q // 2
                            act.wait_ge(slot_full[n % RING], 16 * (2 * PER // RING) * i + 16 * (n // RING + 1))
                            act.wait_ge(*used(past(3 * NF, q + 1)))
                            act.copy(wsp[0][:, q % 4, :], ring[:, n % RING, D * (q % 2):D * (q % 2 + 1)]).then_inc(s.gq_o.up, 1)

                        def hidden_high(c):
                            act.wait_ge(*a.f_sil(past(NF // 2, c + 1)))
                            act.copy(hTs[0][:, 2 * c:2 * c + 2, :],
                                     bank[2 + c % 2][:, 0:2 * P].rearrange("p (a n) -> p a n", a=2)).then_inc(s.gq_on.up, 1)

                        for q in range(4):
                            high(q)
                        for c in range(NF // 2):
                            for r in range(3):
                                high(4 * c + 4 + r)
                            if c:
                                hidden_high(c - 1)
                            high(4 * c + 7)
                            act.wait_ge(*used(past(3 * NF, 4 * c + 8)))
                            act.wait_ge(*a.f_hid(past(NF // 2, c + 1)))
                            act.activation(sil2[:, c % 2, :], bank[c % 2][:, 0:CW], ACT.Silu).then_inc(a.f_mm.up, 1)
                        for q in range(2 * NF + 4, 3 * NF):
                            high(q)
                            if q == 2 * NF + 5:
                                hidden_high(NF // 2 - 1)
                        act.wait_ge(*used(past(3 * NF, 3 * NF + 4)))
                        act.copy(ysb[:, 0:512], bank[4][:, :])
                        act.copy(ysb[:, 512:D], bank[5][:, :]).then_inc(a.m_y.up, 1)
                        act.wait_ge(*s.gq_max(past(1, 2)))
                        tokens_high()
                        selection(past(1, 3))
                act.wait_ge(*a.f_acc(NE + 2))

            load_vectors(0)
            act.dma_start(consts[:, C_ONE:], d["consts"][:, C_ONE:]).then_inc(consts_in, 16)
            act.dma_start(halfc[:, :], d["halfc"]).then_inc(consts_in, 16)

            def squares(g, tiles, at):
                for t in tiles:
                    square(g, t, t - tiles[0], at)

            def square(g, t, before, at):
                if before:
                    act.wait_ge(*g(before))
                act.activation(junk, h[:, t, :], ACT.Square, accum_out=stat[:, 0, at + t:at + t + 1]).then_inc(g.up, 1)

            def root(x, g_ready, g_done):
                act.wait_ge(*g_ready(1))
                act.activation(x, x, ACT.Sqrt).then_inc(g_done.up, 1)

            def prenorm_evac(sub, g_tp, g_ok, tiles):
                for k in range(1, KD, 2):
                    act.wait_ge(*g_tp(k + 1))
                    act.wait_ge(*g_ok(k))
                    for st in ((0, 1) if len(tiles) == NT else (1,)):
                        ins = act.activation(uT[:, k, SEQ * st:SEQ * (st + 1)], bank[k % 4][:, SEQ * st:SEQ * (st + 1)],
                                             ACT.Identity, scale=scl[:, sub, k, 1 - st:2 - st],
                                             bias=mod[:, 24 * sub + k, 1 - st:2 - st])
                    ins.then_inc(g_ok.up, 1)

            def gate_rows(g_m, g_ok, streams):
                for n in range(2 * len(streams)):
                    act.wait_ge(*g_m(n + 1))
                    act.copy(GB[:, streams[n // 2], 512 * (n % 2):512 * (n % 2 + 1)], bank[4 + n][:, :]).then_inc(g_ok.up, 1)

            def post_squares(g, l, tiles):
                for i, t in enumerate(tiles):
                    for hf in range(2):
                        if i or hf:
                            act.wait_ge(*g(2 * i + hf))
                        act.activation(area(A_TR + 6144, 512), bank[2 * t + hf][:, :], ACT.Square,
                                       accum_out=stat[:, 1, 2 * t + hf:2 * t + hf + 1]).then_inc(g.up, 1)

            for l in range(DEPTH):
                s = sig[l]
                ctx_out = l < DEPTH - 1
                tiles = list(range(NT)) if ctx_out else [2, 3]
                lo = 0 if ctx_out else SEQ
                g_whi, g_wlo, g_xhi, g_xlo, g_used = s.m_y, s.m_hTs, s.m_sel, s.m_sT, s.m_st
                for j in range(NADA):
                    act.wait_ge(*s.ada_mm(j + 1))
                    act.copy(ada_rows[:, CW * j:CW * (j + 1)], bank[2 + j % 2][0:2, 0:CW]).then_inc(s.ada_row.up, 1)
                    if 4 <= j < 4 + NT:
                        if l == 0 and j == 4:
                            act.wait_ge(h_in, 64)
                        elif j == 4:
                            act.wait_ge(*sig[0].po_h2(NT))
                        square(s.ssq1, j - 4, j - 4, 0)
                    if j == 5 + NT:
                        root(stat[:, 0, 0:NT], s.rms1, s.rs1)
                prenorm_evac(0, s.tp1, s.u_ok, range(NT))

                unit = 0
                act.wait_ge(*s.pad_ok(1))
                for part in WIN[:-1]:
                    for c0 in part:
                        for q in range(1 if c0 == OFF_AB else 2):
                            act.wait_ge(*s.win_mm(unit + 1))
                            b = bank[unit % 4]
                            half = b[:, :].rearrange("p (a n) -> p a n", a=2)
                            if c0 < OFF_Z:
                                dst, src = conv_in[:, 2 * (c0 // 256) + q, :, HALO:HALO + SEQ], half
                            elif c0 == OFF_F:
                                dst, src = fT[:, q, :], b[:, :]
                            elif c0 == OFF_AB:
                                dst, src = gs[:, 2:4, :, :].rearrange("p a t n -> p t a n"), \
                                    b[:, 0:64].rearrange("p (t a n) -> p t a n", t=NT, a=2)
                            elif c0 == OFF_Z:
                                dst, src = zn[:, 2 * q:2 * q + 2, :], half
                            else:
                                dst, src = gqn[:, 2 * q:2 * q + 2, c0 - OFF_GQA:c0 - OFF_GQA + 256], half
                            act.copy(dst, src).then_inc(s.win_ok.up, 1)
                            unit += 1

                def retention_evac(j):
                    unit = UNITS + j
                    act.wait_ge(*s.win_mm(unit + 1))
                    act.copy(rtn[:, 2 * (j % 2):2 * (j % 2) + 2, CW * (j // 2):CW * (j // 2 + 1)],
                             bank[6 + unit % 2][:, :].rearrange("p (a n) -> p a n", a=2)).then_inc(s.win_ok.up, 1)

                act.wait_ge(prm_in[l], 96)
                act.activation(prm_exp[:, :], bc[:, 448:472], ACT.Exp).then_inc(s.prm_e.up, 1)
                act.wait_ge(*s.ab_x(1))
                link(act.activation(gs[:, 5], gs[:, 4], ACT.Abs))
                act.activation(gs[:, 6], gs[:, 2], ACT.Exp, scale=-1.0)
                link(act.activation(gs[:, 7], gs[:, 5], ACT.Exp, scale=-1.0))
                act.activation(gs[:, 8], gs[:, 7], ACT.Ln, bias=1.0).then_inc(s.ab_e.up, 1)

                for t in range(NT):
                    act.wait_ge(*s.fn_mm1(t + 1))
                    act.copy(area(A_TR, NT, 512)[:, t, :], bank[t][:, :]).then_inc(s.fn_c.up, 1)
                for c in range(2):
                    act.wait_ge(*s.fn_mm2(c + 1))
                    act.copy(yT[:, 3, c, :], bank[4 + c][:, :]).then_inc(s.fn_ok.up, 1)

                ahead = AHEAD[l]
                root(small[:, 32:56], s.gq_sq, s.gq_rs)
                for j in range(ahead // 2):
                    retention_evac(j)
                gT = area(A_TR + 2048, 4, TOK)
                for t in range(NT):
                    act.wait_ge(*s.gq_tp(t + 1))
                    act.copy(gT[:, :, P * t:P * (t + 1)], bank[t][:, :].rearrange("p (c n) -> p c n", c=4)).then_inc(s.gq_T.up, 1)
                Pb = area(A_TR + 4608, 2, 512)
                work = [(t, hh) for t in tiles for hh in range(NH)]
                for n, (t, hh) in enumerate(work):
                    keys = SEQ if t < 2 else TOK
                    act.wait_ge(*s.gq_max(n + 1))
                    if n >= 2:
                        act.wait_ge(*s.gq_pt(n - 1))
                    act.activation(Pb[:, n % 2, 0:keys], bank[n % 2][:, 0:keys], ACT.Exp, bias=small[:, n:n + 1],
                                   scale=HD ** -0.5, accum_out=small[:, 16 + n:17 + n]).then_inc(s.gq_e.up, 1)
                    if n % 2 and ahead + n < 4 * NT:
                        retention_evac((ahead + n) // 2)
                if not ctx_out:
                    retention_evac(7)
                for c in range(2):
                    act.wait_ge(*s.gq_yt(c + 1))
                    act.copy(yT[:, 2, c, lo:TOK], bank[6 + c][:, lo:TOK]).then_inc(s.gq_y.up, 1)

                act.wait_ge(*s.rt_w(1))
                for t in range(NT):
                    act.wait_ge(*s.rt_tp(t + 1))
                    act.copy(area(A_TR, 4, TOK)[:, :, P * t:P * (t + 1)],
                             bank[t][:, :].rearrange("p (c n) -> p c n", c=4)).then_inc(s.rt_T.up, 1)
                for hh in range(NH):
                    if hh:
                        act.wait_ge(*s.rt_wok(hh))
                    for dr in range(2):
                        act.activation(area(A_TR + 2048 + 1024 * dr, 4 * SEQ),
                                       halfc[:, H_DIST + 1024 * dr:H_DIST + 1024 * (dr + 1)], ACT.Exp,
                                       scale=lgam[:, 4 * dr + hh:4 * dr + hh + 1]).then_inc(s.rt_wm.up, 1)
                act.wait_ge(*s.rt_o((2 if ctx_out else 1) * NH))
                act.activation(area(A_TR + 3072, NT, BW), rtn[:, :, 768:1024], ACT.Silu).then_inc(s.rt_silu.up, 1)
                root(small[:, 112 + NH * tiles[0]:112 + NH * NT], s.rt_var, s.rt_rs)
                for c in range(2):
                    act.wait_ge(*s.rt_yt(c + 1))
                    act.copy(yT[:, 1, c, lo:TOK], bank[6 + c][:, lo:TOK]).then_inc(s.rt_y.up, 1)

                act.wait_ge(*s.conv_ok(1))
                for c in range(6):
                    act.activation(conv_out[:, c, :], conv_out[:, c, :], ACT.Silu).then_inc(s.silu_ok.up, 1)
                for t in range(NT):
                    for q in range(2):
                        act.wait_ge(*s.cT_mm(2 * t + q + 1))
                        act.copy(qkv[:, t, 512 * q:512 * q + (256 if q else 512)],
                                 bank[2 * (t % 2) + q][:, 0:(256 if q else 512)]).then_inc(s.cT_ok.up, 1)
                root(small[:, 128:160], s.l2_sq, s.l2_rs)
                for t in range(NT):
                    act.wait_ge(*s.qk_mm(t + 1))
                    tok, b = slice(P * t, P * (t + 1)), bank[4 + t][:, :].rearrange("p (c n) -> p c n", c=4)
                    if t == 0:
                        act.wait_ge(*s.kz_0(1))
                    act.copy(qT[:, :, tok], b[:, 0:2, :])
                    act.copy(kz[0:HD, 0:NH:2, tok], b[0:HD, 2:4, :])
                    act.copy(kz[HD:P, 1:NH:2, tok], b[HD:P, 2:4, :]).then_inc(s.qk_ok.up, 1)
                for dr in range(2):
                    act.wait_ge(*s.gl_ok(1 + dr))
                    act.activation(gg[:, 3:6, :, :], gg[:, 0:3, :, :], ACT.Exp).then_inc(s.gl_e.up, 1)
                    for t in range(NT):
                        n = NT * dr + t
                        act.wait_ge(*s.gd_mm(n + 1))
                        if n >= 2:
                            act.wait_ge(*s.gd_es(n - 1))
                        for hh in range(NH):
                            ins = act.activation(Eb[:, n % 2, hh, :], bank[n % 2][:, P * hh:P * (hh + 1)], ACT.Abs,
                                                 bias=negG[:, t, hh:hh + 1])
                        ins.then_inc(s.gd_abs.up, 1)
                        act.wait_ge(*s.gd_abs(n + 1))
                        act.activation(Eb[:, n % 2, :, :], Eb[:, n % 2, :, :], ACT.Exp, scale=-1.0).then_inc(s.gd_exp.up, 1)
                        if t >= 1:
                            for u in ([n - 1] if t < NT - 1 else [n - 1, n]):
                                act.wait_ge(*s.gd_MT(u + 1))
                                act.copy(MT[:, u % NT, :, :], bank[6 + u % 2][:, :].rearrange("p (h n) -> p h n", h=NH)).then_inc(s.gd_MTs.up, 1)
                    for t in range(NT):
                        act.wait_ge(*s.uw_mm(NT * dr + t + 1))
                        v = bank[4 + t][:, :].rearrange("p (h a n) -> p h a n", h=NH, a=2)
                        act.copy(un[:, t, :].rearrange("p (h n) -> p h n", h=NH), v[:, :, 0, :])
                        act.copy(wn[:, t, :].rearrange("p (h n) -> p h n", h=NH), v[:, :, 1, :]).then_inc(s.uw_ok.up, 1)
                    for t in range(NT):
                        act.wait_ge(*s.wq_mm(NT * dr + t + 1))
                        v = bank[t][:, :].rearrange("p (a c n) -> p a c n", a=2, c=2)
                        act.copy(wT[:, :, P * t:P * (t + 1)], v[:, 0, :, :])
                        act.copy(qtilT[:, :, P * t:P * (t + 1)], v[:, 1, :, :]).then_inc(s.wq_ok.up, 1)
                act.activation(zn[:, :, :], zn[:, :, :], ACT.Silu).then_inc(s.z_silu.up, 1)
                root(small[:, 160 + NH * tiles[0]:160 + NH * NT], s.gdy_sq, s.gdy_rs)
                for c in range(2):
                    act.wait_ge(*s.gdy_tp(c + 1))
                    act.copy(yT[:, 0, c, lo:TOK], bank[c][:, lo:TOK]).then_inc(s.gdy_ok.up, 1)

                act.wait_ge(*s.gdy_n(1))
                def load_branch(br):
                    act.dma_start(wbr[:, (3 - br) % 2], d["w_branch"][l][br].rearrange("(k p) n -> p k n", p=P)).then_inc(
                        branch_in[br], 16)

                def gate(n):
                    br, c = (3, 2, 1, 0)[n // KD], n % KD
                    act.wait_ge(*s.mg_mm(n + 1))
                    if n >= 2:
                        act.wait_ge(*s.mg_add(n - 1))
                    act.activation(area(A_TR, 2, TOK)[:, n % 2, lo:TOK], bank[4 * (n // 2 % 2) + n % 2][:, lo:TOK], ACT.Sigmoid,
                                   bias=colB[:, V_BG + 8 * br + c:V_BG + 8 * br + c + 1]).then_inc(s.mg_sig.up, 1)
                    if c == KD - 1 and br >= 2:
                        load_branch(br - 2)

                load_branch(3)
                load_branch(2)
                act.wait_ge(*s.gdy_ok(2))
                for k in range(4):
                    act.copy(xg_hi[:, k, lo:TOK], uT[:, k, lo:TOK]).then_inc(g_xhi.up, 1)
                for q in range(MW):
                    n = GATES[l] + q // 2
                    act.wait_ge(slot_full[n % RING], 16 * (n // RING + 1))
                    if q >= 3:
                        act.wait_ge(*g_used(q - 2))
                    act.copy(gsp[0][:, q % 3, :], half_slot(GATES[l], q)).then_inc(g_whi.up, 1)
                    if q == 0:
                        for k in range(4, KD):
                            act.copy(xg_hi[:, k, lo:TOK], uT[:, k, lo:TOK]).then_inc(g_xhi.up, 1)
                    if q % 2 == 0 and q >= 4:
                        gate(q - 4)
                        gate(q - 3)
                for n in range(MW - 4, MW):
                    gate(n)
                gate_rows(s.gb_m1, s.gb_ok1, [0, 1] if ctx_out else [1])
                act.wait_ge(*s.po_mm(1))
                post_squares(s.po_sq1, l, tiles)
                root(stat[:, 1, 8 + tiles[0]:12], s.po_ss1, s.po_rs1)
                act.wait_ge(*s.po_h1(len(tiles)))
                squares(s.ssq2, tiles, 4)
                root(stat[:, 0, 4 + tiles[0]:4 + NT], s.rms2, s.rs2)
                gate_rows(s.gb_m2, s.gb_ok2, [0, 1] if ctx_out else [1])
                prenorm_evac(1, s.tp2, s.v_ok, tiles)
                if l == 0:
                    act.wait_ge(*s.v_ok(KD))
                    load_vectors(1)

                sil = area(A_TR, 2, TOK)
                if ctx_out:
                    def input_high(half):
                        for k in range(4 * half, 4 * half + 4):
                            act.copy(x_high(k), uT[:, k, :]).then_inc(g_xhi.up, 1)

                    input_high(0)
                    for q in range(3 * NF):
                        act.wait_ge(slot_full[(FFN0 + q // 2) % RING], 16 * ((FFN0 + q // 2) // RING + 1))
                        if q >= 3:
                            act.wait_ge(*g_used(MW + q - 2))
                        act.copy(dsp[0][:, q % 3, :], half_slot(FFN0, q)).then_inc(g_whi.up, 1)
                        if q == 0:
                            input_high(1)
                        f = q - 2 * NF
                        if f >= 0:
                            if f == 0:
                                act.wait_ge(*g_used(MW + 2 * NF))
                            act.wait_ge(*s.f_hid(f + 1))
                            act.copy(hsp[0][:, f % 3, :], hid[:, f, :]).then_inc(g_xhi.up, 1)
                        if q % 4 == 2 and 6 <= q < 2 * NF + 4:
                            c = (q - 6) // 4
                            act.wait_ge(*g_used(MW + 4 * c + 4))
                            for f in (2 * c, 2 * c + 1):
                                if f >= 2:
                                    act.wait_ge(*s.f_hid(f - 1))
                                act.activation(sil0[:, f % 2, :], bank[4 * (c % 2) + f % 2][:, :], ACT.Silu).then_inc(s.f_sil.up, 1)
                    act.wait_ge(*s.f_out(1))
                    post_squares(s.po_sq2, l, tiles)
                    root(stat[:, 1, 8:12], s.po_ss2, s.po_rs2)
                else:
                    act.wait_ge(*s.rcomb(1))
                    act.activation(small[:, 188:190], small[:, 188:190], ACT.Exp).then_inc(s.rcomb.up, 1)
                    act.wait_ge(*s.rcomb(4))
                    dense = act.value_load(crowded[0:1, 0:1], min_val=0, max_val=1)
                    with act.If(dense):
                        dense_experts_act(s, sil)
                    with act.Else():
                        sparse_experts_act(again)
                    for t in range(2):
                        if t:
                            act.wait_ge(*s.po_sq2(t))
                        act.activation(area(A_TR + 6144, D), macc[:, t, :], ACT.Square,
                                       accum_out=stat[:, 1, 10 + t:11 + t]).then_inc(s.po_sq2.up, 1)
                    root(stat[:, 1, 10:12], s.po_ss2, s.po_rs2)

        @block.gpsimd
        def _(pool):
            link = linker(pool, pool_chain)
            pool.wait_ge(c_in, 48)
            pool.wait_ge(consts_in, 32)

            for l in range(DEPTH):
                s = sig[l]
                ctx_out = l < DEPTH - 1
                t0 = 0 if ctx_out else 2
                if l:
                    pool.wait_ge(*sig[0].po_h2(NT))
                link(pool.memset(conv_in[:, :, :, 0:HALO], 0.0))
                pool.memset(conv_in[:, :, :, HALO + SEQ:], 0.0).then_inc(s.pad_ok.up, 1)

                for hh in range(NH):
                    pool.wait_ge(*s.rt_wm(2 * hh + 2))
                    wf, wb = area(A_TR + 2048, 4, SEQ), area(A_TR + 3072, 4, SEQ)
                    m = halfc[:, H_RM:H_RM + 1024].rearrange("p (d j n) -> p d j n", d=2, j=2)
                    link(pool.tensor_tensor(wf[:, 0:2, :], wf[:, 0:2, :], m[:, 0], ALU.mult))
                    link(pool.tensor_tensor(wb[:, 0:2, :], wb[:, 0:2, :], m[:, 1], ALU.mult))
                    if hh:
                        pool.wait_ge(*s.rt_p((2 if ctx_out else 1) * hh))
                    pool.tensor_tensor(area(A_TR + 4096, 4, SEQ), wf, wb, ALU.add).then_inc(s.rt_wok.up, 1)

                pool.wait_ge(*s.cT_mm(2 * NT))
                pool.memset(kz[HD:P, 0:NH:2, :], 0.0)
                pool.memset(kz[0:HD, 1:NH:2, :], 0.0).then_inc(s.kz_0.up, 1)
                for dr in range(2):
                    for t in range(NT):
                        n = NT * dr + t
                        pool.wait_ge(*s.gd_exp(n + 1))
                        if n >= 2:
                            pool.wait_ge(*s.gd_M(n - 1))
                            pool.wait_ge(*s.gd_A(n - 1))
                        if dr and t == 0:
                            pool.wait_ge(*s.st_oa(NT))
                        pool.tensor_tensor(Es[:, 0, n % 2], Eb[:, n % 2], gmask(dr, 0), ALU.mult)
                        pool.tensor_tensor(Es[:, 1, n % 2], Eb[:, n % 2], gmask(dr, 1), ALU.mult).then_inc(s.gd_es.up, 1)
                        if t >= 1:
                            for u in ([n - 1] if t < NT - 1 else [n - 1, n]):
                                ut = u % NT
                                eye = ident.unsqueeze(1).to_broadcast([P, NH, P])
                                pool.wait_ge(*s.gd_M(u + 1))
                                link(pool.tensor_tensor(X[:, ut], T1[:, ut], gmask(dr, 2), ALU.mult))
                                pool.tensor_tensor(X[:, ut], eye, X[:, ut], ALU.subtract).then_inc(s.gd_X.up, 1)
                                pool.wait_ge(*s.gd_MTs(u + 1))
                                link(pool.tensor_tensor(XT[:, ut], MT[:, ut], gmask(dr, 3), ALU.mult))
                                pool.tensor_tensor(XT[:, ut], eye, XT[:, ut], ALU.subtract).then_inc(s.gd_XT.up, 1)
                    pool.wait_ge(*s.gd_A(NT * (dr + 1)))
                    pool.wait_ge(*s.gl_e(dr + 1))
                    beta = gs[:, 0, :, NH * dr:NH * (dr + 1)]
                    link(pool.tensor_tensor(betaG[:, :, :], beta, gg[:, 3], ALU.mult))
                    q4, k4, v4 = (qkv[:, :, BW * i:BW * (i + 1)].rearrange("p t (h n) -> p t h n", h=NH) for i in range(3))
                    for t in range(NT):
                        pool.tensor_tensor(R[:, t, :, 0:HD], v4[:, t], beta[:, t].unsqueeze(2).to_broadcast([P, NH, HD]), ALU.mult)
                        ins = pool.tensor_tensor(R[:, t, :, HD:P], k4[:, t],
                                                 betaG[:, t].unsqueeze(2).to_broadcast([P, NH, HD]), ALU.mult)
                    ins.then_inc(s.gd_R.up, 1)
                    pool.wait_ge(*s.lv_mm1(LEVELS * NT * (dr + 1)))
                    for t in range(NT):
                        pool.tensor_tensor(qtil[:, t, :].rearrange("p (h n) -> p h n", h=NH), q4[:, t],
                                           gg[:, 3, t].unsqueeze(2).to_broadcast([P, NH, HD]), ALU.mult)
                        ins = pool.tensor_tensor(kdec[:, t, :].rearrange("p (h n) -> p h n", h=NH), k4[:, t],
                                                 gg[:, 4, t].unsqueeze(2).to_broadcast([P, NH, HD]), ALU.mult)
                    ins.then_inc(s.gd_q.up, 1)

        @block.vector
        def _(v):
            link = linker(v, dve_chain)
            v.wait_ge(c_in, 48)
            v.wait_ge(consts_in, 32)
            v.wait_ge(h_in, 64)

            def per_head(x):
                return x.unsqueeze(2).to_broadcast([P, x.shape[1], HD])

            def mean_eps(x, n, g_ready):
                v.tensor_scalar(x, x, 1.0 / n, EPS, ALU.mult, ALU.add).then_inc(g_ready.up, 1)

            def inverse(x, g_done):
                v.wait_ge(*g_done(1))
                link(v.reciprocal(x, x))

            def normalise(g_sq, g_ss, g_rs, g_xs, tiles, at):
                v.wait_ge(*g_sq(len(tiles)))
                x = stat[:, 0, at + tiles[0]:at + NT]
                mean_eps(x, D, g_ss)
                inverse(x, g_rs)
                for t in tiles:
                    v.tensor_scalar(xs[:, t, :], h[:, t, :], stat[:, 0, at + t:at + t + 1], None, ALU.mult).then_inc(g_xs.up, 1)

            def modulate(sub, g_tp, g_ok, tiles):
                for k in range(0, KD, 2):
                    v.wait_ge(*g_tp(k + 1))
                    if k:
                        v.wait_ge(*g_ok(k))
                    for st in ((0, 1) if len(tiles) == NT else (1,)):
                        ins = v.tensor_scalar(uT[:, k, SEQ * st:SEQ * (st + 1)], bank[k % 4][:, SEQ * st:SEQ * (st + 1)],
                                              scl[:, sub, k, 1 - st:2 - st], mod[:, 24 * sub + k, 1 - st:2 - st],
                                              ALU.mult, ALU.add)
                    ins.then_inc(g_ok.up, 1)

            def gate_diag(sub, g_d, g_m, streams):
                for n in range(2 * len(streams)):
                    if n >= 2:
                        v.wait_ge(*g_m(n - 1))
                    st = streams[n // 2]
                    for q in range(4):
                        k = 4 * (n % 2) + q
                        ins = v.tensor_scalar(area(A_TR + 5120 + 512 * (n % 2), 4, P)[:, q], ident,
                                              gpost[:, sub, k, 1 - st:2 - st], None, ALU.mult)
                    ins.then_inc(g_d.up, 1)

            def post_add(g_sq, g_ss, g_rs, g_gb, g_h, tiles):
                t0, nt = tiles[0], len(tiles)
                v.wait_ge(*g_sq(2 * nt))
                ss = stat[:, 1, 0:8].rearrange("p (t a) -> p t a", a=2)
                x = stat[:, 1, 8 + t0:12]
                link(v.tensor_tensor(x, ss[:, t0:NT, 0], ss[:, t0:NT, 1], ALU.add))
                mean_eps(x, D, g_ss)
                inverse(x, g_rs)
                v.wait_ge(*g_gb(nt))
                for t in tiles:
                    for hf in range(2):
                        c = slice(512 * hf, 512 * (hf + 1))
                        link(v.scalar_tensor_tensor(area(A_TR + 512 * hf, 512), bank[2 * t + hf][:, :],
                                                    stat[:, 1, 8 + t:9 + t], GB[:, t // 2, c], ALU.mult, ALU.mult))
                        ins = v.tensor_tensor(h[:, t, c], h[:, t, c], area(A_TR + 512 * hf, 512), ALU.add)
                    ins.then_inc(g_h.up, 1)

            def rope(x, tmp, t, heads):
                tab = consts[:, C_ROPE + 64 * (t - 2):C_ROPE + 64 * (t - 1)]
                cs = tab[:, 0:32].unsqueeze(1).to_broadcast([P, heads, 32])
                sn = tab[:, 32:64].unsqueeze(1).to_broadcast([P, heads, 32])
                y = x.rearrange("p h (a n) -> p h a n", a=2)
                m = tmp.rearrange("p (q h n) -> p q h n", q=4, n=32)
                v.tensor_tensor(m[:, 0], y[:, :, 0], cs, ALU.mult)
                v.tensor_tensor(m[:, 1], y[:, :, 1], sn, ALU.mult)
                v.tensor_tensor(m[:, 2], y[:, :, 0], sn, ALU.mult)
                link(v.tensor_tensor(m[:, 3], y[:, :, 1], cs, ALU.mult))
                v.tensor_tensor(y[:, :, 0], m[:, 0], m[:, 1], ALU.subtract)
                link(v.tensor_tensor(y[:, :, 1], m[:, 2], m[:, 3], ALU.add))

            def dense_experts_dve(s, sil):
                with v.Fori(0, NE) as e:
                    for f in range(NF):
                        v.wait_ge(*s.f_sil(NF * e + (f + 1)))
                        v.tensor_tensor(hid[:, f, 0:SEQ], sil[:, f % 2, 0:SEQ], bank[2 + f % 2][:, 0:SEQ],
                                        ALU.mult).then_inc(s.f_hid.up, 1)
                    v.wait_ge(*s.f_out(e + 1))
                    v.wait_ge(*s.f_acc(e + 1))
                    for t in range(2):
                        for hf in range(2):
                            c = slice(512 * hf, 512 * (hf + 1))
                            ins = v.scalar_tensor_tensor(macc[:, t, c], bank[4 + 2 * t + hf][:, :], comb[:, t, bass.ds(e + 1, 1)],
                                                         macc[:, t, c], ALU.mult, ALU.add)
                    ins.then_inc(s.f_acc.up, 1)

            def sparse_experts_dve(s):
                a = moe
                v.wait_ge(*a.m_y(1))
                for t in range(2):
                    for q in range(2):
                        c = slice(512 * q, 512 * (q + 1))
                        ins = v.tensor_tensor(vns[1][:, t, c], bank[2 + 4 * t + q][:, :], vns[0][:, t, c], ALU.subtract)
                link(ins)

                def select(col):
                    for t in range(2):
                        v.tensor_scalar(sel[:, t, :], iota[:, :], rank[:, t, col], None, ALU.is_equal)
                        ins = v.tensor_scalar(sel_r[:, t, :], iota[:, :], rank[:, t, col], None, ALU.is_equal)
                    ins.then_inc(a.m_sel.up, 1)

                def accumulate(col):
                    for t in range(2):
                        for hf in range(2):
                            c = slice(512 * hf, 512 * (hf + 1))
                            ins = v.scalar_tensor_tensor(macc[:, t, c], bank[(6, 4)[t] + hf][:, :], comb[:, t, col],
                                                         macc[:, t, c], ALU.mult, ALU.add)
                    ins.then_inc(a.f_acc.up, 1)

                def tokens_low():
                    for q in range(2):
                        k = slice(4 * q, 4 * q + 4)
                        ins = v.tensor_tensor(xTs[1][:, k, :], bank[2 + q][:, :].rearrange("p (a n) -> p a n", a=4),
                                              xTs[0][:, k, :], ALU.subtract)
                    ins.then_inc(s.gq_e.up, 1)

                v.memset(selT[:, :, :], 0.0)
                link(v.memset(ysb, 0.0))
                select(slice(0, 1))
                v.wait_ge(*s.gq_ptc(1))
                tokens_low()
                with v.Fori(0, NE // 2) as i:
                    for e in range(2):
                        def past(per, n):
                            return 2 * per * i + (per * e + n)

                        def low(q):
                            n = MOE0 + PER * e + q // 2
                            v.wait_ge(*s.gq_o(past(3 * NF, q + 1)))
                            v.tensor_tensor(wsp[1][:, q % 4, :], ring[:, n % RING, D * (q % 2):D * (q % 2 + 1)],
                                            wsp[0][:, q % 4, :], ALU.subtract).then_inc(s.gq_pt.up, 1)
                            if q % 2 == 0 and q:
                                v.wait_ge(*s.gq_pt(past(3 * NF, q)))
                                v.sem_inc(slot_free, 1)
                            if q == 3 * NF - 1:
                                v.wait_ge(*s.gq_pt(past(3 * NF, q + 1)))
                                v.sem_inc(slot_free, 1)

                        def hidden_low(c):
                            v.wait_ge(*s.gq_on(past(NF // 2, c + 1)))
                            v.tensor_tensor(hTs[1][:, 2 * c:2 * c + 2, :],
                                            bank[2 + c % 2][:, 0:2 * P].rearrange("p (a n) -> p a n", a=2),
                                            hTs[0][:, 2 * c:2 * c + 2, :], ALU.subtract).then_inc(a.m_hTs.up, 1)

                        for q in range(4):
                            low(q)
                        v.wait_ge(*a.f_out(past(1, 1)))
                        v.wait_ge(*a.f_acc(past(1, 1)))
                        accumulate(bass.ds(2 * i + e, 1))
                        v.wait_ge(*a.m_st(past(1, 2)))
                        select(bass.ds(2 * i + (e + 1), 1))
                        for c in range(NF // 2):
                            for r in range(3):
                                low(4 * c + 4 + r)
                            if c:
                                hidden_low(c - 1)
                            low(4 * c + 7)
                            v.wait_ge(*a.f_mm(past(NF // 2, c + 1)))
                            if c >= 2:
                                v.wait_ge(*a.f_sil(past(NF // 2, c - 1)))
                            v.tensor_tensor(hn[:, c % 2, :], sil2[:, c % 2, :], bank[c % 2][:, CW:2 * CW],
                                            ALU.mult).then_inc(a.f_hid.up, 1)
                        for q in range(2 * NF + 4, 3 * NF):
                            low(q)
                            if q == 2 * NF + 5:
                                hidden_low(NF // 2 - 1)
                        v.wait_ge(*s.gq_ptc(past(1, 2)))
                        tokens_low()
                v.wait_ge(*a.f_out(NE + 1))
                v.wait_ge(*a.f_acc(NE + 1))
                accumulate(slice(NE, NE + 1))

            link(v.memset(S[:, :, :, :], 0.0))
            for l in range(DEPTH):
                s = sig[l]
                ctx_out = l < DEPTH - 1
                tiles = list(range(NT)) if ctx_out else [2, 3]
                t0 = tiles[0]
                streams = [0, 1] if ctx_out else [1]
                lo = 0 if ctx_out else SEQ
                g_whi, g_wlo, g_xhi, g_xlo, g_used = s.m_y, s.m_hTs, s.m_sel, s.m_sT, s.m_st

                normalise(s.ssq1, s.rms1, s.rs1, s.xs1, range(NT), 0)
                v.wait_ge(*s.vec_T(1))
                v.tensor_copy(colA[:, :], bank[0][:, 0:80])
                link(v.tensor_copy(colB[:, :], bank[0][:, 80:142]))
                v.sem_inc(s.vec_ok.up, 1)
                v.wait_ge(*s.ada_mm(NADA + 1))
                link(v.tensor_tensor(mod[:, :, :], bank[1][:, 0:96].rearrange("p (n a) -> p n a", a=2),
                                     colA[:, 0:48].unsqueeze(2).to_broadcast([P, 48, 2]), ALU.add))

                def gvec(i):
                    return colA[:, V_NG + 8 * i:V_NG + 8 * (i + 1)].unsqueeze(2).to_broadcast([P, KD, 2])

                for sub in range(2):
                    v.scalar_tensor_tensor(scl[:, sub], mod[:, 24 * sub + 8:24 * sub + 16, :], 1.0, gvec(2 * sub),
                                           ALU.add, ALU.mult)
                    link(v.tensor_tensor(gpost[:, sub], mod[:, 24 * sub + 16:24 * sub + 24, :], gvec(2 * sub + 1), ALU.mult))
                v.sem_inc(s.mod_ok.up, 1)
                modulate(0, s.tp1, s.u_ok, range(NT))

                v.wait_ge(*s.win_ok(6))
                for j in range(TAPS):
                    for c in range(6):
                        o = conv_out[:, c, :].rearrange("p (a n) -> p a n", a=2)
                        x = conv_in[:, c, :, j:j + SEQ]
                        w = colB[:, V_CONV + 6 * j + c:V_CONV + 6 * j + c + 1]
                        if j == 0:
                            ins = v.tensor_scalar(o, x, w, None, ALU.mult)
                        else:
                            ins = v.scalar_tensor_tensor(o, x, w, o, ALU.mult, ALU.add)
                    link(ins)
                v.sem_inc(s.conv_ok.up, 1)

                v.wait_ge(prm_in[l], 96)
                v.wait_ge(*s.win_ok(9))
                v.tensor_tensor(gs[:, 4], gs[:, 3], dtb.unsqueeze(1).to_broadcast([P, NT, 8]), ALU.add).then_inc(s.ab_x.up, 1)
                v.wait_ge(*s.ab_e(1))
                v.wait_ge(*s.prm_e(1))
                v.tensor_scalar(lgam[:, :], prm_exp[:, 16:24], -1.0, None, ALU.mult).then_inc(s.rt_w.up, 1)
                link(v.tensor_scalar(gs[:, 6], gs[:, 6], 1.0, None, ALU.add))
                link(v.reciprocal(gs[:, 0], gs[:, 6]))
                link(v.scalar_tensor_tensor(gs[:, 8], gs[:, 4], 0.0, gs[:, 8], ALU.max, ALU.add))
                v.scalar_tensor_tensor(gs[:, 1], gs[:, 8], -1.0, prm_exp[:, 0:8].unsqueeze(1).to_broadcast([P, NT, 8]),
                                       ALU.mult, ALU.mult).then_inc(s.ab_ok.up, 1)

                v.wait_ge(*s.win_ok(UNITS))
                gn = area(A_TR, NT, 8, HD)
                sq6 = area(A_TR + 4096, 6, HD)
                for t in range(NT):
                    x = gqn[:, t, 0:384].rearrange("p (h n) -> p h n", h=6)
                    link(v.tensor_tensor(sq6, x, x, ALU.mult))
                    ins = v.tensor_reduce(small[:, 32 + 6 * t:38 + 6 * t], sq6, AX, ALU.add)
                    link(ins)
                mean_eps(small[:, 32:56], HD, s.gq_sq)
                inverse(small[:, 32:56], s.gq_rs)
                v.wait_ge(*s.fn_mm2(2))
                for t in range(NT):
                    x = gqn[:, t, 0:384].rearrange("p (h n) -> p h n", h=6)
                    link(v.tensor_tensor(sq6, x, per_head(small[:, 32 + 6 * t:38 + 6 * t]), ALU.mult))
                    v.tensor_tensor(x[:, 0:4], sq6[:, 0:4], qkg[:, 0:HD].unsqueeze(1).to_broadcast([P, 4, HD]), ALU.mult)
                    link(v.tensor_tensor(x[:, 4:6], sq6[:, 4:6], qkg[:, HD:2 * HD].unsqueeze(1).to_broadcast([P, 2, HD]), ALU.mult))
                    if t >= 2:
                        rope(x, area(A_TR + 4608, 768), t, 6)
                    v.tensor_copy(gn[:, t, 0:4, :], x[:, 0:4])
                    for q in range(4):
                        ins = v.tensor_copy(gn[:, t, 4 + q, :], x[:, 4 + q // 2])
                    link(ins)
                v.sem_inc(s.gq_n.up, 1)
                work = [(t, hh) for t in tiles for hh in range(NH)]
                PTb = area(A_TR + 5632, 2, 4, P)
                og = area(A_TR, NT, BW)

                def gq_max(n):
                    t, hh = work[n]
                    keys = SEQ if t < 2 else TOK
                    v.wait_ge(*s.gq_s(n + 1))
                    link(v.tensor_reduce(small[:, 64 + n:65 + n], bank[n % 2][:, 0:keys], AX, ALU.max))
                    v.tensor_scalar(small[:, n:n + 1], small[:, 64 + n:65 + n], -HD ** -0.5, None, ALU.mult).then_inc(s.gq_max.up, 1)

                def gq_pt(n):
                    nk = 2 if work[n][0] < 2 else 4
                    v.wait_ge(*s.gq_pt(n + 1))
                    if n >= 2:
                        v.wait_ge(*s.gq_o(n - 1))
                    v.tensor_copy(PTb[:, n % 2, 0:nk, :], bank[2 + n % 2][:, 0:P * nk].rearrange("p (a n) -> p a n", a=nk)).then_inc(s.gq_ptc.up, 1)

                def gq_norm(n):
                    t, hh = work[n]
                    v.wait_ge(*s.gq_o(n + 1))
                    link(v.reciprocal(small[:, 80 + n:81 + n], small[:, 16 + n:17 + n]))
                    v.tensor_scalar(og[:, t, HD * hh:HD * (hh + 1)], bank[4 + n % 2][:, 0:HD], small[:, 80 + n:81 + n],
                                    None, ALU.mult).then_inc(s.gq_on.up, 1)

                v.wait_ge(*s.gq_tp(NT))
                for n in range(len(work) + 2):
                    if n < len(work):
                        gq_max(n)
                    if 1 <= n <= len(work):
                        gq_pt(n - 1)
                    if n >= 2:
                        gq_norm(n - 2)

                v.wait_ge(*s.win_ok(23))
                v.wait_ge(*s.gq_yt(2))
                for t in (2, 3):
                    for q in range(2):
                        rope(rtn[:, t, 256 * q:256 * (q + 1)].rearrange("p (h n) -> p h n", h=NH),
                             area(A_TR + 5120, 512), t, NH)
                v.sem_inc(s.rt_n.up, 1)
                PR = area(A_TR + 5120, 2, 4, SEQ)
                runits = [(hh, st) for hh in range(NH) for st in streams]
                for n, (hh, st) in enumerate(runits):
                    v.wait_ge(*s.rt_s(n + 1))
                    v.wait_ge(*s.rt_wok(hh + 1))
                    if n >= 2:
                        v.wait_ge(*s.rt_o(n - 1))
                    wsum = area(A_TR + 4096, 4, SEQ)
                    for q in range(1 + st):
                        wq = wsum[:, 2:4, :] if (st == 1 and q == 0) else wsum[:, 0:2, :]
                        ins = v.scalar_tensor_tensor(PR[:, n % 2, 2 * q:2 * q + 2, :],
                                                     bank[4 + 2 * (n % 2) + q][:, :].rearrange("p (a n) -> p a n", a=2),
                                                     HD ** -0.5, wq, ALU.mult, ALU.mult)
                    ins.then_inc(s.rt_p.up, 1)
                v.wait_ge(*s.rt_o(len(runits)))
                orr, cen = area(A_TR, NT, BW), area(A_TR + 1024, NT, BW)
                o4 = orr.rearrange("p t (h n) -> p t h n", h=NH)
                c4 = cen.rearrange("p t (h n) -> p t h n", h=NH)
                mu = small[:, 96:96 + NT * NH].rearrange("p (t h) -> p t h", t=NT)
                va = small[:, 112:112 + NT * NH].rearrange("p (t h) -> p t h", t=NT)
                for t in tiles:
                    ins = v.tensor_copy(orr[:, t, :], bank[t][:, 0:BW])
                link(ins)
                link(v.tensor_reduce(mu[:, t0:NT], o4[:, t0:NT], AX, ALU.add))
                link(v.tensor_scalar(mu[:, t0:NT], mu[:, t0:NT], 1.0 / HD, None, ALU.mult))
                for t in tiles:
                    ins = v.tensor_tensor(o4[:, t], o4[:, t], per_head(mu[:, t]), ALU.subtract)
                link(ins)
                link(v.tensor_tensor(cen[:, t0:NT], orr[:, t0:NT], orr[:, t0:NT], ALU.mult))
                link(v.tensor_reduce(va[:, t0:NT], c4[:, t0:NT], AX, ALU.add))
                mean_eps(va[:, t0:NT], HD, s.rt_var)
                inverse(va[:, t0:NT], s.rt_rs)
                v.wait_ge(*s.rt_silu(1))
                for t in tiles:
                    link(v.tensor_tensor(o4[:, t], o4[:, t], per_head(va[:, t]), ALU.mult))
                    link(v.tensor_tensor(orr[:, t], orr[:, t], retg, ALU.mult))
                    ins = v.tensor_tensor(orr[:, t], orr[:, t], area(A_TR + 3072, NT, BW)[:, t], ALU.mult)
                link(ins)
                v.sem_inc(s.rt_on.up, 1)

                ss8 = small[:, 128:160].rearrange("p (t h) -> p t h", t=NT)
                for t in range(NT):
                    v.wait_ge(*s.cT_ok(2 * t + 1))
                    x = qkv[:, t, 0:512].rearrange("p (h n) -> p h n", h=8)
                    sq = area(A_TR + 4096, 8, HD)
                    link(v.tensor_tensor(sq, x, x, ALU.mult))
                    link(v.tensor_reduce(ss8[:, t], sq, AX, ALU.add))
                mean_eps(ss8, 1, s.l2_sq)
                inverse(ss8, s.l2_rs)
                link(v.tensor_scalar(ss8[:, :, 0:NH], ss8[:, :, 0:NH], HD ** -0.5, None, ALU.mult))
                v.wait_ge(*s.cT_ok(2 * NT))
                for t in range(NT):
                    x = qkv[:, t, 0:512].rearrange("p (h n) -> p h n", h=8)
                    ins = v.tensor_tensor(x, x, per_head(ss8[:, t]), ALU.mult)
                link(ins)
                v.sem_inc(s.l2_ok.up, 1)
                v.wait_ge(*s.gl_mm(1))
                link(v.tensor_copy(gs[:, 9:12], bank[0][:, 0:96].rearrange("p (a t n) -> p a t n", a=3, t=NT)))
                for dr in range(2):
                    hd = slice(NH * dr, NH * (dr + 1))
                    if dr:
                        v.wait_ge(*s.gd_q(1))
                    v.tensor_copy(gg[:, 0], gs[:, 9 + dr, :, hd])
                    v.tensor_scalar(negG[:, :, :], gs[:, 9 + dr, :, hd], -1.0, None, ALU.mult)
                    v.tensor_tensor(gg[:, 1], gs[:, 11, :, hd], gs[:, 9 + dr, :, hd], ALU.subtract)
                    link(v.tensor_copy(gg[:, 2], gs[:, 11, :, hd]))
                    v.sem_inc(s.gl_ok.up, 1)

                    def tile_matrices(n):
                        t = n % NT
                        v.wait_ge(*s.gd_es(n + 1))
                        for hh in range(NH):
                            ins = v.scalar_tensor_tensor(T1[:, t, hh, :], bank[2 + n % 2][:, P * hh:P * (hh + 1)],
                                                         gs[:, 0, t, NH * dr + hh:NH * dr + hh + 1], Es[:, 0, n % 2, hh, :],
                                                         ALU.mult, ALU.mult)
                        ins.then_inc(s.gd_M.up, 1)
                        v.tensor_tensor(AT[:, t], bank[4 + n % 2][:, :].rearrange("p (h n) -> p h n", h=NH),
                                        Es[:, 1, n % 2], ALU.mult).then_inc(s.gd_A.up, 1)

                    for n in range(NT * dr, NT * dr + NT):
                        tile_matrices(n)
                    v.wait_ge(*s.gd_X(NT * (dr + 1)))
                    v.wait_ge(*s.gd_MT(NT * (dr + 1)))
                    for q in range(LEVELS):
                        base = (LEVELS * dr + q) * NT
                        for t in range(NT):
                            v.wait_ge(*s.lv_mm1(base + t + 1))
                            v.tensor_tensor(T1[:, t], bank[t][:, :].rearrange("p (h n) -> p h n", h=NH),
                                            gmask(dr, 4 + q), ALU.mult).then_inc(s.lv_T1.up, 1)
                        for t in range(NT):
                            v.wait_ge(*s.lv_mm2(base + t + 1))
                            if q < LEVELS - 1:
                                v.tensor_tensor(X[:, t], X[:, t], bank[4 + t][:, :].rearrange("p (h n) -> p h n", h=NH),
                                                ALU.subtract)
                            v.tensor_tensor(XT[:, t], XT[:, t], bank[t][:, :].rearrange("p (h n) -> p h n", h=NH),
                                            ALU.subtract).then_inc(s.lv_X.up, 1)
                    v.wait_ge(*s.uw_ok(NT * (dr + 1)))
                    v.wait_ge(*s.gl_e(dr + 1))
                    for i, t in enumerate((0, 1, 2, 3) if dr == 0 else (1, 0, 3, 2)):
                        n = NT * dr + i
                        if i == 0:
                            v.tensor_copy(vnew[:, t, :], un[:, t, :]).then_inc(s.st_v.up, 1)
                        else:
                            v.wait_ge(*s.st_mm(n - dr))
                            v.tensor_tensor(vnew[:, t, :], un[:, t, :], bank[4][:, 0:BW], ALU.subtract).then_inc(s.st_v.up, 1)
                        if i < NT - 1:
                            v.wait_ge(*s.st_s(n - dr + 1))
                            for hh in range(NH):
                                part, c = slice(HD * (hh % 2), HD * (hh % 2 + 1)), hh // 2
                                own = slice(HD * (hh % 2), HD * (hh % 2 + 1))
                                new = S[part, (i + 1) % 2, c, own]
                                upd = bank[5][part, P * c + HD * (hh % 2):P * c + HD * (hh % 2 + 1)]
                                if i == 0:
                                    ins = v.tensor_copy(new, upd)
                                else:
                                    ins = v.scalar_tensor_tensor(new, S[part, i % 2, c, own], gg[part, 5, t, hh:hh + 1], upd,
                                                                 ALU.mult, ALU.add)
                            link(ins)
                            v.sem_inc(s.st_S.up, 1)
                        v.wait_ge(*s.st_o(n + 1))
                        if dr == 0:
                            ins = v.tensor_copy(o_gdn[:, t, :], bank[6 + n % 2][:, 0:BW])
                        else:
                            ins = v.tensor_tensor(o_gdn[:, t, :], o_gdn[:, t, :], bank[6 + n % 2][:, 0:BW], ALU.add)
                        link(ins)
                        v.sem_inc(s.st_oa.up, 1)

                og4 = o_gdn.rearrange("p t (h n) -> p t h n", h=NH)
                ssg = small[:, 160:176].rearrange("p (t h) -> p t h", t=NT)
                link(v.tensor_tensor(wn[:, t0:NT], o_gdn[:, t0:NT], o_gdn[:, t0:NT], ALU.mult))
                ins = v.tensor_reduce(ssg[:, t0:NT], wn.rearrange("p t (h n) -> p t h n", h=NH)[:, t0:NT], AX, ALU.add)
                link(ins)
                mean_eps(ssg[:, t0:NT], HD, s.gdy_sq)
                inverse(ssg[:, t0:NT], s.gdy_rs)
                v.wait_ge(*s.z_silu(1))
                for t in tiles:
                    y = un[:, t, :].rearrange("p (h n) -> p h n", h=NH)
                    link(v.tensor_tensor(y, og4[:, t], per_head(ssg[:, t]), ALU.mult))
                    link(v.tensor_tensor(y, y, gdng.unsqueeze(1).to_broadcast([P, NH, HD]), ALU.mult))
                    ins = v.tensor_tensor(un[:, t], un[:, t], zn[:, t], ALU.mult)
                link(ins)
                v.sem_inc(s.gdy_n.up, 1)

                def merge(n):
                    c = n % KD
                    g, y = area(A_TR, 2, TOK)[:, n % 2, lo:TOK], bank[4 * (n // 2 % 2) + 2 + n % 2][:, lo:TOK]
                    v.wait_ge(*s.mg_sig(n + 1))
                    if n < KD:
                        ins = v.tensor_tensor(accT[:, c, lo:TOK], g, y, ALU.mult)
                    else:
                        link(v.tensor_tensor(g, g, y, ALU.mult))
                        ins = v.tensor_tensor(accT[:, c, lo:TOK], accT[:, c, lo:TOK], g, ALU.add)
                    ins.then_inc(s.mg_add.up, 1)

                for q in range(MW):
                    if q < 2:
                        for k in range(4 * q, 4 * q + 4):
                            v.wait_ge(*g_xhi(k + 1))
                            v.tensor_tensor(x_lo[:, k, lo:TOK], uT[:, k, lo:TOK], xg_hi[:, k, lo:TOK],
                                            ALU.subtract).then_inc(g_xlo.up, 1)
                    v.wait_ge(*g_whi(q + 1))
                    v.tensor_tensor(gsp[1][:, q % 3, :], half_slot(GATES[l], q), gsp[0][:, q % 3, :],
                                    ALU.subtract).then_inc(g_wlo.up, 1)
                    if q % 2:
                        v.wait_ge(*g_wlo(q + 1))
                        v.sem_inc(slot_free, 1)
                    if q % 2 == 0 and q >= 4:
                        merge(q - 4)
                        merge(q - 3)
                for n in range(MW - 4, MW):
                    merge(n)
                gate_diag(0, s.gb_d1, s.gb_m1, streams)
                post_add(s.po_sq1, s.po_ss1, s.po_rs1, s.gb_ok1, s.po_h1, tiles)
                gate_diag(1, s.gb_d2, s.gb_m2, streams)
                normalise(s.ssq2, s.rms2, s.rs2, s.xs2, tiles, 4)
                modulate(1, s.tp2, s.v_ok, tiles)

                sil = area(A_TR, 2, TOK)
                if ctx_out:
                    def input_low(half):
                        for k in range(4 * half, 4 * half + 4):
                            v.wait_ge(*g_xhi(KD + k + 1))
                            v.tensor_tensor(x_lo[:, k, :], uT[:, k, :], x_high(k), ALU.subtract).then_inc(g_xlo.up, 1)

                    v.wait_ge(*s.v_ok(KD))
                    input_low(0)
                    for q in range(3 * NF):
                        v.wait_ge(*g_whi(MW + q + 1))
                        v.tensor_tensor(dsp[1][:, q % 3, :], half_slot(FFN0, q), dsp[0][:, q % 3, :],
                                        ALU.subtract).then_inc(g_wlo.up, 1)
                        if q == 0:
                            input_low(1)
                        f = q - 2 * NF
                        if f >= 0:
                            v.wait_ge(*g_xhi(2 * KD + f + 1))
                            v.tensor_tensor(hsp[1][:, f % 3, :], hid[:, f, :], hsp[0][:, f % 3, :],
                                            ALU.subtract).then_inc(g_xlo.up, 1)
                        if q % 2:
                            v.wait_ge(*g_wlo(MW + q + 1))
                            v.sem_inc(slot_free, 1)
                        if q % 4 == 2 and 6 <= q < 2 * NF + 4:
                            c = (q - 6) // 4
                            for f in (2 * c, 2 * c + 1):
                                v.wait_ge(*s.f_sil(f + 1))
                                v.tensor_tensor(hid[:, f, :], sil0[:, f % 2, :], bank[4 * (c % 2) + 2 + f % 2][:, :],
                                                ALU.mult).then_inc(s.f_hid.up, 1)
                    post_add(s.po_sq2, s.po_ss2, s.po_rs2, s.gb_ok2, s.po_h2, tiles)
                    continue

                v.wait_ge(*s.rlog(1))
                lg, pick1, pick2, msk, t_a, t_b = (route[:, i] for i in range(6))
                idx = iota[:, 0:NE].unsqueeze(1).to_broadcast([P, 2, NE])
                m1, m2, mi, e1, e2, rr = (small[:, 180 + 2 * i:182 + 2 * i] for i in range(6))

                def along(x):
                    return x.unsqueeze(2).to_broadcast([P, 2, NE])

                def first_max(scores, m, pick):
                    link(v.tensor_reduce(m, scores, AX, ALU.max))
                    link(v.tensor_tensor(t_a, scores, along(m), ALU.is_equal))
                    link(v.scalar_tensor_tensor(t_b, idx, float(-NE), t_a, ALU.add, ALU.mult))
                    link(v.tensor_reduce(mi, t_b, AX, ALU.min))
                    link(v.tensor_scalar(mi, mi, float(NE), None, ALU.add))
                    link(v.tensor_tensor(pick, idx, along(mi), ALU.is_equal))

                link(v.tensor_copy(lg, bank[0][:, 0:2 * NE].rearrange("p (t e) -> p t e", t=2)))
                first_max(lg, m1, pick1)
                link(v.tensor_scalar(t_a, pick1, -1.0, 1.0, ALU.mult, ALU.add))
                link(v.tensor_tensor(lg, lg, t_a, ALU.mult))
                link(v.scalar_tensor_tensor(lg, pick1, -3.0e38, lg, ALU.mult, ALU.add))
                first_max(lg, m2, pick2)
                link(v.tensor_tensor(e2, m2, m1, ALU.subtract))
                v.sem_inc(s.rcomb.up, 1)
                v.wait_ge(*s.rcomb(2))
                link(v.tensor_scalar(e1, e2, 1.0, None, ALU.add))
                link(v.reciprocal(rr, e1))
                link(v.tensor_tensor(e2, e2, rr, ALU.mult))
                link(v.tensor_tensor(msk, pick1, pick2, ALU.add))
                v.sem_inc(s.rcomb.up, 1)
                link(v.tensor_tensor(pick1, pick1, along(rr), ALU.mult))
                link(v.tensor_tensor(pick2, pick2, along(e2), ALU.mult))
                link(v.memset(comb[:, :, 0:1], 0.0))
                link(v.tensor_tensor(comb[:, :, 1:NE + 1], pick1, pick2, ALU.add))
                link(v.memset(macc[:, :, :], 0.0))
                v.wait_ge(*s.rlog(2))
                link(v.tensor_tensor(rank[:, :, 0:NE], bank[1][:, 0:2 * NE].rearrange("p (t e) -> p t e", t=2), msk, ALU.mult))
                link(v.tensor_scalar(rank[:, :, 0:NE], rank[:, :, 0:NE], -1.0, None, ALU.add))
                link(v.memset(rank[:, :, NE:NE + 1], -1.0))
                link(v.tensor_reduce(m1[:, 0:1], bank[1][:, 2 * NE:3 * NE], AX, ALU.max))
                link(v.tensor_scalar(crowded[:, :], m1[:, 0:1], float(P), None, ALU.is_gt))
                v.sem_inc(s.f_hid.semaphore, 2)
                v.sem_inc(s.f_acc.semaphore, 1)
                v.sem_inc(s.rcomb.up, 1)
                dense = v.value_load(crowded[0:1, 0:1], min_val=0, max_val=1)
                with v.If(dense):
                    dense_experts_dve(s, sil)
                    v.sem_inc(dve_chain, 2)
                with v.Else():
                    sparse_experts_dve(again)
                v.wait_ge(*s.po_sq2(2))
                mean_eps(stat[:, 1, 10:12], D, s.po_ss2)
                inverse(stat[:, 1, 10:12], s.po_rs2)
                v.wait_ge(*s.gb_ok2(2))
                for t in range(2):
                    link(v.scalar_tensor_tensor(area(A_TR + D * t, D), macc[:, t, :], stat[:, 1, 10 + t:11 + t], GB[:, 1, :],
                                                ALU.mult, ALU.mult))
                    v.tensor_tensor(h[:, 2 + t, :], h[:, 2 + t, :], area(A_TR + D * t, D), ALU.add).then_inc(s.po_h2.up, 1)

        for signal, (name, total) in zip(sig[0], SIGNALS.items()):
            assert signal.raised == total, (name, signal.raised)


def shape_constants():
    import numpy as np
    i = np.arange(P)
    c = np.zeros((P, C_END), np.float32)
    c[:, C_ID:C_ID + P] = np.eye(P)
    c[:, C_ONE:C_ONE + P] = 1
    c[:, C_U:C_U + P] = i[:, None] <= i[None]
    c[:, C_L:C_L + P] = i[:, None] >= i[None]
    tok = np.arange(SEQ)
    inv = np.float32(10000.0) ** (-np.arange(HD // 4, dtype=np.float32) / np.float32(HD // 4))
    ang = np.concatenate([(tok // 64).astype(np.float32)[:, None] * inv, (tok % 64).astype(np.float32)[:, None] * inv], 1)
    rope = np.stack([np.cos(ang), np.sin(ang)], 1).reshape(2, P, 64)
    c[:, C_ROPE:C_ROPE + 128] = rope.transpose(1, 0, 2).reshape(P, 128)
    a = 2 * np.pi * np.outer(np.arange(HD), np.arange(HD)) / HD
    for cs, f in enumerate((np.cos(a), np.sin(a))):
        c[:, C_FD + P * cs:C_FD + P * (cs + 1)] = np.kron(np.eye(2), f / np.sqrt(SEQ * HD))
    a = 2 * np.pi * (np.outer(tok, tok) % SEQ) / SEQ
    ft = np.stack([np.cos(a), -np.sin(a)], 1).reshape(2, P, 2, SEQ)
    c[:, C_FT:C_FT + 1024] = ft.transpose(1, 0, 2, 3).reshape(P, 1024)

    g = np.zeros((P, H_END), np.float16)
    r, q = i[:, None], i[None]
    for dr in range(2):
        low = [r > q, r <= q]
        for lv in range(1 + LEVELS):
            sz = 2 ** lv
            m = (r // (2 * sz) == q // (2 * sz)) & (r // sz % 2 == 1) & (q // sz % 2 == 0)
            low += [m, m.T] if lv == 0 else [m]
        for n, m in enumerate(low):
            g[:, (10 * dr + n) * P:(10 * dr + n + 1) * P] = m.T if dr else m
    key = np.arange(SEQ)[:, None]
    qry = np.arange(SEQ)[None]
    for dr in range(2):
        same = (key - qry) if dr else (qry - key)
        far = (SEQ - qry + key) if dr else (SEQ + qry - key)
        dist = np.concatenate([np.maximum(same, 0), far]).reshape(4, P, SEQ)
        g[:, H_DIST + 1024 * dr:H_DIST + 1024 * (dr + 1)] = dist.transpose(1, 0, 2).reshape(P, 1024)
        msk = (same >= 0).astype(np.float16).reshape(2, P, SEQ)
        g[:, H_RM + 512 * dr:H_RM + 512 * (dr + 1)] = msk.transpose(1, 0, 2).reshape(P, 512)
    iota = np.tile(np.arange(P, dtype=np.float32), (P, 1))
    return {"consts": c, "halfc": g, "iota": iota}


_INS = ["x", "c", "ctx", "c_ctx", "ada_w", "ada_b", "norm_g", "w_in", "conv_w", "gdn_a_log", "gdn_dt_bias",
        "gdn_norm_g", "ret_log_decay_raw", "ret_norm_g", "qk_norm_g", "w_branch", "w_gate", "b_gate", "w_out",
        "ffn_w1", "ffn_w3", "ffn_w2", "moe_router", "moe_w1", "moe_w3", "moe_w2"]


def kernel(**inputs):
    import numpy as _np
    import concourse.bacc as _bacc
    from concourse.bass_utils import run_bass_kernel_spmd as _run

    nc = _bacc.Bacc("TRN2", target_bir_lowering=False, num_devices=1)
    arrays, d = {}, {}
    given = {name: inputs[name] for name in _INS}
    for name, a in {**given, **shape_constants()}.items():
        a = _np.ascontiguousarray(a)
        arrays[f"in_{name}_dram"] = a
        d[name] = nc.dram_tensor(f"in_{name}_dram", a.shape, mybir.dt.from_np(a.dtype), kind="ExternalInput").ap()
    for name in ("moe_w1", "moe_w3", "moe_w2"):
        d[name] = d[name].rearrange("a e k n -> (a e) k n")
    out = nc.dram_tensor("out_dram", (1, SEQ, D), F32, kind="ExternalOutput").ap()
    build_program(nc, d, out.rearrange("b t n -> (b t) n"))
    r = _run(nc, [arrays], core_ids=[0])
    return r.results[0]["out_dram"]
```
